# Optimizing a Trainium2 kernel written in Bass

```python
import math
import jax
import jax.numpy as jnp
from jax import lax
import numpy as np

D_MODEL = 1024
BATCH = 1
SEQ = 256
DEPTH = 1

GRID_W = 64
CTX_LEN = 256
ATTN_HEADS = 8
ATTN_KV_HEADS = 2
ATTN_HEAD_DIM = 64
ATTN_WINDOW = 128
ATTN_BLOCK = 128
ROPE_BASE = 10000.0
ROPE_PAIRS = ATTN_HEAD_DIM // 4
DN_HEADS = 4
DN_HEAD_DIM = 128
DN_CONV = 5
DN_CHUNK = 64
PEER_HEADS = 8
PEER_KEYS = 128
PEER_EXPERTS = PEER_KEYS * PEER_KEYS
PEER_KEY_DIM = 128
PEER_KEY_HALF = PEER_KEY_DIM // 2
PEER_TOPK = 16
PEER_BLOCK = 128
RMS_EPS = 1e-6
L2_EPS = 1e-6
ATTN_Q = ATTN_HEADS * ATTN_HEAD_DIM
ATTN_KV = ATTN_KV_HEADS * ATTN_HEAD_DIM
DN_WIDTH = DN_HEADS * DN_HEAD_DIM
IN_SPLITS = (ATTN_Q, ATTN_KV, ATTN_KV, 3 * DN_WIDTH, DN_WIDTH, DN_HEADS, DN_HEADS, DN_HEADS, DN_HEADS, 2 * D_MODEL)
IN_COLS = sum(IN_SPLITS)
F32 = jnp.float32


def rmsnorm(x, gain):
    x32 = x.astype(F32)
    y = x32 * lax.rsqrt(jnp.mean(x32 * x32, axis=-1, keepdims=True) + RMS_EPS)
    return (y * gain.astype(F32)).astype(x.dtype)

def l2norm(x):
    x32 = x.astype(F32)
    return x32 * lax.rsqrt(jnp.sum(x32 * x32, axis=-1, keepdims=True) + L2_EPS)

def rope_angles(pos):
    inv_freq = ROPE_BASE ** (-jnp.arange(ROPE_PAIRS, dtype=F32) / ROPE_PAIRS)
    ang = pos.astype(F32)[:, None] * inv_freq[None, :]
    return jnp.cos(ang)[:, None, :], jnp.sin(ang)[:, None, :]

def rotate_pairs(x, cos, sin):
    x1, x2 = jnp.split(x.astype(F32), 2, axis=-1)
    return jnp.concatenate([x1 * cos - x2 * sin, x1 * sin + x2 * cos], axis=-1)

def axial_rope(x, rope):
    cos_r, sin_r, cos_c, sin_c = rope
    x_row, x_col = jnp.split(x, 2, axis=-1)
    out = jnp.concatenate([rotate_pairs(x_row, cos_r, sin_r), rotate_pairs(x_col, cos_c, sin_c)], axis=-1)
    return out.astype(x.dtype)

def short_conv(u, w):
    pad = DN_CONV // 2
    return lax.conv_general_dilated(u, w[:, None, :].astype(u.dtype), window_strides=(1,), padding=[(pad, pad)], dimension_numbers=('NWC', 'WIO', 'NWC'), feature_group_count=u.shape[-1])

def project_mixer_inputs(h, w_in, b_gate, conv_w):
    B, T, _ = h.shape
    p = h @ w_in
    offsets = np.cumsum(IN_SPLITS)[:-1].tolist()
    q_a, k_a, v_a, qkv_d, z_d, a_f, a_b, b_f, b_b, gates = jnp.split(p, offsets, axis=-1)
    qkv_d = jax.nn.silu(short_conv(qkv_d, conv_w))
    q_d, k_d, v_d = jnp.split(qkv_d, 3, axis=-1)
    g_attn, g_dn = jnp.split(jax.nn.sigmoid(gates + b_gate), 2, axis=-1)
    dn_heads = lambda t: t.reshape(B, T, DN_HEADS, DN_HEAD_DIM)
    return {
        'q_attn': q_a.reshape(B, T, ATTN_HEADS, ATTN_HEAD_DIM),
        'k_attn': k_a.reshape(B, T, ATTN_KV_HEADS, ATTN_HEAD_DIM),
        'v_attn': v_a.reshape(B, T, ATTN_KV_HEADS, ATTN_HEAD_DIM),
        'q_dn': l2norm(dn_heads(q_d)) * DN_HEAD_DIM ** -0.5,
        'k_dn': l2norm(dn_heads(k_d)),
        'v_dn': dn_heads(v_d).astype(F32),
        'z_dn': dn_heads(z_d),
        'a_f': a_f, 'a_b': a_b, 'b_f': b_f, 'b_b': b_b,
        'gate_attn': g_attn, 'gate_dn': g_dn,
    }

def windowed_attention(q, k, v, k_ctx, v_ctx, sink):
    B, S, H, hd = q.shape
    KV = k.shape[2]
    G = H // KV
    L = k_ctx.shape[1]
    nb = S // ATTN_BLOCK
    span = ATTN_BLOCK + 2 * ATTN_WINDOW
    scale = hd ** -0.5
    qb = jnp.moveaxis(q.reshape(B, nb, ATTN_BLOCK, KV, G, hd), 1, 0)
    pad = ((0, 0), (ATTN_WINDOW, ATTN_WINDOW), (0, 0), (0, 0))
    kp = jnp.pad(k, pad)
    vp = jnp.pad(v, pad)
    s_sink = jnp.broadcast_to(sink.astype(F32).reshape(1, KV, G, 1, 1), (B, KV, G, ATTN_BLOCK, 1))
    s_ctx_all = None

    def one_block(args):
        i, qi = args
        start = i * ATTN_BLOCK
        kw = lax.dynamic_slice_in_dim(kp, start, span, axis=1)
        vw = lax.dynamic_slice_in_dim(vp, start, span, axis=1)
        qpos = start + jnp.arange(ATTN_BLOCK)
        kpos = start - ATTN_WINDOW + jnp.arange(span)
        valid = (kpos[None, :] >= 0) & (kpos[None, :] < S) & (jnp.abs(qpos[:, None] - kpos[None, :]) <= ATTN_WINDOW)
        s_loc = jnp.einsum('bqkgd,bjkd->bkgqj', qi, kw, preferred_element_type=F32) * scale
        s_loc = jnp.where(valid, s_loc, -jnp.inf)
        s_ctx = jnp.einsum('bqkgd,bjkd->bkgqj', qi, k_ctx, preferred_element_type=F32) * scale
        p = jax.nn.softmax(jnp.concatenate([s_loc, s_ctx, s_sink], axis=-1), axis=-1)
        p_loc = p[..., :span].astype(v.dtype)
        p_ctx = p[..., span:span + L].astype(v.dtype)
        return jnp.einsum('bkgqj,bjkd->bqkgd', p_loc, vw) + jnp.einsum('bkgqj,bjkd->bqkgd', p_ctx, v_ctx)

    out = lax.map(one_block, (jnp.arange(nb), qb))
    return jnp.moveaxis(out, 0, 1).reshape(B, S, H * hd)

def context_attention(q, k, v, sink):
    B, L, H, hd = q.shape
    KV = k.shape[2]
    G = H // KV
    qg = q.reshape(B, L, KV, G, hd)
    s = jnp.einsum('bqkgd,bjkd->bkgqj', qg, k, preferred_element_type=F32) * hd ** -0.5
    s_sink = jnp.broadcast_to(sink.astype(F32).reshape(1, KV, G, 1, 1), (B, KV, G, L, 1))
    p = jax.nn.softmax(jnp.concatenate([s, s_sink], axis=-1), axis=-1)[..., :L]
    o = jnp.einsum('bkgqj,bjkd->bqkgd', p.astype(v.dtype), v)
    return o.reshape(B, L, H * hd)

def gated_delta_chunked(q, k, v, g, beta, state0):
    B, T, H, DK = q.shape
    DV = v.shape[-1]
    C = DN_CHUNK
    N = T // C

    def chunks(a):
        return jnp.moveaxis(a.reshape((B, N, C, H) + a.shape[3:]), 3, 1)

    qc, kc, vc = chunks(q.astype(F32)), chunks(k.astype(F32)), chunks(v.astype(F32))
    gc, bc = chunks(g.astype(F32)), chunks(beta.astype(F32))
    Gcum = jnp.cumsum(gc, axis=-1)
    incl = jnp.tril(jnp.ones((C, C), bool))
    strict = jnp.tril(jnp.ones((C, C), bool), -1)
    decay = jnp.exp(jnp.where(incl, Gcum[..., :, None] - Gcum[..., None, :], -jnp.inf))
    kb = kc * bc[..., None]
    A = jnp.where(strict, jnp.einsum('bhnid,bhnjd->bhnij', kb, kc) * decay, 0.0)
    eye = jnp.eye(C, dtype=F32)
    t_inv = lax.linalg.triangular_solve(A + eye, jnp.broadcast_to(eye, A.shape), left_side=True, lower=True, unit_diagonal=True)
    W = t_inv @ (kb * jnp.exp(Gcum)[..., None])
    U = t_inv @ (vc * bc[..., None])
    attn = jnp.einsum('bhnid,bhnjd->bhnij', qc, kc) * decay
    q_dec = qc * jnp.exp(Gcum)[..., None]
    k_tail = kc * jnp.exp(Gcum[..., -1:] - Gcum)[..., None]
    g_tot = jnp.exp(Gcum[..., -1])

    def step(S, xs):
        W_n, U_n, attn_n, qd_n, kt_n, gt_n = xs
        v_new = U_n - jnp.einsum('bhcd,bhde->bhce', W_n, S)
        o = jnp.einsum('bhcd,bhde->bhce', qd_n, S) + jnp.einsum('bhij,bhje->bhie', attn_n, v_new)
        S = S * gt_n[..., None, None] + jnp.einsum('bhcd,bhce->bhde', kt_n, v_new)
        return S, o

    xs = tuple(jnp.moveaxis(a, 2, 0) for a in (W, U, attn, q_dec, k_tail, g_tot))
    S_fin, o = lax.scan(step, state0.astype(F32), xs)
    o = o.transpose(1, 0, 3, 2, 4).reshape(B, T, H, DV)
    return o, S_fin

def decay_and_beta(a_logit, b_logit, a_log, dt_bias):
    g = -jnp.exp(a_log.astype(F32)) * jax.nn.softplus(a_logit.astype(F32) + dt_bias.astype(F32))
    return g, jax.nn.sigmoid(b_logit.astype(F32))

def bidirectional_delta(m, a_log_f, dt_bias_f, a_log_b, dt_bias_b, state_f, state_b):
    g_f, beta_f = decay_and_beta(m['a_f'], m['b_f'], a_log_f, dt_bias_f)
    g_b, beta_b = decay_and_beta(m['a_b'], m['b_b'], a_log_b, dt_bias_b)
    q, k, v = m['q_dn'], m['k_dn'], m['v_dn']
    o_f, s_f = gated_delta_chunked(q, k, v, g_f, beta_f, state_f)
    flip = lambda t: jnp.flip(t, axis=1)
    o_b, s_b = gated_delta_chunked(flip(q), flip(k), flip(v), flip(g_b), flip(beta_b), state_b)
    return o_f + flip(o_b), s_f, s_b

def gated_head_norm(o, z, gain):
    B, T = o.shape[:2]
    y = o * lax.rsqrt(jnp.mean(o * o, axis=-1, keepdims=True) + RMS_EPS) * gain.astype(F32)
    y = y * jax.nn.silu(z.astype(F32))
    return y.reshape(B, T, DN_WIDTH).astype(z.dtype)

def merge_branches(o_attn, o_dn, m, w_br_attn, w_br_dn, w_out):
    y = m['gate_attn'] * (o_attn @ w_br_attn) + m['gate_dn'] * (o_dn @ w_br_dn)
    return y @ w_out

def peer_ffn(h, w_q, keys, u_table, v_table):
    shape = h.shape
    blocks = h.reshape(-1, PEER_BLOCK, shape[-1])

    def block(hb):
        q = (hb @ w_q).reshape(PEER_BLOCK, PEER_HEADS, 2, PEER_KEY_HALF)
        s = jnp.einsum('thpd,hpkd->thpk', q, keys, preferred_element_type=F32)
        half_s, half_i = lax.top_k(s, PEER_TOPK)
        cand = half_s[:, :, 0, :, None] + half_s[:, :, 1, None, :]
        best_s, best_c = lax.top_k(cand.reshape(PEER_BLOCK, PEER_HEADS, PEER_TOPK * PEER_TOPK), PEER_TOPK)
        i1 = jnp.take_along_axis(half_i[:, :, 0], best_c // PEER_TOPK, axis=-1)
        i2 = jnp.take_along_axis(half_i[:, :, 1], best_c % PEER_TOPK, axis=-1)
        experts = i1 * PEER_KEYS + i2
        gate = jax.nn.softmax(best_s, axis=-1)
        act = jax.nn.gelu(jnp.einsum('td,thkd->thk', hb, u_table[experts], preferred_element_type=F32))
        return jnp.einsum('thk,thkd->td', (gate * act).astype(hb.dtype), v_table[experts])

    return lax.map(block, blocks).reshape(shape)

def first_inputs(seed: int = 0) -> dict:
    key = jax.random.key(seed)
    ks = jax.random.split(key, 26)
    D = D_MODEL
    L = DEPTH
    nrm = lambda k, shape, scale: jax.random.normal(k, shape, F32) * scale

    def a_log(k):
        return jnp.log(jax.random.uniform(k, (L, DN_HEADS), F32, 1.0, 16.0))

    def dt_bias(k):
        dt = jnp.exp(jax.random.uniform(k, (L, DN_HEADS), F32, math.log(1e-3), math.log(1e-1)))
        return dt + jnp.log(-jnp.expm1(-dt))

    return {
        'x': nrm(ks[0], (BATCH, SEQ, D), 1.0),
        'c': nrm(ks[1], (BATCH, D), 1.0),
        'ctx': nrm(ks[2], (BATCH, CTX_LEN, D), 1.0),
        'c_ctx': nrm(ks[3], (D,), 1.0),
        'w_ada': nrm(ks[4], (L, D, 6 * D), 0.5 * D ** -0.5),
        'b_ada': nrm(ks[5], (L, 6 * D), 0.01),
        'norm_mix': 1.0 + nrm(ks[6], (L, D), 0.01),
        'norm_ffn': 1.0 + nrm(ks[7], (L, D), 0.01),
        'w_in': nrm(ks[8], (L, D, IN_COLS), D ** -0.5),
        'b_gate': nrm(ks[9], (L, 2 * D), 0.01),
        'attn_sink': nrm(ks[10], (L, ATTN_HEADS), 0.5),
        'dn_conv': nrm(ks[11], (L, DN_CONV, 3 * DN_WIDTH), DN_CONV ** -0.5),
        'dn_a_log_f': a_log(ks[12]),
        'dn_dt_bias_f': dt_bias(ks[13]),
        'dn_a_log_b': a_log(ks[14]),
        'dn_dt_bias_b': dt_bias(ks[15]),
        'dn_norm': 1.0 + nrm(ks[16], (L, DN_HEAD_DIM), 0.01),
        'w_br_attn': nrm(ks[17], (L, ATTN_Q, D), ATTN_Q ** -0.5),
        'w_br_dn': nrm(ks[18], (L, DN_WIDTH, D), DN_WIDTH ** -0.5),
        'w_out': nrm(ks[19], (L, D, D), D ** -0.5),
        'peer_wq': nrm(ks[20], (L, D, PEER_HEADS * PEER_KEY_DIM), D ** -0.5),
        'peer_keys': nrm(ks[21], (L, PEER_HEADS, 2, PEER_KEYS, PEER_KEY_HALF), PEER_KEY_HALF ** -0.5),
        'peer_u': nrm(ks[22], (L, PEER_EXPERTS, D), D ** -0.5),
        'peer_v': nrm(ks[23], (L, PEER_EXPERTS, D), PEER_HEADS ** -0.5),
        'final_norm': 1.0 + nrm(ks[24], (D,), 0.01),
    }

def first_block(x, c, ctx, c_ctx, w_ada, b_ada, norm_mix, norm_ffn, w_in, b_gate, attn_sink, dn_conv,
              dn_a_log_f, dn_dt_bias_f, dn_a_log_b, dn_dt_bias_b, dn_norm, w_br_attn, w_br_dn, w_out,
              peer_wq, peer_keys, peer_u, peer_v, final_norm):
    B, S, D = x.shape
    rows = S // GRID_W
    row_pos = jnp.repeat(jnp.arange(rows, dtype=jnp.int32), GRID_W)
    col_pos = jnp.tile(jnp.arange(GRID_W, dtype=jnp.int32), rows)
    rope = (*rope_angles(row_pos), *rope_angles(col_pos))
    zero_state = jnp.zeros((B, DN_HEADS, DN_HEAD_DIM, DN_HEAD_DIM), F32)

    for layer in range(DEPTH):
        mod = jax.nn.silu(c) @ w_ada[layer] + b_ada[layer]
        sh1, sc1, gt1, sh2, sc2, gt2 = [t[:, None, :] for t in jnp.split(mod, 6, axis=-1)]
        cmod = jax.nn.silu(c_ctx) @ w_ada[layer] + b_ada[layer]
        csh1, csc1, cgt1, csh2, csc2, cgt2 = jnp.split(cmod, 6, axis=-1)

        hc = rmsnorm(ctx, norm_mix[layer]) * (1.0 + csc1) + csh1
        mc = project_mixer_inputs(hc, w_in[layer], b_gate[layer], dn_conv[layer])
        oc_dn, st_f, st_b = bidirectional_delta(mc, dn_a_log_f[layer], dn_dt_bias_f[layer], dn_a_log_b[layer], dn_dt_bias_b[layer], zero_state, zero_state)

        h = rmsnorm(x, norm_mix[layer]) * (1.0 + sc1) + sh1
        m = project_mixer_inputs(h, w_in[layer], b_gate[layer], dn_conv[layer])
        q_lat = axial_rope(m['q_attn'], rope)
        k_lat = axial_rope(m['k_attn'], rope)
        o_attn = windowed_attention(q_lat, k_lat, m['v_attn'], mc['k_attn'], mc['v_attn'], attn_sink[layer])
        o_dn, _, _ = bidirectional_delta(m, dn_a_log_f[layer], dn_dt_bias_f[layer], dn_a_log_b[layer], dn_dt_bias_b[layer], st_f, st_b)
        o_dn = gated_head_norm(o_dn, m['z_dn'], dn_norm[layer])
        x = x + gt1 * merge_branches(o_attn, o_dn, m, w_br_attn[layer], w_br_dn[layer], w_out[layer])

        h2 = rmsnorm(x, norm_ffn[layer]) * (1.0 + sc2) + sh2
        x = x + gt2 * peer_ffn(h2, peer_wq[layer], peer_keys[layer], peer_u[layer], peer_v[layer])

        if layer + 1 < DEPTH:
            oc_attn = context_attention(mc['q_attn'], mc['k_attn'], mc['v_attn'], attn_sink[layer])
            oc_dn_g = gated_head_norm(oc_dn, mc['z_dn'], dn_norm[layer])
            ctx = ctx + cgt1 * merge_branches(oc_attn, oc_dn_g, mc, w_br_attn[layer], w_br_dn[layer], w_out[layer])
            hc2 = rmsnorm(ctx, norm_ffn[layer]) * (1.0 + csc2) + csh2
            ctx = ctx + cgt2 * peer_ffn(hc2, peer_wq[layer], peer_keys[layer], peer_u[layer], peer_v[layer])

    return rmsnorm(x, final_norm)


MOBA_HEADS = 8
MOBA_HEAD_DIM = 64
MOBA_BLOCK = 256
MOBA_TOPK = 3
MOBA_Q_CHUNK = 64
RG_WIDTH = D_MODEL
RG_BLOCKS = 16
RG_BLOCK_DIM = RG_WIDTH // RG_BLOCKS
RG_CONV = 4
RG_C = 8.0
RG_A_MIN = 0.9
RG_A_MAX = 0.999
DIFF_HEADS = 4
DIFF_HEAD_DIM = 64
DIFF_Q_BLOCK = 128
D_FF = 2816
FFN_CONV = 3
N_BRANCHES = 3

MOBA_WIDTH = MOBA_HEADS * MOBA_HEAD_DIM
DIFF_QK_WIDTH = DIFF_HEADS * 2 * DIFF_HEAD_DIM
DIFF_V_WIDTH = DIFF_HEADS * 2 * DIFF_HEAD_DIM
IN_WIDTHS = (MOBA_WIDTH, MOBA_WIDTH, MOBA_WIDTH, DIFF_QK_WIDTH, DIFF_QK_WIDTH, DIFF_V_WIDTH, RG_WIDTH, RG_WIDTH, N_BRANCHES * D_MODEL)
IN_COLS_2 = sum(IN_WIDTHS)


def rms_norm(x, g):
    xf = x.astype(jnp.float32)
    y = xf * lax.rsqrt(jnp.mean(xf * xf, axis=-1, keepdims=True) + RMS_EPS)
    return (y * g.astype(jnp.float32)).astype(x.dtype)

def alibi_slopes(n):
    return 2.0 ** (-8.0 * jnp.arange(1, n + 1, dtype=jnp.float32) / n)

def causal_dwconv(x, w, b):
    k_w = w.shape[0]
    s = x.shape[1]
    xp = jnp.pad(x, ((0, 0), (k_w - 1, 0), (0, 0)))
    y = b
    for j in range(k_w):
        y = y + w[j] * xp[:, j:j + s]
    return y

def split_offsets():
    return np.cumsum(np.array(IN_WIDTHS[:-1])).tolist()

def moba_attention(q, k, v):
    B, S, H, D = q.shape
    nb = -(-S // MOBA_BLOCK)
    s_pad = nb * MOBA_BLOCK
    pad = ((0, 0), (0, s_pad - S), (0, 0), (0, 0))
    q, k, v = [jnp.pad(t, pad).transpose(0, 2, 1, 3) for t in (q, k, v)]
    kb = k.reshape(B, H, nb, MOBA_BLOCK, D)
    vb = v.reshape(B, H, nb, MOBA_BLOCK, D)
    slopes = alibi_slopes(H)[None, :, None, None]
    scale = D ** -0.5
    kmean = jnp.mean(kb.astype(jnp.float32), axis=3)
    gate = jnp.einsum('bhsd,bhnd->bhsn', q.astype(jnp.float32), kmean)
    q_blk = jnp.arange(s_pad) // MOBA_BLOCK
    past = jnp.arange(nb)[None, :] < q_blk[:, None]
    gate = jnp.where(past, gate, -jnp.inf)
    n_sel = min(MOBA_TOPK, nb)
    _, sel = lax.top_k(gate, n_sel)
    bi = jnp.arange(B)[:, None, None, None]
    hi = jnp.arange(H)[None, :, None, None]
    n_chunks = s_pad // MOBA_Q_CHUNK

    def chunk(c):
        q0 = c * MOBA_Q_CHUNK
        blk = q0 // MOBA_BLOCK
        qc = lax.dynamic_slice_in_dim(q, q0, MOBA_Q_CHUNK, axis=2)
        selc = lax.dynamic_slice_in_dim(sel, q0, MOBA_Q_CHUNK, axis=2)
        qpos = q0 + jnp.arange(MOBA_Q_CHUNK)
        k_own = lax.dynamic_index_in_dim(kb, blk, axis=2, keepdims=False)
        v_own = lax.dynamic_index_in_dim(vb, blk, axis=2, keepdims=False)
        kpos_own = blk * MOBA_BLOCK + jnp.arange(MOBA_BLOCK)
        dist_own = (qpos[:, None] - kpos_own[None, :]).astype(jnp.float32)
        l_own = jnp.einsum('bhqd,bhkd->bhqk', qc, k_own).astype(jnp.float32) * scale - slopes * dist_own
        l_own = jnp.where(dist_own >= 0, l_own, -jnp.inf)
        k_sel = kb[bi, hi, selc]
        v_sel = vb[bi, hi, selc]
        kpos_sel = selc[..., None] * MOBA_BLOCK + jnp.arange(MOBA_BLOCK)
        dist_sel = (qpos[None, None, :, None, None] - kpos_sel).astype(jnp.float32)
        l_sel = jnp.einsum('bhqd,bhqnkd->bhqnk', qc, k_sel).astype(jnp.float32) * scale - slopes[..., None] * dist_sel
        valid = (selc < blk)[..., None]
        l_sel = jnp.where(valid, l_sel, -jnp.inf)
        n_keys = n_sel * MOBA_BLOCK
        logits = jnp.concatenate([l_sel.reshape(B, H, MOBA_Q_CHUNK, n_keys), l_own], axis=-1)
        p = jax.nn.softmax(logits, axis=-1).astype(v.dtype)
        p_sel = p[..., :n_keys].reshape(B, H, MOBA_Q_CHUNK, n_sel, MOBA_BLOCK)
        p_own = p[..., n_keys:]
        return (jnp.einsum('bhqnk,bhqnkd->bhqd', p_sel, v_sel)
                + jnp.einsum('bhqk,bhkd->bhqd', p_own, v_own))

    out = lax.map(chunk, jnp.arange(n_chunks))
    out = out.transpose(1, 0, 3, 2, 4).reshape(B, s_pad, H, D)
    return out[:, :S]

def diff_attention(q, k, v, lam, lam_init, subln_g):
    B, S, H, _, Dh = q.shape
    q = q.transpose(0, 2, 3, 1, 4)
    k = k.transpose(0, 2, 3, 1, 4)
    v = v.transpose(0, 2, 1, 3)
    slopes = alibi_slopes(H)[None, :, None, None, None]
    scale = Dh ** -0.5
    kpos = jnp.arange(S)
    n_blocks = S // DIFF_Q_BLOCK

    def block(c):
        q0 = c * DIFF_Q_BLOCK
        qc = lax.dynamic_slice_in_dim(q, q0, DIFF_Q_BLOCK, axis=3)
        qpos = q0 + jnp.arange(DIFF_Q_BLOCK)
        dist = (qpos[:, None] - kpos[None, :]).astype(jnp.float32)
        logits = jnp.einsum('bhmqd,bhmkd->bhmqk', qc, k).astype(jnp.float32) * scale - slopes * dist
        logits = jnp.where(dist >= 0, logits, -jnp.inf)
        p = jax.nn.softmax(logits, axis=-1)
        w = p[:, :, 0] - lam * p[:, :, 1]
        return jnp.einsum('bhqk,bhkd->bhqd', w.astype(v.dtype), v)

    out = lax.map(block, jnp.arange(n_blocks))
    out = out.transpose(1, 0, 3, 2, 4).reshape(B, S, H, 2 * Dh)
    out = rms_norm(out, subln_g) * (1.0 - lam_init)
    return out.reshape(B, S, H * 2 * Dh)

def rg_lru(x, w_a, b_a, w_x, b_x, lam):
    B, S, C = x.shape
    xb = x.reshape(B, S, RG_BLOCKS, RG_BLOCK_DIM)
    r = jax.nn.sigmoid(jnp.einsum('bsnc,ncd->bsnd', xb, w_a).reshape(B, S, C) + b_a)
    i = jax.nn.sigmoid(jnp.einsum('bsnc,ncd->bsnd', xb, w_x).reshape(B, S, C) + b_x)
    log_a = -RG_C * r.astype(jnp.float32) * jax.nn.softplus(-lam.astype(jnp.float32))
    a = jnp.exp(log_a)
    mult = jnp.sqrt(-jnp.expm1(2.0 * log_a))
    b = mult * (i * x).astype(jnp.float32)

    def combine(left, right):
        a1, b1 = left
        a2, b2 = right
        return a1 * a2, a2 * b1 + b2

    _, h = lax.associative_scan(combine, (a, b), axis=1)
    return h.astype(x.dtype)

def second_inputs(seed: int = 0) -> dict:
    key = jax.random.key(seed)
    ks = jax.random.split(key, 26)
    f32 = jnp.float32
    L = DEPTH

    def nrm(k, shape, scale):
        return jax.random.normal(k, shape, f32) * scale

    def gain(k, shape):
        return 1.0 + nrm(k, shape, 0.01)

    a_c = jax.random.uniform(ks[10], (L, RG_WIDTH), f32, RG_A_MIN, RG_A_MAX)
    a0 = a_c ** (1.0 / RG_C)
    return {
        'x': nrm(ks[0], (BATCH, SEQ, D_MODEL), 1.0),
        'norm_mix_g': gain(ks[1], (L, D_MODEL)),
        'w_in': nrm(ks[2], (L, D_MODEL, IN_COLS_2), D_MODEL ** -0.5),
        'b_gate': nrm(ks[3], (L, N_BRANCHES * D_MODEL), 0.01),
        'rg_conv_w': nrm(ks[4], (L, RG_CONV, RG_WIDTH), RG_CONV ** -0.5),
        'rg_conv_b': nrm(ks[5], (L, RG_WIDTH), 0.01),
        'rg_w_a': nrm(ks[6], (L, RG_BLOCKS, RG_BLOCK_DIM, RG_BLOCK_DIM), RG_BLOCK_DIM ** -0.5),
        'rg_b_a': nrm(ks[7], (L, RG_WIDTH), 0.01),
        'rg_w_x': nrm(ks[8], (L, RG_BLOCKS, RG_BLOCK_DIM, RG_BLOCK_DIM), RG_BLOCK_DIM ** -0.5),
        'rg_b_x': nrm(ks[9], (L, RG_WIDTH), 0.01),
        'rg_lambda': jnp.log(a0) - jnp.log1p(-a0),
        'diff_lq1': nrm(ks[11], (L, DIFF_HEAD_DIM), 0.1),
        'diff_lk1': nrm(ks[12], (L, DIFF_HEAD_DIM), 0.1),
        'diff_lq2': nrm(ks[13], (L, DIFF_HEAD_DIM), 0.1),
        'diff_lk2': nrm(ks[14], (L, DIFF_HEAD_DIM), 0.1),
        'diff_subln_g': gain(ks[15], (L, 2 * DIFF_HEAD_DIM)),
        'w_branch_a': nrm(ks[16], (L, MOBA_WIDTH, D_MODEL), MOBA_WIDTH ** -0.5),
        'w_branch_b': nrm(ks[17], (L, RG_WIDTH, D_MODEL), RG_WIDTH ** -0.5),
        'w_branch_c': nrm(ks[18], (L, DIFF_V_WIDTH, D_MODEL), DIFF_V_WIDTH ** -0.5),
        'w_out': nrm(ks[19], (L, D_MODEL, D_MODEL), D_MODEL ** -0.5),
        'norm_ffn_g': gain(ks[20], (L, D_MODEL)),
        'ffn_up': nrm(ks[21], (L, D_MODEL, 2 * D_FF), D_MODEL ** -0.5),
        'ffn_conv_w': nrm(ks[22], (L, FFN_CONV, 2 * D_FF), FFN_CONV ** -0.5),
        'ffn_conv_b': nrm(ks[23], (L, 2 * D_FF), 0.01),
        'ffn_down': nrm(ks[24], (L, D_FF, D_MODEL), D_FF ** -0.5),
        'final_norm_g': gain(ks[25], (D_MODEL,)),
    }

def second_block(x, norm_mix_g, w_in, b_gate, rg_conv_w, rg_conv_b, rg_w_a, rg_b_a, rg_w_x, rg_b_x,
              rg_lambda, diff_lq1, diff_lk1, diff_lq2, diff_lk2, diff_subln_g, w_branch_a, w_branch_b,
              w_branch_c, w_out, norm_ffn_g, ffn_up, ffn_conv_w, ffn_conv_b, ffn_down, final_norm_g):
    B, S = x.shape[0], x.shape[1]
    offs = split_offsets()
    for l in range(DEPTH):
        h = rms_norm(x, norm_mix_g[l])
        proj = h @ w_in[l]
        qa, ka, va, qc, kc, vc, rx, rgate, gates = jnp.split(proj, offs, axis=-1)
        ya = moba_attention(qa.reshape(B, S, MOBA_HEADS, MOBA_HEAD_DIM),
                            ka.reshape(B, S, MOBA_HEADS, MOBA_HEAD_DIM),
                            va.reshape(B, S, MOBA_HEADS, MOBA_HEAD_DIM)).reshape(B, S, MOBA_WIDTH)
        xr = causal_dwconv(rx, rg_conv_w[l], rg_conv_b[l])
        yb = rg_lru(xr, rg_w_a[l], rg_b_a[l], rg_w_x[l], rg_b_x[l], rg_lambda[l]) * jax.nn.gelu(rgate)
        lam_init = 0.8 - 0.6 * math.exp(-0.3 * l)
        lam = (jnp.exp(jnp.sum(diff_lq1[l].astype(jnp.float32) * diff_lk1[l].astype(jnp.float32)))
               - jnp.exp(jnp.sum(diff_lq2[l].astype(jnp.float32) * diff_lk2[l].astype(jnp.float32)))
               + lam_init)
        yc = diff_attention(qc.reshape(B, S, DIFF_HEADS, 2, DIFF_HEAD_DIM),
                            kc.reshape(B, S, DIFF_HEADS, 2, DIFF_HEAD_DIM),
                            vc.reshape(B, S, DIFF_HEADS, 2 * DIFF_HEAD_DIM),
                            lam, lam_init, diff_subln_g[l])
        g = jax.nn.sigmoid(gates + b_gate[l]).reshape(B, S, N_BRANCHES, D_MODEL)
        merged = (g[:, :, 0] * (ya @ w_branch_a[l])
                  + g[:, :, 1] * (yb @ w_branch_b[l])
                  + g[:, :, 2] * (yc @ w_branch_c[l]))
        x = x + merged @ w_out[l]
        h = rms_norm(x, norm_ffn_g[l])
        u = causal_dwconv(h @ ffn_up[l], ffn_conv_w[l], ffn_conv_b[l])
        u_gate, u_val = jnp.split(u, 2, axis=-1)
        x = x + (jax.nn.gelu(u_gate) * u_val) @ ffn_down[l]
    return rms_norm(x, final_norm_g)


_first_inputs = second_inputs


def second_inputs(seed=0):
    import zlib

    import numpy as np

    out = dict(_first_inputs(seed))
    spreads = {}
    factors = {'norm_mix_g': 6.101,
     'b_gate': 25.959,
     'rg_conv_b': 3.952,
     'rg_b_a': 41.249,
     'rg_b_x': 34.099,
     'diff_lk2': 3.38,
     'diff_subln_g': 64.0,
     'norm_ffn_g': 34.906,
     'ffn_conv_b': 33.875,
     'final_norm_g': 31.228,
     'diff_lk1': 2.838}
    for name, (base, spread) in spreads.items():
        noise = np.random.default_rng([zlib.crc32(name.encode()), seed]).standard_normal(out[name].shape)
        drawn = base * np.exp(spread * noise) if base else spread * noise
        out[name] = jnp.asarray(drawn.astype(out[name].dtype))
    for name, factor in factors.items():
        out[name] = (out[name] * factor).astype(out[name].dtype)
    return out


_narrow_inputs = second_inputs


def second_inputs(seed=0):

    out = dict(_narrow_inputs(seed))
    wider = {'rg_conv_b': 4.18,
     'diff_subln_g': 4.82,
     'norm_ffn_g': 4.72,
     'ffn_conv_b': 4.69,
     'final_norm_g': 6.31}
    for name, times in wider.items():
        mean = out[name].mean()
        out[name] = (mean + times * (out[name] - mean)).astype(out[name].dtype)
    return out


def setup_inputs(seed=0):
    out = dict(first_inputs(seed))
    for name, value in second_inputs(seed + 1).items():
        if name != "x":
            out[name + "_2"] = value
    return out


def reference(
    x, c, ctx, c_ctx, w_ada, b_ada, norm_mix, norm_ffn, w_in, b_gate, attn_sink, dn_conv,
    dn_a_log_f, dn_dt_bias_f, dn_a_log_b, dn_dt_bias_b, dn_norm, w_br_attn, w_br_dn, w_out,
    peer_wq, peer_keys, peer_u, peer_v, final_norm, norm_mix_g_2, w_in_2, b_gate_2, rg_conv_w_2,
    rg_conv_b_2, rg_w_a_2, rg_b_a_2, rg_w_x_2, rg_b_x_2, rg_lambda_2, diff_lq1_2, diff_lk1_2,
    diff_lq2_2, diff_lk2_2, diff_subln_g_2, w_branch_a_2, w_branch_b_2, w_branch_c_2, w_out_2,
    norm_ffn_g_2, ffn_up_2, ffn_conv_w_2, ffn_conv_b_2, ffn_down_2, final_norm_g_2,
):
    x = first_block(
        x, c, ctx, c_ctx, w_ada, b_ada, norm_mix, norm_ffn, w_in, b_gate, attn_sink, dn_conv,
        dn_a_log_f, dn_dt_bias_f, dn_a_log_b, dn_dt_bias_b, dn_norm, w_br_attn, w_br_dn, w_out,
        peer_wq, peer_keys, peer_u, peer_v, final_norm,
    )
    return second_block(
        x, norm_mix_g_2, w_in_2, b_gate_2, rg_conv_w_2, rg_conv_b_2, rg_w_a_2, rg_b_a_2,
        rg_w_x_2, rg_b_x_2, rg_lambda_2, diff_lq1_2, diff_lk1_2, diff_lq2_2, diff_lk2_2,
        diff_subln_g_2, w_branch_a_2, w_branch_b_2, w_branch_c_2, w_out_2, norm_ffn_g_2,
        ffn_up_2, ffn_conv_w_2, ffn_conv_b_2, ffn_down_2, final_norm_g_2,
    )


_drawn_inputs = setup_inputs


def setup_inputs(seed=0):
    import zlib

    import numpy as np

    out = dict(_drawn_inputs(seed))
    spreads = {}
    factors = {'b_gate': 3.833, 'attn_sink': 8.0}
    for name, (base, spread) in spreads.items():
        noise = np.random.default_rng([zlib.crc32(name.encode()), seed]).standard_normal(out[name].shape)
        drawn = base * np.exp(spread * noise) if base else spread * noise
        out[name] = jnp.asarray(drawn.astype(out[name].dtype))
    for name, factor in factors.items():
        out[name] = (out[name] * factor).astype(out[name].dtype)
    return out
```

```python
from contextlib import ExitStack

import numpy as np
import concourse.bass as bass
from concourse import mybir

F32 = mybir.dt.float32
U32 = mybir.dt.uint32
ALU = mybir.AluOpType
ACT = mybir.ActivationFunctionType
AX = mybir.AxisListType.X

P = 128
D = 1024
KT = D // P
S = 256
EPS = 1e-6
NEG = -1e30

LAM_INIT = 0.2
RING = 8
N_ADA, N_WIN, N_BR, N_OUT, N_WQ, N_KEYS, N_PEER, N_IN2, N_RGW, N_BR2, N_OUT2, N_FFN = np.cumsum(
    [0, 48, 39, 8, 8, 8, 2, 256, 64, 2, 16, 8]).tolist()
FF = 2816
FT = FF // P
N_ALL = N_FFN + 3 * FT

COLS = dict(c2=16, b_ada=48, norm_mix=8, norm_ffn=8, final_norm=8, b_gate=16, conv=60, a_log=8, dt=8,
            sink=8, dn_norm=1, norm_mix2=8, b_gate2=24, rg_conv=32, rg_conv_b=8, rg_ba=8, rg_bx=8,
            rg_lambda=8, lam=256, subln=1, norm_ffn2=8, ff_conv=132, ff_conv_b=44, final2=8)
COL_AT = dict(zip(COLS, np.cumsum([0] + list(COLS.values())).tolist()))
N_COLS = sum(COLS.values())
MATS = dict(ident=128, ones=128, iota=128, alibi=512, eps=1)
MATS1 = dict(tri=256, level=14 * 128)
MATSA = dict(perm=128, cos=256, sin=256, band=1024)
MAT_AT = dict(zip(MATS, np.cumsum([0] + list(MATS.values())).tolist()))
MAT1_AT = dict(zip(MATS1, np.cumsum([0] + list(MATS1.values())).tolist()))
MATA_AT = dict(zip(MATSA, np.cumsum([0] + list(MATSA.values())).tolist()))

SEMS = """params_in x_in out_written tiles_done phase
silu_c mod_bank_free mod_rows mod_cols mod_ready
squares sums roots inverse normed
proj_free padded conv_free conv_done conv_used projected
ab_ready decay_in decay_sums decay_ready tail_gap
l2_squares l2_sums l2_roots l2_done
swap_done roped
score_done logits_out max_ready exped sums_done turned turned_out weighted o_scaled o_turned o_moved
tok_turned tok_ready k_products gb_ready g_rows gaps decays mask_ready y_done y_out p_done
inv_ready wu_done wu_ready scan_ws v_new scan_o scan_s state_ready o_part
head_sq head_stat head_root head_normed head_turned dn_ready
merged resid route_q route_scores scores_out ranked ranks_turned ranks_out gate_in gate_exp
hot1_ready hot2_ready key2_ready pool_step w_psum w_out gelu_done gated
dve_chain act_chain
rg_in rg_conv_done rg_gates rg_sig rg_coeff rg_mult rg_ln rg_pow rg_square lam_exp
logits2 probs2 maps2 o2_stat o2_root o2_ready ff_out ff_conv ff_taps ff_gelu ff_act final_done""".split()


def build(nc, wstream, x_t, cols_in, mats_in, mats1_in, matsa_in, out):
    ctx = ExitStack()
    with ctx:
        arena = ctx.enter_context(nc.sbuf_tensor("arena", [P, 53200], F32))
        ps = ctx.enter_context(nc.psum_tensor("banks", [P, 8, 512], F32))
        sem = {n: ctx.enter_context(nc.semaphore(n)) for n in SEMS}
        loaded = [ctx.enter_context(nc.semaphore(f"slot{s}_loaded")) for s in range(RING)]

        holes = [[0, 53200]]

        def take(n):
            for h in holes:
                if h[1] >= n:
                    at = h[0]
                    h[0] += n
                    h[1] -= n
                    return at
            raise MemoryError(f"arena: {n} of {holes}")

        def give(at, n):
            holes.append([at, n])
            holes.sort()
            for a in range(len(holes) - 1, 0, -1):
                if holes[a - 1][0] + holes[a - 1][1] == holes[a][0]:
                    holes[a - 1][1] += holes.pop(a)[1]

        held = {}
        tops = [53200]

        def buf(name, *dims):
            n = int(np.prod(dims))
            at = take(n)
            held[name] = (at, n)
            v = arena[:, at:at + n]
            if len(dims) > 1:
                names = "abcd"[:len(dims)]
                v = v.rearrange(f"p ({' '.join(names)}) -> p {' '.join(names)}", **dict(zip(names[1:], dims[1:])))
            return v

        def top(name, *dims):
            n = int(np.prod(dims))
            h = holes[-1]
            assert h[1] >= n and h[0] + h[1] == tops[0], (name, holes)
            h[1] -= n
            tops[0] -= n
            holes_low = tops[0]
            v = arena[:, holes_low:holes_low + n]
            if len(dims) > 1:
                names = "abcd"[:len(dims)]
                v = v.rearrange(f"p ({' '.join(names)}) -> p {' '.join(names)}", **dict(zip(names[1:], dims[1:])))
            return v

        def release(*names):
            for n in names:
                give(*held.pop(n))

        def bc(ap, axis, n):
            return ap.unsqueeze(axis).to_broadcast([*ap.shape[:axis], n, *ap.shape[axis:]])

        def bank(b, *dims):
            v = ps[:, b, 0:int(np.prod(dims))]
            names = "abcd"[:len(dims)]
            if len(dims) > 1:
                v = v.rearrange(f"p ({' '.join(names)}) -> p {' '.join(names)}", **dict(zip(names[1:], dims[1:])))
            return v

        ring = buf("ring", RING, 1024)
        colbuf = buf("cols", N_COLS)
        mats = buf("mats", sum(MATS.values()))
        small = buf("small", 96)
        modT = buf("modT", 48, 2)
        gain1 = buf("gain1", 2, KT)
        gain2 = buf("gain2", KT)
        root = buf("root", 512)
        rstd = buf("rstd", 512)
        xc = buf("xc", KT, 2 * S)
        mats1 = buf("mats1", sum(MATS1.values()))

        def col(name, *dims):
            v = colbuf[:, COL_AT[name]:COL_AT[name] + COLS[name]]
            if dims:
                names = "abcd"[:len(dims)]
                v = v.rearrange(f"p ({' '.join(names)}) -> p {' '.join(names)}", **dict(zip(names[1:], dims[1:])))
            return v

        def mat(name):
            if name in MATS:
                return mats[:, MAT_AT[name]:MAT_AT[name] + MATS[name]]
            if name in MATS1:
                return mats1[:, MAT1_AT[name]:MAT1_AT[name] + MATS1[name]]
            return matsa[:, MATA_AT[name]:MATA_AT[name] + MATSA[name]]

        ident, ones = mat("ident"), mat("ones")

        eps = mat("eps")
        modrow = buf("modrow", 6144)
        csT = buf("csT", KT, 2)
        release("modrow", "csT")
        gatesT = buf("gatesT", 16, S)
        oaT = buf("oaT", 4, S)
        odT = buf("odT", 4, S)
        szT = buf("szT", 4, S)
        qdT = buf("qdT", 4, S)
        kdT = buf("kdT", 4, 2 * S)
        ab = buf("ab", 4, 16)
        vdT = buf("vdT", 4, 2 * S)
        qaT = buf("qaT", 4, S)
        kaT = buf("kaT", 2 * S)
        vtm = buf("vtm", 4, P)
        matsa = buf("matsa", sum(MATSA.values()))
        sq = buf("sq", KT, 2 * S)
        hT = buf("hT", KT, 2 * S)
        pad = buf("pad", 2, 2, 260)
        cvo = buf("cvo", 2, 2, S)
        release("sq", "hT", "pad", "cvo")
        swp = buf("swp", 2, S)
        logit = buf("logit", 4, 512)
        turn = buf("turn", 2, 4, P)
        otm = buf("otm", 2, 512)
        l2r = buf("l2r", 2, 512)
        l2q = buf("l2q", 2, 512)
        stat = [{n: small[:, 16 + 24 * d + 4 * i:20 + 24 * d + 4 * i] for i, n in enumerate(("mx", "nm", "sk", "rs", "ri", "es"))}
                for d in range(2)]
        release("swp", "logit", "turn", "otm", "l2r", "l2q", "qaT", "kaT", "vtm", "matsa")
        dec = {n: buf("dec_" + n, 4, 8) for n in ("g", "beta", "G", "eG", "eT", "tail", "kbe", "t1", "t2")}
        ktok = buf("ktok", 4, 4, P)
        vtok = buf("vtok", 4, 4, P)
        release("vdT")
        wt = buf("wt", 8, 4, P)
        uu = buf("uu", 8, 4, P)
        at = buf("at", 4, 4, P)
        pair = [{n: buf(f"{n}{d}", 4, P) for n in ("A", "M", "T", "Z", "Y", "R")} for d in range(2)]
        gbr = [buf(f"gbr{d}", 4, P) for d in range(2)]
        state = [buf(f"state{d}", 4, P) for d in range(2)]
        vnew = [buf(f"vnew{d}", 4, P) for d in range(2)]
        osum = buf("osum", 2, 4, P)

        release("ab", "qdT", "kdT", "szT", "mats1", *("dec_" + n for n in dec), "ktok", "vtok", "wt", "uu", "at",
                *(f"{n}{d}" for d in range(2) for n in ("A", "M", "T", "Z", "Y", "R", "gbr", "state", "vnew")), "osum")
        res = top("res", KT, S)
        h2T = top("h2T", KT, S)
        rT = top("rT", 3, S)
        yT = buf("yT", KT, S)
        sq2 = buf("sq2", KT, S)
        qpT = buf("qpT", KT, S)
        sc = buf("sc", 2, 16, P)
        v16 = buf("v16", 16, 16)
        i16 = buf("i16", 16, 16)
        i16f = buf("i16f", 16, 16)
        cand = buf("cand", 8, 16, 16)
        b16 = buf("b16", 8, 16)
        c16 = buf("c16", 8, 16)
        pick = buf("pick", 8, 16)
        pickf = buf("pickf", 8, 16)
        hot = buf("hot", 8, 16, 16)
        rank = buf("rank", 2, 3, 8, 16)
        gsum = buf("gsum", 8)
        release("yT", "sq2", "qpT", "sc", "v16", "i16", "i16f", "cand", "b16", "c16", "pick", "pickf", "hot", "rank",
                "gsum", "oaT", "odT", "gatesT", "xc")
        W = buf("W", S, P)
        hot1 = buf("hot1", 8, P)
        hot2 = buf("hot2", 8, P)
        release("hot1", "hot2")
        gelu = buf("gelu", 2, S)
        gated = buf("gated", 2, S)
        release("W", "gelu", "gated")
        x2T = buf("x2T", KT, S)
        sq3 = buf("sq3", KT, S)
        h3T = h2T
        g2T = buf("g2T", 24, S)
        q2 = [buf(f"q2{i}", 4, S) for i in range(2)]
        k2 = [buf(f"k2{i}", 4, S) for i in range(2)]
        v2 = [buf(f"v2{i}", 2, 512) for i in range(2)]
        rxp = buf("rxp", KT, S + 3)
        rgl = buf("rgl", KT, S)
        xr = buf("xr", KT, S)
        rr = sq3
        ii = buf("ii", KT, S)
        dca = buf("dca", KT, S)
        thn = buf("thn", KT, S)
        o2 = [buf(f"o2{i}", 2, 512) for i in range(2)]
        o2T = [buf(f"o2T{i}", 4, S) for i in range(2)]
        lg = buf("lg", 2, 4, S)
        tn2 = buf("tn2", 2, 2, P)
        vec = buf("vec", 400)
        release("rxp", "xr", "ii", "dca", "thn", "q20", "q21", "k20", "k21", "v20", "v21", "o20", "o21")
        y2T = buf("y2T", KT, S)
        h4T = buf("h4T", KT, S)
        upp = buf("upp", 2, 2, S + 2)
        upc = buf("upc", 2, 2, S)
        fft = buf("fft", 2, S)
        outb = buf("outb", KT, S)

        qd_flat, kd_flat = (v.rearrange("p a b -> p (a b)") for v in (qdT, kdT))
        tri = mat("tri").rearrange("p (d i) -> p d i", d=2)
        level = mat("level").rearrange("p (d l i) -> p d l i", d=2, l=7)
        band = mat("band").rearrange("p (q k) -> p q k", q=2)
        chunks = (2, 3, 0, 1)
        scan = (chunks, (3, 2, 1, 0))
        tile_at = lambda n: ring[:, n % RING, :]
        FFN_HEAD = [(N_FFN, 0), (N_FFN + 1, 1)]
        before = lambda s: max(n for n in range(N_FFN) if n % RING == s) + 1
        loads = lambda s: len(range(s, N_FFN, RING))

        block = ctx.enter_context(nc.Block())

        @block.sync
        def _(sp):
            sp.dma_start(colbuf, cols_in).then_inc(sem["params_in"], 16)
            sp.dma_start(mats, mats_in).then_inc(sem["params_in"], 16)
            for n in range(RING):
                sp.dma_start(tile_at(n), wstream[n]).then_inc(loaded[n], 16)
            sp.dma_start(xc.rearrange("p a b -> p (a b)"), x_t).then_inc(sem["x_in"], 16)
            sp.dma_start(mats1, mats1_in).then_inc(sem["x_in"], 16)
            sp.dma_start(matsa, matsa_in).then_inc(sem["x_in"], 16)
            with sp.Fori(1, N_FFN // RING) as i:
                for s in range(RING):
                    sp.wait_ge(sem["tiles_done"], (i - 1) * RING + s + 1)
                    sp.dma_start(ring[:, s, :], wstream[i * RING + s]).then_inc(loaded[s], 16)
            for n in range(N_FFN // RING * RING, N_FFN):
                sp.wait_ge(sem["tiles_done"], n - RING + 1)
                sp.dma_start(tile_at(n), wstream[n]).then_inc(loaded[n % RING], 16)
            for n, s in FFN_HEAD:
                sp.wait_ge(sem["tiles_done"], before(s))
                sp.dma_start(ring[:, s, :], wstream[n]).then_inc(loaded[s], 16)
            for q in range(6):
                sp.wait_ge(sem["tiles_done"], before(2 + q))
                sp.dma_start(ring[:, 2 + q, :], wstream[N_FFN + 2 + q]).then_inc(loaded[2 + q], 16)
            with sp.Fori(1, FT // 2 - 1) as i:
                for q in range(6):
                    sp.wait_ge(sem["tiles_done"], N_FFN + 2 + 6 * (i - 1) + q + 1)
                    sp.dma_start(ring[:, 2 + q, :], wstream[N_FFN + 2 + i * 6 + q]).then_inc(loaded[2 + q], 16)
            for q in range(4):
                n = N_ALL - 4 + q
                sp.wait_ge(sem["tiles_done"], n - 6 + 1)
                sp.dma_start(ring[:, 2 + q, :], wstream[n]).then_inc(loaded[2 + q], 16)
            for half in range(2):
                sp.wait_ge(sem["final_done"], half + 1)
                sp.dma_start(out[:, 4 * S * half:4 * S * half + 4 * S],
                             outb[:, 4 * half:4 * half + 4, :].rearrange("p a b -> p (a b)")).then_inc(sem["out_written"], 16)
            sp.wait_ge(sem["out_written"], 32)

        def phase_end(eng, n):
            eng.drain().then_inc(sem["phase"], 1)
            eng.wait_ge(sem["phase"], 4 * n)

        @block.tensor
        def _(pe):
            def tile_ready(n):
                pe.wait_ge(loaded[n % RING], 16 * (n // RING + 1))

            pe.wait_ge(sem["silu_c"], 1)
            with pe.Fori(0, 6) as i:
                for half in range(2):
                    pe.wait_ge(sem["mod_bank_free"], 2 * i + half + 1)
                    for q in range(4):
                        s = 4 * half + q
                        pe.wait_ge(loaded[s], 16 * i + 16)
                        for k in range(2):
                            mm = pe.matmul(ps[0:2, half, :], csT[:, 2 * q + k, :], ring[:, s, 512 * k:512 * k + 512],
                                           start=(q == 0 and k == 0), stop=(q == 3 and k == 1))
                        mm.then_inc(sem["tiles_done"], 1)
            pe.wait_ge(sem["mod_bank_free"], 14)
            for t in range(48):
                mm = pe.matmul(ps[:, 2, 2 * t:2 * t + 2], modrow[0:2, P * t:P * t + P], ident[0:2, 0:2],
                               start=True, stop=True)
            mm.then_inc(sem["mod_cols"], 1)

            def sum_squares(r, n, b=3):
                for k in range(KT):
                    pe.wait_ge(sem["squares"], KT * r + k + 1)
                    mm = pe.matmul(ps[:, b, 0:n], ones, sq[:, k, 0:n], start=(k == 0), stop=(k == KT - 1))
                mm.then_inc(sem["sums"], 1)

            sum_squares(0, 512)
            pe.wait_ge(sem["normed"], 1)
            for t in range(39):
                n = N_WIN + t
                b = 4 + t % 4
                pe.wait_ge(sem["proj_free"], t + 1)
                tile_ready(n)
                w = tile_at(n)
                if t in (5, 22):
                    m = P if t == 5 else 16
                    for tt in range(4):
                        for k in range(KT):
                            mm = pe.matmul(ps[:, b, m * tt:m * tt + m], hT[:, k, P * tt:P * tt + P],
                                           w[:, P * k:P * k + m], start=(k == 0), stop=(k == KT - 1))
                else:
                    m = 512 if t == 4 or 10 <= t < 18 else S
                    for k in range(KT):
                        mm = pe.matmul(ps[:, b, 0:m], w[:, P * k:P * k + P], hT[:, k, 0:m],
                                       start=(k == 0), stop=(k == KT - 1))
                mm.then_inc(sem["tiles_done"], 1)
            phase_end(pe, 1)

            for t in range(5):
                if t >= 2:
                    pe.wait_ge(sem["roped"], t - 1)
                src = qaT[:, t, :] if t < 4 else kaT[:, 0:S]
                pe.matmul(ps[:, 6 + t % 2, 0:S], mat("perm"), src, start=True, stop=True).then_inc(sem["swap_done"], 1)
            for c in range(6):
                pe.wait_ge(sem["l2_squares"], c + 1)
                pe.matmul(ps[:, c, :], ones, l2q[:, c % 2, :], start=True, stop=True).then_inc(sem["l2_sums"], 1)

            def scores(g):
                qt, kv = g // 2, g % 2
                for t in range(4):
                    if g == 0 and t == 0:
                        pe.wait_ge(sem["roped"], 5)
                        pe.wait_ge(sem["l2_done"], 6)
                    if g:
                        pe.wait_ge(sem["logits_out"], 4 * (g - 1) + t + 1)
                    r = slice(64 * kv, 64 * kv + 64)
                    pe.matmul(ps[:, t, :], qaT[r, t, P * qt:P * qt + P], kaT[r, :], start=True, stop=True).then_inc(
                        sem["score_done"], 1)

            def turn_probs(u):
                pe.wait_ge(sem["exped"], u + 1)
                if u >= 2:
                    pe.wait_ge(sem["turned_out"], u - 1)
                for c in range(4):
                    mm = pe.transpose(ps[:, 4 + u % 2, P * c:P * c + P], logit[:, u % 4, P * c:P * c + P], ident)
                mm.then_inc(sem["turned"], 1)

            def weigh(u):
                g = u // 4
                pe.wait_ge(sem["turned_out"], u + 1)
                if u % 4 == 0 and g >= 2:
                    pe.wait_ge(sem["o_scaled"], g - 1)
                for c in range(4):
                    mm = pe.matmul(ps[:, 6 + g % 2, 64 * (u % 4):64 * (u % 4) + 64], turn[:, u % 2, c, :],
                                   vtm[:, c, 64 * (g % 2):64 * (g % 2) + 64], start=(c == 0), stop=(c == 3))
                mm.then_inc(sem["weighted"], 1)

            scores(0)
            for g in range(4):
                if g < 3:
                    scores(g + 1)
                for t in range(4):
                    turn_probs(4 * g + t)
                    if t:
                        weigh(4 * g + t - 1)
                weigh(4 * g + 3)
            pe.wait_ge(sem["o_scaled"], 4)
            for qt in range(2):
                for f in range(4):
                    mm = pe.transpose(ps[:, qt, P * f:P * f + P], otm[:, qt, P * f:P * f + P], ident)
                mm.then_inc(sem["o_turned"], 1)
            phase_end(pe, 2)

            for n in range(8):
                if n >= 2:
                    pe.wait_ge(sem["tok_ready"], n - 1)
                src = kdT if n < 4 else vdT
                for h in range(4):
                    mm = pe.transpose(ps[:, 4 + n % 2, P * h:P * h + P], src[:, h, P * (n % 4):P * (n % 4) + P], ident)
                mm.then_inc(sem["tok_turned"], 1)
            pe.wait_ge(sem["decay_in"], 1)
            for d in range(2):
                pe.matmul(ps[:, 0, 16 * d:16 * d + 16], tri[:, d, :], dec["g"][:, :, 4 * d:4 * d + 4], start=True, stop=True)
            pe.matmul(ps[:, 0, 32:64], ones, dec["g"], start=True, stop=True).then_inc(sem["decay_sums"], 1)
            pe.wait_ge(sem["decay_ready"], 1)

            for n, tt in enumerate(chunks):
                c = slice(P * tt, P * tt + P)
                if n:
                    pe.wait_ge(sem["inv_ready"], 2 * n)
                for h in range(4):
                    mm = pe.matmul(ps[:, 0, P * h:P * h + P], kdT[:, h, c], kdT[:, h, c], start=True, stop=True)
                if tt < 2:
                    for h in range(4):
                        mm = pe.matmul(ps[:, 1, P * h:P * h + P], kdT[:, h, c], qdT[:, h, c], start=True, stop=True)
                mm.then_inc(sem["k_products"], 1)
                for d in range(2):
                    pe.wait_ge(sem["gb_ready"], 2 * n + d + 1)
                    for h in range(4):
                        mm = pe.matmul(ps[:, 2 + d, P * h:P * h + P], gbr[d][:, h, :], tri[:, d, :], start=True, stop=True)
                    mm.then_inc(sem["g_rows"], 1)
                for l in range(7):
                    for d in range(2):
                        b = pair[d]
                        pe.wait_ge(sem["mask_ready"], 14 * n + 2 * l + d + 1)
                        if l == 0:
                            if n:
                                pe.wait_ge(sem["wu_ready"], 2 * (n - 1) + d + 1)
                            for h in range(4):
                                mm = pe.matmul(ps[:, 4 + d, P * h:P * h + P], b["M"][:, h, :], ident, start=True, stop=True)
                            mm.then_inc(sem["y_done"], 1)
                            continue
                        for h in range(4):
                            mm = pe.matmul(ps[:, 4 + d, P * h:P * h + P], b["M"][:, h, :], b["Z"][:, h, :], start=True, stop=True)
                        mm.then_inc(sem["y_done"], 1)
                    for d in range(2):
                        if l == 0:
                            continue
                        b = pair[d]
                        pe.wait_ge(sem["y_out"], 12 * n + 2 * (l - 1) + d + 1)
                        for h in range(4):
                            mm = pe.matmul(ps[:, d, P * h:P * h + P], b["T"][:, h, :], b["Y"][:, h, :], start=True, stop=True)
                        if l < 6:
                            for h in range(4):
                                mm = pe.matmul(ps[:, 2 + d, P * h:P * h + P], b["Y"][:, h, :], b["T"][:, h, :], start=True, stop=True)
                        mm.then_inc(sem["p_done"], 1)
                for d in range(2):
                    b = pair[d]
                    pe.wait_ge(sem["inv_ready"], 2 * n + d + 1)
                    for h in range(4):
                        pe.matmul(ps[:, 4 + d, P * h:P * h + P], b["M"][:, h, :], b["Z"][:, h, :], start=True, stop=True)
                    for h in range(4):
                        mm = pe.matmul(ps[:, 6 + d, P * h:P * h + P], b["Z"][:, h, :], b["T"][:, h, :], start=True, stop=True)
                    mm.then_inc(sem["wu_done"], 1)

            pe.wait_ge(sem["wu_ready"], 8)
            for st in range(4):
                for d in range(2):
                    tt = scan[d][st]
                    g = 4 * d + tt
                    pe.wait_ge(sem["state_ready"], 2 * st + d + 1)
                    for h in range(4):
                        mm = pe.matmul(ps[:, 4 * d, P * h:P * h + P], wt[:, g, h, :], state[d][:, h, :], start=True, stop=True)
                    mm.then_inc(sem["scan_ws"], 1)
                    if tt < 2:
                        for h in range(4):
                            pe.matmul(ps[:, 4 * d + 1, P * h:P * h + P], qdT[:, h, P * tt:P * tt + P], state[d][:, h, :],
                                      start=True, stop=True)
                for d in range(2):
                    tt = scan[d][st]
                    pe.wait_ge(sem["v_new"], 2 * st + d + 1)
                    if st < 3:
                        for h in range(4):
                            mm = pe.matmul(ps[:, 4 * d + 3, P * h:P * h + P], pair[d]["R"][:, h, :], vnew[d][:, h, :],
                                           start=True, stop=True)
                        mm.then_inc(sem["scan_s"], 1)
                    if tt < 2:
                        for h in range(4):
                            mm = pe.matmul(ps[:, 4 * d + 2, P * h:P * h + P], at[:, 2 * d + tt, h, :], vnew[d][:, h, :],
                                           start=True, stop=True)
                        mm.then_inc(sem["scan_o"], 1)
            pe.wait_ge(sem["head_normed"], 1)
            for tt in range(2):
                for h in range(4):
                    mm = pe.transpose(ps[:, tt, P * h:P * h + P], osum[:, tt, h, :], ident)
                mm.then_inc(sem["head_turned"], 1)
            phase_end(pe, 3)

            for d in range(KT):
                tile_ready(N_BR + d)
                w = tile_at(N_BR + d)
                if d >= 4:
                    pe.wait_ge(sem["merged"], d - 3)
                for k in range(4):
                    pe.matmul(ps[:, d % 4, 0:S], w[:, P * k:P * k + P], oaT[:, k, :], start=(k == 0), stop=(k == 3))
                for k in range(4):
                    mm = pe.matmul(ps[:, d % 4, S:2 * S], w[:, 512 + P * k:512 + P * k + P], odT[:, k, :],
                                   start=(k == 0), stop=(k == 3))
                mm.then_inc(sem["tiles_done"], 1)

            def full(n, src, b, free=None):
                tile_ready(n)
                if free:
                    pe.wait_ge(*free)
                w = tile_at(n)
                for k in range(KT):
                    mm = pe.matmul(ps[:, b, 0:S], w[:, P * k:P * k + P], src[:, k, :], start=(k == 0), stop=(k == KT - 1))
                mm.then_inc(sem["tiles_done"], 1)

            pe.wait_ge(sem["merged"], KT)
            for d in range(KT):
                full(N_OUT + d, yT, 4 + d % 4, (sem["resid"], d - 3) if d >= 4 else None)

            def sum_squares2(r, src, b=3):
                for k in range(KT):
                    pe.wait_ge(sem["squares"], KT * r + k + 1)
                    mm = pe.matmul(ps[:, b, 0:S], ones, src[:, k, :], start=(k == 0), stop=(k == KT - 1))
                mm.then_inc(sem["sums"], 1)

            sum_squares2(1, sq2)
            pe.wait_ge(sem["normed"], 2)
            for h in range(KT):
                full(N_WQ + h, h2T, 4 + h % 4, (sem["route_q"], h - 3) if h >= 4 else None)
            for h in range(8):
                pe.wait_ge(sem["route_q"], h + 1)
                if h % 4 == 0:
                    tile_ready(N_KEYS + h // 4)
                for tt in range(2):
                    j = 2 * h + tt
                    if j >= 4:
                        pe.wait_ge(sem["scores_out"], j - 3)
                    pe.matmul(ps[:, j % 4, 0:S], qpT[:, h, P * tt:P * tt + P],
                              tile_at(N_KEYS + h // 4)[:, S * (h % 4):S * (h % 4) + S], start=True, stop=True).then_inc(
                                  sem["route_scores"], 1)
                if h % 4 == 3:
                    pe.drain().then_inc(sem["tiles_done"], 1)
            for tt in range(2):
                pe.wait_ge(sem["ranked"], tt + 1)
                for c in range(3):
                    mm = pe.transpose(ps[:, 4 + tt, P * c:P * c + P], rank[:, tt, c, :, :].rearrange("p a b -> p (a b)"), ident)
                mm.then_inc(sem["ranks_turned"], 1)
            phase_end(pe, 4)

            with pe.Fori(0, S // 8) as i:
                for t in range(8):
                    pe.wait_ge(sem["hot1_ready"], 8 * i + t + 1)
                    pe.wait_ge(sem["hot2_ready"], 8 * i + t + 1)
                    if t % 4 == 0:
                        pe.wait_ge(sem["w_out"], 2 * i + t // 4 + 1)
                    pe.matmul(ps[:, 6 + t // 4, P * (t % 4):P * (t % 4) + P], hot1[:, t, :], hot2[:, t, :],
                              start=True, stop=True).then_inc(sem["w_psum"], 1)

            pe.wait_ge(sem["w_out"], 2 + S // 4)

            def experts_up(slot, count, b, free):
                pe.wait_ge(loaded[slot], count)
                pe.wait_ge(sem["gelu_done"], free)
                for k in range(KT):
                    mm = pe.matmul(ps[:, 4 + b, 0:S], ring[:, slot, P * k:P * k + P], h2T[:, k, :],
                                   start=(k == 0), stop=(k == KT - 1))
                mm.then_inc(sem["tiles_done"], 1)

            def experts_down(slot, count, b, ready, first=False, last=False):
                pe.wait_ge(loaded[slot], count)
                pe.wait_ge(sem["gated"], ready)
                for d in range(KT):
                    mm = pe.matmul(ps[:, d // 2, S * (d % 2):S * (d % 2) + S], ring[:, slot, P * d:P * d + P], gated[:, b, :],
                                   start=(first and d % 2 == 0), stop=last, skip_group_check=True)
                mm.then_inc(sem["tiles_done"], 1)

            at_n = lambda n: (n % RING, 16 * (n // RING + 1))
            experts_up(*at_n(N_PEER), 0, 1)
            for j in range(1, 4):
                experts_up(*at_n(N_PEER + 2 * j - 1), j % 2, j + 1)
                experts_down(*at_n(N_PEER + 2 * j), (j - 1) % 2, j, first=(j == 1))
            with pe.Fori(1, P // 4) as i:
                for jj in range(4):
                    n = N_PEER + 2 * jj - 1
                    experts_up(n % RING, 16 * (n // RING + 1) + 16 * i, jj % 2, 4 * i + jj + 1)
                    experts_down((n + 1) % RING, 16 * ((n + 1) // RING + 1) + 16 * i, (jj - 1) % 2, 4 * i + jj)
            experts_down(*at_n(N_PEER + 255), 1, P, last=True)
            sum_squares2(2, sq3, 5)
            phase_end(pe, 5)

            sum_squares2(3, sq3, 3)
            pe.wait_ge(sem["normed"], 4)
            for t in range(64):
                n = N_IN2 + t
                free = (sem["proj_free"], 39 + t + 1)
                if t // 4 in (6, 9):
                    tile_ready(n)
                    pe.wait_ge(*free)
                    for tt in range(2):
                        for k in range(KT):
                            mm = pe.matmul(ps[:, 4 + t % 4, P * tt:P * tt + P], h3T[:, k, P * tt:P * tt + P],
                                           tile_at(n)[:, P * k:P * k + P], start=(k == 0), stop=(k == KT - 1))
                    mm.then_inc(sem["tiles_done"], 1)
                else:
                    full(n, h3T, 4 + t % 4, free)
            tile_ready(N_RGW)
            tile_ready(N_RGW + 1)
            pe.wait_ge(sem["rg_conv_done"], KT)
            for j in range(KT):
                if j >= 4:
                    pe.wait_ge(sem["rg_sig"], j - 3)
                a = pe.matmul(ps[:, j % 4, 0:S], tile_at(N_RGW)[:, P * j:P * j + P], xr[:, j, :], start=True, stop=True)
                x = pe.matmul(ps[:, j % 4, S:2 * S], tile_at(N_RGW + 1)[:, P * j:P * j + P], xr[:, j, :], start=True, stop=True)
                if j == KT - 1:
                    a.then_inc(sem["tiles_done"], 1)
                    x.then_inc(sem["tiles_done"], 1)
                else:
                    x.then_inc(sem["rg_gates"], 1)

            def scores2(g):
                qt = g // 2 % 2
                for t in range(4):
                    u = 4 * (g % 2) + t
                    r = slice(64 * (u % 2), 64 * (u % 2) + 64)
                    if g:
                        pe.wait_ge(sem["logits2"], 4 * (g - 1) + t + 1)
                    else:
                        pe.wait_ge(sem["rg_sig"], KT)
                    pe.matmul(ps[:, t, 0:S], q2[g // 4][r, u // 2, P * qt:P * qt + P], k2[g // 4][r, u // 2, :],
                              start=True, stop=True).then_inc(sem["score_done"], 1)

            def turn2(v, g, t):
                pe.wait_ge(sem["probs2"], v + 1)
                if v >= 2:
                    pe.wait_ge(sem["turned_out"], 16 + v - 1)
                for c in range(2):
                    mm = pe.transpose(ps[:, 4 + v % 2, P * c:P * c + P], lg[:, g % 2, t, P * c:P * c + P], ident)
                mm.then_inc(sem["turned"], 1)

            def weigh2(v, g, t):
                pe.wait_ge(sem["turned_out"], 16 + v + 1)
                if g >= 2 and t == 0:
                    pe.wait_ge(sem["o_scaled"], 4 + g - 1)
                m = 64 if g < 4 else P
                at0 = (256 * (g % 2) + 64 * t) if g < 4 else (256 * (g % 2) + P * (t // 2))
                o = 64 * t if g < 4 else P * (t // 2)
                for c in range(2):
                    mm = pe.matmul(ps[:, 6 + g % 2, o:o + m], tn2[:, v % 2, c, :], v2[g // 4][:, c, at0:at0 + m],
                                   start=(c == 0), stop=(c == 1))
                mm.then_inc(sem["weighted"], 1)

            scores2(0)
            v = 0
            for g in range(8):
                if g < 7:
                    scores2(g + 1)
                ts = (0, 1, 2, 3) if g < 4 else (0, 2)
                for n, t in enumerate(ts):
                    turn2(v + n, g, t)
                    if n:
                        weigh2(v + n - 1, g, ts[n - 1])
                weigh2(v + len(ts) - 1, g, ts[-1])
                v += len(ts)
            pe.wait_ge(sem["o2_ready"], 1)
            for m in range(2):
                for qt in range(2):
                    for f in range(4):
                        mm = pe.transpose(ps[:, 2 * m + qt, P * f:P * f + P], o2[m][:, qt, P * f:P * f + P], ident)
                    mm.then_inc(sem["o_turned"], 1)
            phase_end(pe, 6)

            for d in range(KT):
                n = N_BR2 + 2 * d
                b = 2 * (d % 2)
                tile_ready(n)
                if d >= 2:
                    pe.wait_ge(sem["merged"], KT + d - 1)
                for m in range(2):
                    for k in range(4):
                        mm = pe.matmul(ps[:, b, S * m:S * m + S], tile_at(n)[:, 512 * m + P * k:512 * m + P * k + P], o2T[m][:, k, :],
                                       start=(k == 0), stop=(k == 3))
                mm.then_inc(sem["tiles_done"], 1)
                full(n + 1, rgl, b + 1)
            pe.wait_ge(sem["merged"], 2 * KT)
            for d in range(KT):
                full(N_OUT2 + d, y2T, 4 + d % 4, (sem["resid"], 2 * KT + d - 3) if d >= 4 else None)
            sum_squares2(4, sq3, 3)
            pe.wait_ge(sem["normed"], 5)

            def ffn_up(slots, counts, b, free):
                for m in range(2):
                    pe.wait_ge(loaded[slots[m]], counts[m])
                    if m == 0:
                        pe.wait_ge(sem["ff_out"], free)
                    for k in range(KT):
                        mm = pe.matmul(ps[:, 4 + b, S * m:S * m + S], ring[:, slots[m], P * k:P * k + P], h4T[:, k, :],
                                       start=(k == 0), stop=(k == KT - 1))
                    mm.then_inc(sem["tiles_done"], 1)

            def ffn_down(slot, count, b, ready, first=False, last=False):
                pe.wait_ge(loaded[slot], count)
                pe.wait_ge(sem["ff_act"], ready)
                for d in range(KT):
                    mm = pe.matmul(ps[:, d // 2, S * (d % 2):S * (d % 2) + S], ring[:, slot, P * d:P * d + P], fft[:, b, :],
                                   start=(first and d % 2 == 0), stop=last, skip_group_check=True)
                mm.then_inc(sem["tiles_done"], 1)

            nth = lambda s, i: 16 * (loads(s) + 1) + 16 * i
            ffn_up((0, 1), (nth(0, 0), nth(1, 0)), 0, 1)
            for i in (0,):
                ffn_up((2, 3), (nth(2, i), nth(3, i)), 1, 2)
                ffn_down(4, nth(4, i), 0, 1, first=True)
                ffn_up((5, 6), (nth(5, i), nth(6, i)), 0, 3)
                ffn_down(7, nth(7, i), 1, 2)
            with pe.Fori(1, FT // 2 - 1) as i:
                ffn_up((2, 3), (nth(2, i), nth(3, i)), 1, 2 * i + 2)
                ffn_down(4, nth(4, i), 0, 2 * i + 1)
                ffn_up((5, 6), (nth(5, i), nth(6, i)), 0, 2 * i + 3)
                ffn_down(7, nth(7, i), 1, 2 * i + 2)
            i = FT // 2 - 1
            ffn_up((2, 3), (nth(2, i), nth(3, i)), 1, 2 * i + 2)
            ffn_down(4, nth(4, i), 0, 2 * i + 1)
            ffn_down(5, nth(5, i), 1, 2 * i + 2, last=True)
            sum_squares2(5, sq3, 6)

        @block.scalar
        def _(act):
            def link(ins):
                link.n += 1
                ins.then_inc(sem["act_chain"], 1)
                act.wait_ge(sem["act_chain"], link.n)
            link.n = 0

            act.sem_inc(sem["mod_bank_free"], 2)
            act.sem_inc(sem["proj_free"], 4)
            act.wait_ge(sem["params_in"], 32)
            act.activation(csT, col("c2", KT, 2), ACT.Silu).then_inc(sem["silu_c"], 1)
            with act.Fori(0, 12) as i:
                act.wait_ge(sem["tiles_done"], 4 * i + 4)
                act.activation(modrow[0:2, bass.ds(i * 512, 512)], ps[0:2, bass.ds(i % 2, 1), :].rearrange("p a b -> p (a b)"), ACT.Copy).then_inc(
                    sem["mod_bank_free"], 1)

            def squares(x, n):
                for k in range(KT):
                    act.activation(sq[:, k, 0:n], x[:, k, 0:n], ACT.Square).then_inc(sem["squares"], 1)

            def roots(r, n, b=3):
                act.wait_ge(sem["sums"], r + 1)
                act.activation(root[:, 0:n], ps[:, b, 0:n], ACT.Sqrt, bias=eps, scale=1.0 / D).then_inc(sem["roots"], 1)

            act.wait_ge(sem["x_in"], 48)
            squares(xc, 512)
            roots(0, 512)
            def conv_silu(j):
                two = 1 if j < 4 else 2
                act.wait_ge(sem["conv_done"], j + 2)
                src = cvo[:, j % 2, 0:two, :]
                if j < 4:
                    dst = qdT[:, j, :].unsqueeze(1)
                else:
                    dst = (kdT if j < 8 else vdT)[:, j % 4, :].rearrange("p (a b) -> p a b", a=2)
                act.activation(dst, src, ACT.Silu).then_inc(sem["conv_used"], 1)

            nconv = 0
            order = list(range(39))
            for t in order:
                b = 4 + t % 4
                act.wait_ge(sem["tiles_done"], N_WIN + t + 1)
                if t < 4:
                    o = act.activation(qaT[:, t, :], ps[:, b, 0:S], ACT.Copy, scale=0.125)
                elif t == 4:
                    o = act.activation(kaT, ps[:, b, :], ACT.Copy)
                elif t == 5:
                    o = act.activation(vtm.rearrange("p a b -> p (a b)"), ps[:, b, :], ACT.Copy)
                elif t < 18:
                    j = t - 6
                    two = 1 if j < 4 else 2
                    act.wait_ge(sem["conv_done"], j)
                    o = act.activation(pad[:, j % 2, 0:two, 2:2 + S], bank(b, 2, S)[:, 0:two, :], ACT.Copy)
                elif t < 22:
                    o = act.activation(szT[:, t - 18, :], ps[:, b, 0:S], ACT.Silu)
                elif t == 22:
                    o = act.activation(ab.rearrange("p a b -> p (a b)"), ps[:, b, 0:64], ACT.Copy)
                else:
                    o = act.activation(gatesT[:, t - 23, :], ps[:, b, 0:S], ACT.Sigmoid,
                                       bias=col("b_gate")[:, t - 23:t - 22])
                o.then_inc(sem["proj_free"], 1)
                if 7 <= t < 19:
                    conv_silu(t - 7)
            phase_end(act, 1)

            for c in range(8):
                if c < 6:
                    if c >= 2:
                        act.wait_ge(sem["l2_sums"], c - 1)
                    src = qd_flat[:, 512 * c:512 * c + 512] if c < 2 else kd_flat[:, 512 * (c - 2):512 * (c - 2) + 512]
                    act.activation(l2q[:, c % 2, :], src, ACT.Square).then_inc(sem["l2_squares"], 1)
                if c >= 2:
                    act.wait_ge(sem["l2_sums"], c - 1)
                    if c >= 4:
                        act.wait_ge(sem["l2_done"], c - 3)
                    act.activation(l2r[:, c % 2, :], ps[:, c - 2, :], ACT.Sqrt, bias=eps).then_inc(sem["l2_roots"], 1)

            for g in range(4):
                st = stat[g % 2]
                act.wait_ge(sem["max_ready"], g + 1)
                for t in range(4):
                    act.activation(logit[:, t, :], logit[:, t, :], ACT.Exp, bias=st["nm"][:, t:t + 1],
                                   accum_out=st["rs"][:, t:t + 1]).then_inc(sem["exped"], 1)
                act.activation(st["es"], st["sk"], ACT.Exp).then_inc(sem["sums_done"], 1)
                for u in range(4 * g, 4 * g + 4):
                    act.wait_ge(sem["turned"], u + 1)
                    if u >= 2:
                        act.wait_ge(sem["weighted"], u - 1)
                    act.activation(turn[:, u % 2, :, :].rearrange("p a b -> p (a b)"), ps[:, 4 + u % 2, :], ACT.Copy).then_inc(
                        sem["turned_out"], 1)
            for qt in range(2):
                act.wait_ge(sem["o_turned"], qt + 1)
                act.activation(oaT[:, :, P * qt:P * qt + P], bank(qt, 4, P), ACT.Copy).then_inc(sem["o_moved"], 1)
            phase_end(act, 2)

            act.activation(dec["beta"], ab[:, :, 8:16], ACT.Sigmoid).then_inc(sem["act_chain"], 1)
            act.activation(small[:, 64:72], col("a_log"), ACT.Exp).then_inc(sem["act_chain"], 1)
            act.wait_ge(sem["ab_ready"], 1)
            act.activation(dec["t2"], dec["t2"], ACT.Exp, scale=-1.0).then_inc(sem["act_chain"], 1)
            act.wait_ge(sem["act_chain"], 3)
            act.activation(dec["t2"], dec["t2"], ACT.Ln, bias=1.0).then_inc(sem["act_chain"], 1)
            for n in range(8):
                act.wait_ge(sem["tok_turned"], n + 1)
                dst = (ktok if n < 4 else vtok)[:, n % 4, :, :].rearrange("p a b -> p (a b)")
                act.activation(dst, ps[:, 4 + n % 2, :], ACT.Copy).then_inc(sem["tok_ready"], 1)
            act.wait_ge(sem["decay_sums"], 1)
            for d in range(2):
                act.activation(dec["G"][:, :, 4 * d:4 * d + 4], ps[:, 0, 16 * d:16 * d + 16].rearrange("p (a b) -> p a b", a=4), ACT.Copy)
            act.activation(dec["eT"], ps[:, 0, 32:64].rearrange("p (a b) -> p a b", a=4), ACT.Copy).then_inc(sem["decay_ready"], 1)
            act.wait_ge(sem["decay_ready"], 1)
            act.activation(dec["eG"], dec["G"], ACT.Exp).then_inc(sem["act_chain"], 1)
            act.wait_ge(sem["tail_gap"], 1)
            act.activation(dec["tail"], dec["tail"], ACT.Exp)
            act.activation(dec["eT"], dec["eT"], ACT.Exp).then_inc(sem["act_chain"], 1)

            for n, tt in enumerate(chunks):
                for d in range(2):
                    b = pair[d]
                    act.wait_ge(sem["gaps"], 2 * n + d + 1)
                    act.activation(b["Y"], b["Y"], ACT.Exp, scale=-1.0)
                    act.activation(b["R"], b["R"], ACT.Exp).then_inc(sem["decays"], 1)
                for l in range(1, 7):
                    for d in range(2):
                        act.wait_ge(sem["y_done"], 14 * n + 2 * l + d + 1)
                        act.activation(pair[d]["Y"].rearrange("p a b -> p (a b)"), ps[:, 4 + d, :], ACT.Copy).then_inc(sem["y_out"], 1)
                for d in range(2):
                    act.wait_ge(sem["wu_done"], 2 * n + d + 1)
                    act.activation(wt[:, 4 * d + tt, :, :], bank(4 + d, 4, P), ACT.Copy)
                    act.activation(uu[:, 4 * d + tt, :, :], bank(6 + d, 4, P), ACT.Copy).then_inc(sem["wu_ready"], 1)
            act.wait_ge(sem["head_stat"], 1)
            act.activation(small[:, 72:80], small[:, 72:80], ACT.Sqrt, bias=eps, scale=1.0 / P).then_inc(sem["head_root"], 1)
            phase_end(act, 3)

            for k in range(KT):
                act.wait_ge(sem["resid"], k + 1)
                act.activation(sq2[:, k, :], res[:, k, :], ACT.Square).then_inc(sem["squares"], 1)
            roots(1, S)
            for h in range(KT):
                act.wait_ge(sem["tiles_done"], N_WQ + h + 1)
                act.activation(qpT[:, h, :], ps[:, 4 + h % 4, 0:S], ACT.Copy).then_inc(sem["route_q"], 1)
            for j in range(16):
                act.wait_ge(sem["route_scores"], j + 1)
                act.activation(sc[:, j % 2, 2 * (j // 2):2 * (j // 2) + 2, :], bank(j % 4, 2, P), ACT.Copy).then_inc(
                    sem["scores_out"], 1)
            for tt in range(2):
                act.wait_ge(sem["gate_in"], tt + 1)
                act.activation(b16, b16, ACT.Exp).then_inc(sem["gate_exp"], 1)
            for tt in range(2):
                act.wait_ge(sem["ranks_turned"], tt + 1)
                act.activation(rT[:, :, P * tt:P * tt + P], bank(4 + tt, 3, P), ACT.Copy).then_inc(sem["ranks_out"], 1)
            act.sem_inc(sem["w_out"], 2)
            act.sem_inc(sem["gelu_done"], 2)
            phase_end(act, 4)

            Wflat = W.rearrange("p a b -> p (a b)")
            with act.Fori(0, S // 8) as i:
                for half in range(2):
                    act.wait_ge(sem["w_psum"], 8 * i + 4 * half + 12)
                    act.activation(Wflat[:, bass.ds(i * 1024 + 512 * half, 512)], ps[:, 6 + half, :], ACT.Copy).then_inc(
                        sem["w_out"], 1)

            def expert_gelu(done, b, free):
                act.wait_ge(sem["tiles_done"], done)
                act.wait_ge(sem["gated"], free)
                act.activation(gelu[:, b, :], ps[:, 4 + b, 0:S], ACT.Gelu_apprx_tanh).then_inc(sem["gelu_done"], 1)

            for j in range(4):
                act.wait_ge(sem["tiles_done"], N_PEER + max(2 * j - 1, 0) + 1)
                if j >= 2:
                    act.wait_ge(sem["gated"], j - 1)
                act.activation(gelu[:, j % 2, :], ps[:, 4 + j % 2, 0:S], ACT.Gelu_apprx_tanh).then_inc(sem["gelu_done"], 1)
            with act.Fori(1, P // 4) as i:
                for jj in range(4):
                    expert_gelu(N_PEER + 8 * i + 2 * jj, jj % 2, 4 * i + jj - 1)
            for k in range(KT):
                act.wait_ge(sem["resid"], KT + k + 1)
                act.activation(sq3[:, k, :], res[:, k, :], ACT.Square).then_inc(sem["squares"], 1)
            roots(2, S, 5)
            phase_end(act, 5)

            for k in range(KT):
                act.activation(sq3[:, k, :], x2T[:, k, :], ACT.Square).then_inc(sem["squares"], 1)
            roots(3, S, 3)
            act.wait_ge(sem["normed"], 4)
            for t in range(64):
                act.wait_ge(sem["tiles_done"], N_IN2 + t + 1)
                src = ps[:, 4 + t % 4, 0:S]
                kind, f = t // 4, t % 4
                if kind < 2:
                    o = act.activation(rxp[:, t, 3:3 + S], src, ACT.Copy)
                elif kind < 4:
                    o = act.activation(rgl[:, t - 8, :], src, ACT.Gelu_apprx_tanh)
                elif kind in (4, 7):
                    o = act.activation(q2[kind // 7][:, f, :], src, ACT.Copy, scale=0.125)
                elif kind in (5, 8):
                    o = act.activation(k2[kind // 8][:, f, :], src, ACT.Copy)
                elif kind in (6, 9):
                    o = act.activation(v2[kind // 9][:, :, P * f:P * f + P], bank(4 + f, 2, P), ACT.Copy)
                else:
                    o = act.activation(g2T[:, t - 40, :], src, ACT.Sigmoid, bias=col("b_gate2")[:, t - 40:t - 39])
                o.then_inc(sem["proj_free"], 1)
            for j in range(KT):
                if j < KT - 1:
                    act.wait_ge(sem["rg_gates"], j + 1)
                else:
                    act.wait_ge(sem["tiles_done"], N_BR2)
                act.activation(rr[:, j, :], ps[:, j % 4, 0:S], ACT.Sigmoid, bias=col("rg_ba")[:, j:j + 1])
                act.activation(ii[:, j, :], ps[:, j % 4, S:2 * S], ACT.Sigmoid, bias=col("rg_bx")[:, j:j + 1]).then_inc(sem["rg_sig"], 1)
            act.wait_ge(sem["rg_in"], 1)
            act.activation(vec[:, 8:16], vec[:, 8:16], ACT.Exp, scale=-1.0).then_inc(sem["act_chain"], 1)
            act.activation(vec[:, 32:34], vec[:, 32:34], ACT.Exp).then_inc(sem["lam_exp"], 1)
            act.wait_ge(sem["act_chain"], 7)
            act.activation(vec[:, 8:16], vec[:, 8:16], ACT.Ln, bias=1.0).then_inc(sem["rg_ln"], 1)
            act.wait_ge(sem["rg_coeff"], 1)
            act.wait_ge(sem["rg_sig"], KT)
            for j in range(KT):
                act.activation(dca[:, j, :], rr[:, j, :], ACT.Exp, scale=vec[:, 16 + j:17 + j])
                act.activation(thn[:, j, :], rr[:, j, :], ACT.Tanh, scale=vec[:, 24 + j:25 + j]).then_inc(sem["rg_pow"], 1)
            act.wait_ge(sem["rg_square"], 1)
            act.activation(thn, thn, ACT.Sqrt).then_inc(sem["rg_mult"], 1)

            v = 0
            for g in range(8):
                st = stat[g % 2]
                act.wait_ge(sem["max_ready"], 4 + g + 1)
                for t in range(4):
                    act.activation(lg[:, g % 2, t, :], lg[:, g % 2, t, :], ACT.Exp, bias=st["nm"][:, t:t + 1],
                                   accum_out=st["rs"][:, t:t + 1]).then_inc(sem["probs2" if g < 4 else "maps2"], 1)
                for t in range(4 if g < 4 else 2):
                    act.wait_ge(sem["turned"], 16 + v + 1)
                    if v >= 2:
                        act.wait_ge(sem["weighted"], 16 + v - 1)
                    act.activation(tn2[:, v % 2, :, :], bank(4 + v % 2, 2, P), ACT.Copy).then_inc(sem["turned_out"], 1)
                    v += 1
            act.wait_ge(sem["o2_stat"], 1)
            act.activation(vec[:, 40:48], vec[:, 40:48], ACT.Sqrt, bias=eps, scale=1.0 / P).then_inc(sem["o2_root"], 1)
            for m in range(2):
                for qt in range(2):
                    act.wait_ge(sem["o_turned"], 2 + 2 * m + qt + 1)
                    dst = o2T[m][:, :, P * qt:P * qt + P]
                    if m == 0:
                        o = act.activation(dst, bank(qt, 4, P), ACT.Copy)
                    else:
                        o = act.activation(dst, bank(2 + qt, 4, P), ACT.Identity, scale=vec[:, 48:49])
                    o.then_inc(sem["o_moved"], 1)
            phase_end(act, 6)

            for k in range(KT):
                act.wait_ge(sem["resid"], 2 * KT + k + 1)
                act.activation(sq3[:, k, :], res[:, k, :], ACT.Square).then_inc(sem["squares"], 1)
            roots(4, S, 3)

            act.sem_inc(sem["ff_out"], 2)

            def up_out(done, b, free):
                act.wait_ge(sem["tiles_done"], done)
                act.wait_ge(sem["ff_conv"], free)
                act.activation(upp[:, b, :, 2:2 + S], bank(4 + b, 2, S), ACT.Copy).then_inc(sem["ff_out"], 1)

            def ff_gelu(ready, b):
                act.wait_ge(sem["ff_conv"], ready)
                act.activation(upc[:, b, 0, :], upc[:, b, 0, :], ACT.Gelu_apprx_tanh).then_inc(sem["ff_gelu"], 1)

            up_out(N_FFN + 2, 0, 1)
            up_out(N_FFN + 4, 1, 2)
            ff_gelu(3, 0)
            with act.Fori(1, FT // 2) as i:
                up_out(N_FFN + 6 * i + 1, 0, 2 * i + 1)
                ff_gelu(2 * i + 2, 1)
                up_out(N_FFN + 6 * i + 4, 1, 2 * i + 2)
                ff_gelu(2 * i + 3, 0)
            ff_gelu(FT + 2, 1)
            for k in range(KT):
                act.wait_ge(sem["resid"], 3 * KT + k + 1)
                act.activation(sq3[:, k, :], res[:, k, :], ACT.Square).then_inc(sem["squares"], 1)
            roots(5, S, 6)

        @block.vector
        def _(dve):
            def link(ins):
                link.n += 1
                ins.then_inc(sem["dve_chain"], 1)
                dve.wait_ge(sem["dve_chain"], link.n)
            link.n = 0

            link(dve.memset(pad, 0.0))
            dve.wait_ge(sem["mod_cols"], 1)
            link(dve.tensor_tensor(modT, bank(2, 48, 2), bc(col("b_ada"), 2, 2), ALU.add))
            link(dve.tensor_scalar(gain1, modT[:, 8:16, :].rearrange("p a b -> p b a"), 1.0, None, ALU.add))
            dve.tensor_tensor(gain1, gain1, bc(col("norm_mix"), 1, 2), ALU.mult)
            dve.tensor_scalar(small[:, 0:8], modT[:, 32:40, 0], 1.0, None, ALU.add)
            link(dve.memset(small[:, 8:9], 0.0))
            link(dve.tensor_tensor(gain2, small[:, 0:8], col("norm_ffn"), ALU.mult))

            def inverse(r, n):
                dve.wait_ge(sem["roots"], r + 1)
                link(dve.reciprocal(rstd[:, 0:n], root[:, 0:n]))

            inverse(0, 512)
            for half in range(2):
                c = slice(S * half, S * half + S)
                for k in range(KT):
                    dve.scalar_tensor_tensor(hT[:, k, c], xc[:, k, c], gain1[:, half, k:k + 1], rstd[:, c],
                                             ALU.mult, ALU.mult)
                link(dve.memset(small[:, 8:9], 0.0))
                for k in range(KT):
                    o = dve.tensor_scalar(hT[:, k, c], hT[:, k, c], modT[:, k, half:half + 1], None, ALU.add)
            o.then_inc(sem["normed"], 1)
            taps = col("conv", 12, 5)
            dve.sem_inc(sem["conv_done"], 1)
            for j in range(12):
                two = 1 if j < 4 else 2
                dve.wait_ge(sem["proj_free"], 4 + 6 + j + 1)
                if j >= 2:
                    dve.wait_ge(sem["conv_used"], j - 1)
                dst = cvo[:, j % 2, 0:two, :]
                src = lambda d: pad[:, j % 2, 0:two, d:d + S]
                link(dve.tensor_scalar(dst, src(0), taps[:, j, 0:1], None, ALU.mult))
                for d in range(1, 5):
                    o = dve.scalar_tensor_tensor(dst, src(d), taps[:, j, d:d + 1], dst, ALU.mult, ALU.add)
                    if d < 4:
                        link(o)
                o.then_inc(sem["conv_done"], 1)
            phase_end(dve, 1)

            for t in range(5):
                dve.wait_ge(sem["swap_done"], t + 1)
                v = qaT[:, t, :] if t < 4 else kaT[:, 0:S]
                dve.tensor_tensor(v, v, mat("cos"), ALU.mult)
                link(dve.tensor_tensor(swp[:, t % 2, :], ps[:, 6 + t % 2, 0:S], mat("sin"), ALU.mult))
                dve.tensor_tensor(v, v, swp[:, t % 2, :], ALU.add).then_inc(sem["roped"], 1)
            for c in range(6):
                dve.wait_ge(sem["l2_roots"], c + 1)
                link(dve.reciprocal(l2r[:, c % 2, :], l2r[:, c % 2, :]))
                v = qd_flat[:, 512 * c:512 * c + 512] if c < 2 else kd_flat[:, 512 * (c - 2):512 * (c - 2) + 512]
                dve.scalar_tensor_tensor(v, v, float(P) ** -0.5 if c < 2 else 1.0, l2r[:, c % 2, :],
                                         ALU.mult, ALU.mult).then_inc(sem["l2_done"], 1)

            def logits(g):
                st = stat[g % 2]
                for t in range(4):
                    dve.wait_ge(sem["score_done"], 4 * g + t + 1)
                    if g:
                        dve.wait_ge(sem["turned"], 4 * (g - 1) + t + 1)
                    dve.tensor_tensor_reduce(logit[:, t, :], ps[:, t, :], band[:, g // 2, :], 1.0, NEG, ALU.add, ALU.max,
                                             st["mx"][:, t:t + 1]).then_inc(sem["logits_out"], 1)

            def maxima(g):
                st = stat[g % 2]
                sink = col("sink")[:, 4 * (g % 2):4 * (g % 2) + 4]
                dve.wait_ge(sem["logits_out"], 4 * g + 4)
                link(dve.tensor_tensor(st["mx"], st["mx"], sink, ALU.max))
                dve.tensor_scalar(st["nm"], st["mx"], -1.0, None, ALU.mult)
                dve.tensor_tensor(st["sk"], sink, st["mx"], ALU.subtract).then_inc(sem["max_ready"], 1)

            def weights(g):
                st = stat[g % 2]
                dve.wait_ge(sem["sums_done"], g + 1)
                link(dve.tensor_tensor(st["ri"], st["rs"], st["es"], ALU.add))
                link(dve.reciprocal(st["ri"], st["ri"]))

            logits(0)
            for g in range(4):
                maxima(g)
                weights(g)
                if g < 3:
                    logits(g + 1)
                dve.wait_ge(sem["weighted"], 4 * g + 4)
                o = otm[:, g // 2, 256 * (g % 2):256 * (g % 2) + 256].rearrange("p (a b) -> p a b", a=4)
                dve.tensor_tensor(o, bank(6 + g % 2, 4, 64), bc(stat[g % 2]["ri"], 2, 64), ALU.mult).then_inc(sem["o_scaled"], 1)
            phase_end(dve, 2)

            a = ab[:, :, 0:8]
            link(dve.tensor_tensor(dec["t1"], a, bc(col("dt"), 1, 4), ALU.add))
            dve.scalar_tensor_tensor(dec["t2"], dec["t1"], -1.0, dec["t1"], ALU.mult, ALU.max).then_inc(sem["ab_ready"], 1)
            link(dve.tensor_scalar(dec["t1"], dec["t1"], 0.0, None, ALU.max))
            dve.wait_ge(sem["act_chain"], 4)
            link(dve.tensor_tensor(dec["t1"], dec["t1"], dec["t2"], ALU.add))
            dve.scalar_tensor_tensor(dec["g"], dec["t1"], -1.0, bc(small[:, 64:72], 1, 4), ALU.mult, ALU.mult).then_inc(
                sem["decay_in"], 1)
            dve.wait_ge(sem["decay_ready"], 1)
            dve.tensor_tensor(dec["tail"], dec["eT"], dec["G"], ALU.subtract).then_inc(sem["tail_gap"], 1)
            dve.wait_ge(sem["act_chain"], 5)
            dve.tensor_tensor(dec["kbe"], dec["beta"], dec["eG"], ALU.mult)
            dve.memset(state[0], 0.0)
            dve.memset(state[1], 0.0)
            dve.wait_ge(sem["decay_in"], 1)
            for d in range(2):
                o = dve.tensor_copy(gbr[d], bc(dec["g"][:, chunks[0], 4 * d:4 * d + 4], 2, P))
                o.then_inc(sem["gb_ready"], 1)
            dve.wait_ge(sem["act_chain"], 6)

            for n, tt in enumerate(chunks):
                head = lambda name, d: bc(dec[name][:, tt, 4 * d:4 * d + 4], 2, P)
                for d in range(2):
                    b = pair[d]
                    dve.wait_ge(sem["g_rows"], 2 * n + d + 1)
                    if n:
                        dve.wait_ge(sem["wu_done"], 2 * (n - 1) + d + 1)
                    link(dve.tensor_tensor(b["R"], bank(2 + d, 4, P), head("G", d), ALU.subtract))
                    dve.tensor_scalar(b["Y"], b["R"], 0.0, None, ALU.max)
                    dve.tensor_scalar(b["R"], b["R"], 0.0, None, ALU.min).then_inc(sem["gaps"], 1)
                    if n < 3:
                        dve.tensor_copy(gbr[d], bc(dec["g"][:, chunks[n + 1], 4 * d:4 * d + 4], 2, P)).then_inc(sem["gb_ready"], 1)
                dve.wait_ge(sem["k_products"], n + 1)
                for d in range(2):
                    b = pair[d]
                    dve.wait_ge(sem["decays"], 2 * n + d + 1)
                    link(dve.tensor_tensor(b["A"], b["Y"], bank(0, 4, P), ALU.mult))
                    link(dve.tensor_tensor(b["A"], b["A"], head("beta", d), ALU.mult))
                    dve.tensor_tensor(b["M"], b["A"], bc(level[:, d, 0, :], 1, 4), ALU.mult).then_inc(sem["mask_ready"], 1)
                    if tt < 2:
                        s = at[:, 2 * d + tt, :, :]
                        link(dve.tensor_tensor(s, b["R"], bank(1, 4, P), ALU.mult))
                        link(dve.tensor_tensor(s, s, bc(tri[:, d, :], 1, 4), ALU.mult))
                for d in range(2):
                    b = pair[d]
                    dve.wait_ge(sem["mask_ready"], 14 * n + d + 1)
                    dve.tensor_tensor(b["T"], bc(ident, 1, 4), b["M"], ALU.subtract)
                    dve.wait_ge(sem["y_done"], 14 * n + d + 1)
                    link(dve.tensor_tensor(b["Z"], bc(ident, 1, 4), bank(4 + d, 4, P), ALU.subtract))
                    dve.tensor_tensor(b["M"], b["A"], bc(level[:, d, 1, :], 1, 4), ALU.mult).then_inc(sem["mask_ready"], 1)
                for l in range(1, 7):
                    for d in range(2):
                        b = pair[d]
                        dve.wait_ge(sem["p_done"], 12 * n + 2 * (l - 1) + d + 1)
                        o = dve.tensor_tensor(b["Z"], b["Z"], bank(d, 4, P), ALU.subtract)
                        if l < 6:
                            dve.tensor_tensor(b["T"], b["T"], bank(2 + d, 4, P), ALU.subtract)
                            dve.tensor_tensor(b["M"], b["A"], bc(level[:, d, l + 1, :], 1, 4), ALU.mult).then_inc(
                                sem["mask_ready"], 1)
                            continue
                        dve.wait_ge(sem["tok_ready"], 8)
                        dve.tensor_tensor(b["M"], ktok[:, tt, :, :], head("kbe", d), ALU.mult)
                        dve.tensor_tensor(b["T"], vtok[:, tt, :, :], head("beta", d), ALU.mult).then_inc(sem["inv_ready"], 1)

            dve.sem_inc(sem["state_ready"], 2)
            for d in range(2):
                dve.tensor_tensor(pair[d]["R"], ktok[:, scan[d][0], :, :], bc(dec["tail"][:, scan[d][0], 4 * d:4 * d + 4], 2, P), ALU.mult)
            for st in range(4):
                for d in range(2):
                    tt = scan[d][st]
                    dve.wait_ge(sem["scan_ws"], 2 * st + d + 1)
                    dve.wait_ge(sem["wu_ready"], 8)
                    dve.tensor_tensor(vnew[d], uu[:, 4 * d + tt, :, :], bank(4 * d, 4, P), ALU.subtract).then_inc(sem["v_new"], 1)
                for d in range(2):
                    tt = scan[d][st]
                    head = lambda name: bc(dec[name][:, tt, 4 * d:4 * d + 4], 2, P)
                    if tt < 2:
                        dve.wait_ge(sem["scan_o"], 2 * (st - 2) + d + 1)
                        t = pair[d]["A"]
                        link(dve.tensor_tensor(t, bank(4 * d + 1, 4, P), head("eG"), ALU.mult))
                        if st == 2:
                            link(dve.tensor_tensor(osum[:, tt, :, :], t, bank(4 * d + 2, 4, P), ALU.add))
                        else:
                            link(dve.tensor_tensor(t, t, bank(4 * d + 2, 4, P), ALU.add))
                            link(dve.tensor_tensor(osum[:, tt, :, :], osum[:, tt, :, :], t, ALU.add))
                    if st < 3:
                        nxt = scan[d][st + 1]
                        dve.wait_ge(sem["scan_s"], 2 * st + d + 1)
                        link(dve.tensor_tensor(state[d], state[d], head("eT"), ALU.mult))
                        dve.tensor_tensor(state[d], state[d], bank(4 * d + 3, 4, P), ALU.add).then_inc(sem["state_ready"], 1)
                        dve.tensor_tensor(pair[d]["R"], ktok[:, nxt, :, :],
                                          bc(dec["tail"][:, nxt, 4 * d:4 * d + 4], 2, P), ALU.mult)
            flat = osum.rearrange("p a b c -> p (a b) c")
            sqo = vnew[0]
            for tt in range(2):
                link(dve.tensor_tensor(sqo, osum[:, tt, :, :], osum[:, tt, :, :], ALU.mult))
                o = dve.tensor_reduce(small[:, 72 + 4 * tt:76 + 4 * tt], sqo, AX, ALU.add)
                if tt == 0:
                    link(o)
            o.then_inc(sem["head_stat"], 1)
            dve.wait_ge(sem["head_root"], 1)
            link(dve.reciprocal(small[:, 72:80], small[:, 72:80]))
            dve.tensor_tensor(flat, flat, bc(small[:, 72:80], 2, P), ALU.mult).then_inc(sem["head_normed"], 1)
            for tt in range(2):
                dve.wait_ge(sem["head_turned"], tt + 1)
                dve.scalar_tensor_tensor(odT[:, :, P * tt:P * tt + P], bank(tt, 4, P), col("dn_norm"),
                                         szT[:, :, P * tt:P * tt + P], ALU.mult, ALU.mult).then_inc(sem["dn_ready"], 1)
            phase_end(dve, 3)

            for d in range(KT):
                dve.wait_ge(sem["tiles_done"], N_BR + d + 1)
                t = root[:, S * (d % 2):S * (d % 2) + S]
                link(dve.tensor_tensor(t, ps[:, d % 4, 0:S], gatesT[:, d, :], ALU.mult))
                link(dve.tensor_tensor(yT[:, d, :], ps[:, d % 4, S:2 * S], gatesT[:, 8 + d, :], ALU.mult))
                dve.tensor_tensor(yT[:, d, :], yT[:, d, :], t, ALU.add).then_inc(sem["merged"], 1)
            for d in range(KT):
                dve.wait_ge(sem["tiles_done"], N_OUT + d + 1)
                dve.scalar_tensor_tensor(res[:, d, :], ps[:, 4 + d % 4, 0:S], modT[:, 16 + d, 0:1], xc[:, d, 0:S],
                                         ALU.mult, ALU.add).then_inc(sem["resid"], 1)

            def norm(r, dst, src, gain, shift=None):
                inverse(r, S)
                for k in range(KT):
                    o = dve.scalar_tensor_tensor(dst[:, k, :], src[:, k, :], gain[:, k:k + 1], rstd[:, 0:S], ALU.mult, ALU.mult)
                if shift is not None:
                    link(o)
                    for k in range(KT):
                        o = dve.tensor_scalar(dst[:, k, :], dst[:, k, :], shift[:, k, 0:1], None, ALU.add)
                return o

            norm(1, h2T, res, gain2, modT[:, 24:32, :]).then_inc(sem["normed"], 1)

            for tt in range(2):
                if tt:
                    dve.wait_ge(sem["ranked"], 1)
                dve.wait_ge(sem["scores_out"], 16)
                u16 = i16.bitcast(U32)
                cu = c16.bitcast(U32)
                pu = pick.bitcast(U32)

                def best(n, vals, idx, src):
                    for r in range(2):
                        c = slice(8 * r, 8 * r + 8)
                        for q in range(n):
                            o = dve.max(vals(q)[:, c], src(q))
                        link(o)
                        for q in range(n):
                            o = dve.max_index(idx(q)[:, c], vals(q)[:, c], src(q))
                        link(o)
                        if r == 0:
                            for q in range(n):
                                o = dve.match_replace(src(q), vals(q)[:, c], src(q), -3e38)
                            link(o)

                best(16, lambda q: v16[:, q, :], lambda q: u16[:, q, :], lambda q: sc[:, tt, q, :])
                dve.tensor_copy(i16f, u16)
                halves = v16.rearrange("p (h e) k -> p h e k", e=2)
                link(dve.tensor_tensor(cand, bc(halves[:, :, 0, :], 3, 16), bc(halves[:, :, 1, :], 2, 16), ALU.add))
                best(8, lambda q: b16[:, q, :], lambda q: cu[:, q, :], lambda q: cand[:, q, :, :].rearrange("p a b -> p (a b)"))
                link(dve.tensor_copy(gsum, b16[:, :, 0]))
                dve.tensor_tensor(b16, b16, bc(gsum, 2, 16), ALU.subtract).then_inc(sem["gate_in"], 1)
                i16h = i16f.rearrange("p (h e) k -> p h e k", e=2)
                for e in range(2):
                    if e == 0:
                        link(dve.tensor_scalar(pu, cu, 4, None, ALU.logical_shift_right))
                    else:
                        link(dve.tensor_scalar(pu, cu, 15, None, ALU.bitwise_and))
                    link(dve.tensor_copy(pickf, pu))
                    iota16 = mat("iota")[:, 0:16]
                    for h in range(8):
                        o = dve.tensor_tensor(hot[:, h, :, :], bc(iota16, 1, 16), bc(pickf[:, h, :], 2, 16), ALU.is_equal)
                    link(o)
                    for h in range(8):
                        o = dve.tensor_tensor(hot[:, h, :, :], hot[:, h, :, :], bc(i16h[:, h, e, :], 1, 16), ALU.mult)
                    link(o)
                    link(dve.tensor_reduce(rank[:, tt, e, :, :], hot, AX, ALU.add))
                dve.wait_ge(sem["gate_exp"], tt + 1)
                link(dve.tensor_reduce(gsum, b16, AX, ALU.add))
                link(dve.reciprocal(gsum, gsum))
                dve.tensor_tensor(rank[:, tt, 2, :, :], b16, bc(gsum, 2, 16), ALU.mult).then_inc(sem["ranked"], 1)
            dve.sem_inc(sem["w_psum"], 8)
            phase_end(dve, 4)

            with dve.Fori(0, S // 8) as i:
                for t in range(8):
                    dve.wait_ge(sem["w_psum"], 8 * i + t + 1)
                    dve.tensor_scalar(hot1[:, t, :], mat("iota"), rT[:, 0, bass.ds(8 * i + t, 1)], rT[:, 2, bass.ds(8 * i + t, 1)],
                                      ALU.is_equal, ALU.mult).then_inc(sem["hot1_ready"], 1)

            def gate(j, b, done, free):
                dve.wait_ge(sem["gelu_done"], done)
                if free is not None:
                    dve.wait_ge(sem["tiles_done"], free)
                dve.tensor_tensor(gated[:, b, :], gelu[:, b, :], W[:, :, bass.ds(j, 1)].rearrange("p a b -> p (a b)"), ALU.mult).then_inc(
                    sem["gated"], 1)

            for j in range(4):
                if j == 0:
                    dve.wait_ge(sem["w_out"], 2 + S // 4)
                gate(j, j % 2, j + 3, N_PEER + 2 * j - 1 if j >= 2 else None)
            with dve.Fori(1, P // 4) as i:
                for jj in range(4):
                    gate(4 * i + jj, jj % 2, 4 * i + jj + 3, N_PEER + 8 * i + 2 * jj - 1)
            dve.wait_ge(sem["tiles_done"], N_IN2)
            for d in range(KT):
                dve.scalar_tensor_tensor(res[:, d, :], ps[:, d // 2, S * (d % 2):S * (d % 2) + S], modT[:, 40 + d, 0:1],
                                         res[:, d, :], ALU.mult, ALU.add).then_inc(sem["resid"], 1)
            norm(2, x2T, res, col("final_norm")).then_inc(sem["normed"], 1)
            phase_end(dve, 5)

            norm(3, h3T, x2T, col("norm_mix2")).then_inc(sem["normed"], 1)
            dve.memset(rxp[:, :, 0:3], 0.0)
            lam = col("rg_lambda")
            link(dve.scalar_tensor_tensor(vec[:, 8:16], lam, -1.0, lam, ALU.mult, ALU.max))
            link(dve.tensor_scalar(vec[:, 0:8], lam, -1.0, 0.0, ALU.mult, ALU.max))
            lam4 = col("lam", 4, 64)
            link(dve.tensor_tensor(vec[:, 64:192].rearrange("p (a b) -> p a b", a=2), lam4[:, 0:2, :], lam4[:, 2:4, :], ALU.mult))
            dve.tensor_reduce(vec[:, 32:34], vec[:, 64:192].rearrange("p (a b) -> p a b", a=2), AX, ALU.add).then_inc(sem["rg_in"], 1)
            taps = col("rg_conv", KT, 4)
            for j in range(KT):
                dve.wait_ge(sem["proj_free"], 4 + 39 + j + 1)
                link(dve.tensor_scalar(xr[:, j, :], rxp[:, j, 0:S], taps[:, j, 0:1], col("rg_conv_b")[:, j:j + 1], ALU.mult, ALU.add))
                for c in range(1, 4):
                    o = dve.scalar_tensor_tensor(xr[:, j, :], rxp[:, j, c:c + S], taps[:, j, c:c + 1], xr[:, j, :], ALU.mult, ALU.add)
                    if c < 3:
                        link(o)
                o.then_inc(sem["rg_conv_done"], 1)
            dve.wait_ge(sem["rg_ln"], 1)
            link(dve.tensor_tensor(vec[:, 0:8], vec[:, 0:8], vec[:, 8:16], ALU.add))
            dve.tensor_scalar(vec[:, 16:24], vec[:, 0:8], -8.0, None, ALU.mult)
            dve.tensor_scalar(vec[:, 24:32], vec[:, 0:8], 8.0, None, ALU.mult).then_inc(sem["rg_coeff"], 1)
            dve.wait_ge(sem["lam_exp"], 1)
            link(dve.tensor_tensor(vec[:, 34:35], vec[:, 33:34], vec[:, 32:33], ALU.subtract))
            dve.tensor_scalar(vec[:, 34:35], vec[:, 34:35], -LAM_INIT, None, ALU.add)
            dve.tensor_scalar(vec[:, 48:49], col("subln"), 1.0 - LAM_INIT, None, ALU.mult)
            flat = lambda v: v.rearrange("p a b -> p (a b)")
            dve.wait_ge(sem["rg_sig"], KT)
            link(dve.tensor_tensor(flat(ii), flat(ii), flat(xr), ALU.mult))
            dve.wait_ge(sem["rg_pow"], KT)
            link(dve.tensor_tensor(flat(xr), flat(dca), flat(dca), ALU.mult))
            dve.scalar_tensor_tensor(flat(thn), flat(xr), 1.0, flat(thn), ALU.add, ALU.mult).then_inc(sem["rg_square"], 1)
            dve.wait_ge(sem["rg_mult"], 1)
            link(dve.tensor_tensor(flat(ii), flat(ii), flat(thn), ALU.mult))
            for j in range(KT):
                o = dve.tensor_tensor_scan(xr[:, j, :], dca[:, j, :], ii[:, j, :], 0.0, ALU.mult, ALU.add)
            link(o)
            dve.tensor_tensor(flat(rgl), flat(rgl), flat(xr), ALU.mult)

            def logits2(g):
                st = stat[g % 2]
                qt = g // 2 % 2
                for t in range(4):
                    u = 4 * (g % 2) + t
                    slope = 2.0 ** -(u + 1) if g < 4 else 2.0 ** (-2.0 * (u // 2 + 1))
                    dve.wait_ge(sem["score_done"], 16 + 4 * g + t + 1)
                    if g >= 2 and t == 0:
                        dve.wait_ge(sem["turned"], 16 + (4 * (g - 1) if g <= 5 else 16 + 2 * (g - 5)))
                    o = dve.scalar_tensor_tensor(lg[:, g % 2, t, :], alibi[:, qt, :], slope, ps[:, t, 0:S], ALU.mult, ALU.add)
                    o.then_inc(sem["logits2"], 1)
                dve.wait_ge(sem["logits2"], 4 * g + 4)
                link(dve.tensor_reduce(st["mx"], lg[:, g % 2, :, :], AX, ALU.max))
                dve.tensor_scalar(st["nm"], st["mx"], -1.0, None, ALU.mult).then_inc(sem["max_ready"], 1)

            alibi = mat("alibi").rearrange("p (q k) -> p q k", q=2)
            logits2(0)
            v = 0
            for g in range(8):
                st = stat[g % 2]
                qt = g // 2 % 2
                if g < 4:
                    dve.wait_ge(sem["probs2"], 4 * g + 4)
                    link(dve.reciprocal(st["ri"], st["rs"]))
                else:
                    dve.wait_ge(sem["maps2"], 4 * (g - 4) + 4)
                    link(dve.reciprocal(st["ri"], st["rs"]))
                    link(dve.tensor_scalar(st["es"], st["ri"], vec[:, 34:35], None, ALU.mult))
                    for t in (0, 2):
                        p0, p1 = lg[:, g % 2, t, :], lg[:, g % 2, t + 1, :]
                        link(dve.tensor_scalar(p0, p0, st["ri"][:, t:t + 1], None, ALU.mult))
                        dve.scalar_tensor_tensor(p0, p1, st["es"][:, t + 1:t + 2], p0, ALU.mult, ALU.add).then_inc(sem["probs2"], 1)
                if g < 7:
                    logits2(g + 1)
                v += 4 if g < 4 else 2
                dve.wait_ge(sem["weighted"], 16 + v)
                c = slice(256 * (g % 2), 256 * (g % 2) + 256)
                if g < 4:
                    o = o2[0][:, qt, c].rearrange("p (a b) -> p a b", a=4)
                    dve.tensor_tensor(o, bank(6 + g % 2, 4, 64), bc(st["ri"], 2, 64), ALU.mult).then_inc(sem["o_scaled"], 1)
                else:
                    dve.tensor_copy(o2[1][:, qt, c], ps[:, 6 + g % 2, 0:256]).then_inc(sem["o_scaled"], 1)
            dve.wait_ge(sem["o_scaled"], 12)
            heads = o2[1].rearrange("p a (b c) -> p (a b) c", b=4)
            tmp = flat(lg[:, 0, :, :]).rearrange("p (a b) -> p a b", a=8)
            link(dve.tensor_tensor(tmp, heads, heads, ALU.mult))
            dve.tensor_reduce(vec[:, 40:48], tmp, AX, ALU.add).then_inc(sem["o2_stat"], 1)
            dve.wait_ge(sem["o2_root"], 1)
            link(dve.reciprocal(vec[:, 40:48], vec[:, 40:48]))
            dve.tensor_tensor(heads, heads, bc(vec[:, 40:48], 2, P), ALU.mult).then_inc(sem["o2_ready"], 1)
            phase_end(dve, 6)

            for d in range(KT):
                dve.wait_ge(sem["tiles_done"], N_BR2 + 2 * d + 2)
                b = 2 * (d % 2)
                y, t = y2T[:, d, :], fft[:, d % 2, :]
                dve.tensor_tensor(t, ps[:, b, 0:S], g2T[:, d, :], ALU.mult)
                link(dve.tensor_tensor(y, ps[:, b, S:2 * S], g2T[:, 16 + d, :], ALU.mult))
                link(dve.tensor_tensor(y, y, t, ALU.add))
                link(dve.tensor_tensor(t, ps[:, b + 1, 0:S], g2T[:, 8 + d, :], ALU.mult))
                dve.tensor_tensor(y, y, t, ALU.add).then_inc(sem["merged"], 1)
            for d in range(KT):
                dve.wait_ge(sem["tiles_done"], N_OUT2 + d + 1)
                dve.tensor_tensor(res[:, d, :], ps[:, 4 + d % 4, 0:S], x2T[:, d, :], ALU.add).then_inc(sem["resid"], 1)
            norm(4, h4T, res, col("norm_ffn2")).then_inc(sem["normed"], 1)
            link(dve.memset(upp[:, :, :, 0:2], 0.0))

            dve.sem_inc(sem["ff_conv"], 2)
            taps3 = col("ff_conv", 44, 3)
            bias3 = col("ff_conv_b")

            def ff_taps(f, b, ready, free):
                dve.wait_ge(sem["ff_out"], ready)
                if free is not None:
                    dve.wait_ge(sem["ff_act"], free)
                one = lambda v, c: v[:, bass.ds(c, 1)]
                for m in range(2):
                    c = f + FT * m
                    dve.tensor_scalar(upc[:, b, m, :], upp[:, b, m, 0:S], one(taps3[:, :, 0], c), one(bias3, c), ALU.mult, ALU.add
                                      ).then_inc(sem["ff_taps"], 1)
                for r in range(1, 3):
                    for m in range(2):
                        c = f + FT * m
                        dve.wait_ge(sem["ff_taps"], 4 * f + 2 * r - 1 + m)
                        o = dve.scalar_tensor_tensor(upc[:, b, m, :], upp[:, b, m, r:r + S], one(taps3[:, :, r], c), upc[:, b, m, :],
                                                     ALU.mult, ALU.add)
                        if r == 1:
                            o.then_inc(sem["ff_taps"], 1)
                o.then_inc(sem["ff_conv"], 1)

            def ff_gate(f, b, ready, free):
                dve.wait_ge(sem["ff_gelu"], ready)
                if free is not None:
                    dve.wait_ge(sem["tiles_done"], free)
                dve.tensor_tensor(fft[:, b, :], upc[:, b, 0, :], upc[:, b, 1, :], ALU.mult).then_inc(sem["ff_act"], 1)

            ff_taps(0, 0, 3, None)
            ff_taps(1, 1, 4, None)
            ff_gate(0, 0, 1, None)
            ff_taps(2, 0, 5, 1)
            ff_gate(1, 1, 2, None)
            ff_taps(3, 1, 6, 2)
            ff_gate(2, 0, 3, N_FFN + 5)
            with dve.Fori(2, FT // 2) as i:
                ff_taps(2 * i, 0, 2 * i + 3, 2 * i - 1)
                ff_gate(2 * i - 1, 1, 2 * i, N_FFN + 6 * i - 4)
                ff_taps(2 * i + 1, 1, 2 * i + 4, 2 * i)
                ff_gate(2 * i, 0, 2 * i + 1, N_FFN + 6 * i - 1)
            ff_gate(FT - 1, 1, FT, N_ALL - 4)
            dve.wait_ge(sem["tiles_done"], N_ALL)
            for d in range(KT):
                dve.tensor_tensor(res[:, d, :], ps[:, d // 2, S * (d % 2):S * (d % 2) + S], res[:, d, :], ALU.add).then_inc(sem["resid"], 1)
            inverse(5, S)
            for k in range(KT):
                o = dve.scalar_tensor_tensor(outb[:, k, :], res[:, k, :], col("final2")[:, k:k + 1], rstd[:, 0:S], ALU.mult, ALU.mult)
                if k % 4 == 3:
                    o.then_inc(sem["final_done"], 1)

        @block.gpsimd
        def _(pool):
            for n in range(1, 5):
                phase_end(pool, n)
            with pool.Fori(0, S // 8) as i:
                for half in range(2):
                    key2 = small[:, 80 + 4 * half:84 + 4 * half]
                    pool.wait_ge(sem["w_psum"], 8 * i + 4 * half + 4)
                    pool.sem_inc(sem["pool_step"], 1)
                    pool.tensor_copy(key2, rT[:, 1, bass.ds(8 * i + 4 * half, 4)]).then_inc(sem["key2_ready"], 1)
                    pool.wait_ge(sem["key2_ready"], 2 * i + half + 1)
                    pool.sem_inc(sem["pool_step"], 1)
                    for t in range(4):
                        pool.tensor_scalar(hot2[:, 4 * half + t, :], mat("iota"), key2[:, t:t + 1], None, ALU.is_equal).then_inc(
                            sem["hot2_ready"], 1)
            for n in range(5, 7):
                phase_end(pool, n)


def col_tiles(w):
    f = w.shape[1] // P
    return w.reshape(KT, P, f, P).transpose(2, 1, 0, 3).reshape(f, P, KT * P)


def columns(v, n):
    return v.reshape(n, P).T


def shape_constants():
    i = np.arange(P)
    ident = np.eye(P)
    d = np.arange(S)
    alibi = np.zeros((P, 2, S))
    band = np.zeros((P, 2, 512))
    for qt in range(2):
        q = qt * P + i[:, None]
        dist = q - d[None, :]
        alibi[:, qt] = np.where(dist >= 0, -dist, NEG)
        band[:, qt, 0:S] = np.where(np.abs(dist) <= 128, 0.0, NEG)
    mats = np.concatenate([ident, np.ones((P, P)), np.tile(i, (P, 1)), alibi.reshape(P, -1),
                           np.full((P, 1), EPS)], 1)
    f = i % 64
    partner = np.where(f % 32 < 16, i + 16, i - 16)
    perm = np.zeros((P, P))
    perm[partner, i] = 1.0
    inv = (np.float32(10000.0) ** (-np.arange(16, dtype=np.float32) / np.float32(16))).astype(np.float32)
    t = np.arange(S)
    pos = np.where((f < 32)[:, None], (t // 64)[None, :], (t % 64)[None, :]).astype(np.float32)
    ang = (pos * inv[f % 16][:, None]).astype(np.float32).astype(np.float64)
    cos, sin = np.cos(ang), np.sin(ang) * np.where(f % 32 < 16, -1.0, 1.0)[:, None]
    tri = np.stack([i[:, None] <= i[None, :], i[:, None] >= i[None, :]], 1)
    level = np.zeros((P, 2, 7, P))
    for l in range(7):
        s = 2 ** l
        low = (i[:, None] // (2 * s) == i[None, :] // (2 * s)) & (i[:, None] // s % 2 == 1) & (i[None, :] // s % 2 == 0)
        level[:, 0, l], level[:, 1, l] = low, low.T
    mats1 = np.concatenate([tri.reshape(P, -1), level.reshape(P, -1)], 1)
    matsa = np.concatenate([perm, cos, sin, band.reshape(P, -1)], 1)
    return mats.astype(np.float32), mats1.astype(np.float32), matsa.astype(np.float32)


def lay_out(a):
    a = {k: np.asarray(v) for k, v in a.items()}
    w_in = a["w_in"][0]
    q = w_in[:, :512].reshape(D, 2, 4, 64).transpose(0, 2, 1, 3).reshape(D, 512)
    small = np.zeros((D, P), np.float32)
    small[:, :16] = w_in[:, 2816:2832]
    win = np.concatenate([q, w_in[:, 512:2816], small, w_in[:, 2832:]], 1)
    ada = a["w_ada"][0].reshape(4, 2, P, 12, 512).transpose(3, 0, 2, 1, 4).reshape(48, P, 1024)
    br = np.concatenate([a["w_br_attn"][0], a["w_br_dn"][0]], 0)
    keys = np.zeros((P, 8, 2, P), np.float32)
    pk = a["peer_keys"][0]
    for half in range(2):
        keys[64 * half:64 * half + 64, :, half] = pk[:, half].transpose(2, 0, 1)
    keys = keys.reshape(P, 2, 1024).transpose(1, 0, 2)
    u = a["peer_u"][0].reshape(P, P, KT, P).transpose(1, 3, 2, 0).reshape(P, P, 1024)
    v = a["peer_v"][0].reshape(P, P, D).transpose(1, 0, 2)
    peer = np.concatenate([u[:1], np.stack([u[1:], v[:-1]], 1).reshape(254, P, 1024), v[-1:]], 0)
    w2 = a["w_in_2"][0]
    in2 = np.concatenate([w2[:, 3072:5120], w2[:, :3072], w2[:, 5120:]], 1)
    rgw = np.zeros((P, 2, 8, P), np.float32)
    for g, name in enumerate(("rg_w_a_2", "rg_w_x_2")):
        w = a[name][0].reshape(8, 2, 64, 64)
        for half in range(2):
            rgw[64 * half:64 * half + 64, g, :, 64 * half:64 * half + 64] = w[:, half].transpose(1, 0, 2)
    rgw = rgw.reshape(P, 2, 1024).transpose(1, 0, 2)
    br2 = np.concatenate([a["w_branch_a_2"][0], a["w_branch_c_2"][0], a["w_branch_b_2"][0]], 0)
    br2 = br2.reshape(2, 8, P, 8, P).transpose(3, 0, 2, 1, 4).reshape(16, P, 1024)
    up = a["ffn_up_2"][0]
    upt = col_tiles(up)
    down = a["ffn_down_2"][0].reshape(FT, P, D)
    ffn = np.concatenate([upt[:1], upt[FT:FT + 1],
                          np.stack([upt[1:FT], upt[FT + 1:], down[:-1]], 1).reshape(3 * FT - 3, P, 1024), down[-1:]], 0)
    wstream = np.concatenate([ada, col_tiles(win), col_tiles(br), col_tiles(a["w_out"][0]), col_tiles(a["peer_wq"][0]),
                              keys, peer, col_tiles(in2), rgw, br2, col_tiles(a["w_out_2"][0]), ffn], 0)
    assert wstream.shape[0] == N_ALL
    x_t = np.stack([a["x"][0], a["ctx"][0]], 0).reshape(2, S, KT, P).transpose(3, 2, 0, 1).reshape(P, -1)
    wide = lambda v: np.broadcast_to(v.reshape(1, -1), (P, v.size))
    c = dict(
        c2=np.stack([a["c"][0], a["c_ctx"]], 0).reshape(2, KT, P).transpose(2, 1, 0).reshape(P, -1),
        b_ada=columns(a["b_ada"][0], 48), norm_mix=columns(a["norm_mix"][0], 8), norm_ffn=columns(a["norm_ffn"][0], 8),
        final_norm=columns(a["final_norm"], 8), b_gate=columns(a["b_gate"][0], 16),
        conv=a["dn_conv"][0].reshape(5, 12, P).transpose(2, 1, 0).reshape(P, -1),
        a_log=wide(np.stack([a["dn_a_log_f"][0], a["dn_a_log_b"][0]])),
        dt=wide(np.stack([a["dn_dt_bias_f"][0], a["dn_dt_bias_b"][0]])),
        sink=wide(a["attn_sink"][0]), dn_norm=columns(a["dn_norm"][0], 1), norm_mix2=columns(a["norm_mix_g_2"][0], 8),
        b_gate2=columns(a["b_gate_2"][0], 24), rg_conv=a["rg_conv_w_2"][0].reshape(4, 8, P).transpose(2, 1, 0).reshape(P, -1),
        rg_conv_b=columns(a["rg_conv_b_2"][0], 8), rg_ba=columns(a["rg_b_a_2"][0], 8), rg_bx=columns(a["rg_b_x_2"][0], 8),
        rg_lambda=columns(a["rg_lambda_2"][0], 8),
        lam=wide(np.concatenate([a["diff_lq1_2"][0], a["diff_lq2_2"][0], a["diff_lk1_2"][0], a["diff_lk2_2"][0]])),
        subln=columns(a["diff_subln_g_2"][0], 1), norm_ffn2=columns(a["norm_ffn_g_2"][0], 8),
        ff_conv=a["ffn_conv_w_2"][0].reshape(3, 44, P).transpose(2, 1, 0).reshape(P, -1),
        ff_conv_b=columns(a["ffn_conv_b_2"][0], 44), final2=columns(a["final_norm_g_2"], 8))
    cols = np.concatenate([c[n] for n in COLS], 1)
    assert cols.shape == (P, N_COLS)
    mats, mats1, matsa = shape_constants()
    return {"wstream": wstream, "x_t": x_t, "cols": cols, "mats": mats, "mats1": mats1, "matsa": matsa}


def kernel(**inputs):
    import concourse.bacc as bacc
    from concourse.bass_utils import run_bass_kernel_spmd

    arrays = {k: np.ascontiguousarray(v) for k, v in lay_out(inputs).items()}
    nc = bacc.Bacc("TRN2", target_bir_lowering=False, num_devices=1)
    args = [nc.dram_tensor(n, v.shape, F32, kind="ExternalInput").ap() for n, v in arrays.items()]
    out = nc.dram_tensor("out_t", (P, KT * S), F32, kind="ExternalOutput").ap()
    build(nc, *args, out)
    got = run_bass_kernel_spmd(nc, [arrays], core_ids=[0]).results[0]["out_t"]
    return np.ascontiguousarray(got.reshape(P, KT, S).transpose(2, 1, 0).reshape(1, S, D))
```

```python
from contextlib import ExitStack

import numpy as np
import concourse.bass as bass
from concourse import mybir

F32 = mybir.dt.float32
F32R = mybir.dt.float32r
U32 = mybir.dt.uint32
ALU = mybir.AluOpType
ACT = mybir.ActivationFunctionType
AX = mybir.AxisListType.X

P = 128
D = 1024
KT = D // P
S = 256
EPS = 1e-6
NEG = -1e30

LAM_INIT = 0.2
RING = 4
N_ADA, N_WIN, N_BR, N_OUT, N_WQ, N_KEYS, N_PEER, N_IN2, N_BR2, N_OUT2, N_FFN = np.cumsum(
    [0, 48, 39, 8, 8, 8, 2, 256, 64, 16, 8]).tolist()
FF = 2816
FT = FF // P
N_ALL = N_FFN + 3 * FT
SPLIT = 2 * (KT * S + 4 * 512 + 2 * S)
ARENA = 53200 - SPLIT
M_PEER, M_IN2, M_FFN, M_ALL = 0, 256, 256 + 64, 256 + 64 + 3 * FT
tile_of = lambda m: m + N_PEER if m < M_FFN else m - M_FFN + N_FFN

COLS = dict(c2=16, b_ada=48, norm_mix=8, norm_ffn=8, final_norm=8, b_gate=16, conv=60, a_log=8, dt=8,
            sink=8, dn_norm=1, norm_mix2=8, b_gate2=24, rg_conv=32, rg_conv_b=8, rg_ba=8, rg_bx=8,
            rg_lambda=8, lam=256, subln=1, norm_ffn2=8, ff_conv=132, ff_conv_b=44, final2=8)
COL_AT = dict(zip(COLS, np.cumsum([0] + list(COLS.values())).tolist()))
N_COLS = sum(COLS.values())
MATS = dict(ident=128, ones=128, iota=128, alibi=512, eps=1)
MATS1 = dict(tri=256, level=14 * 128)
MATSA = dict(perm=128, cos=256, sin=256, band=1024)
MAT_AT = dict(zip(MATS, np.cumsum([0] + list(MATS.values())).tolist()))
MAT1_AT = dict(zip(MATS1, np.cumsum([0] + list(MATS1.values())).tolist()))
MATA_AT = dict(zip(MATSA, np.cumsum([0] + list(MATSA.values())).tolist()))

SEMS = """params_in x_in out_written tiles_done phase
silu_c mod_bank_free mod_cols squares sums roots normed
proj_free conv_done conv_used ab_ready decay_in decay_sums decay_ready tail_gap
l2_squares l2_sums l2_roots l2_done
swap_done roped
score_done logits_out max_ready exped sums_done turned turned_out weighted o_scaled o_turned o_moved
tok_turned tok_ready k_products gb_ready g_rows gaps decays mask_ready late_mask z_ready t_ready y_done y_out p_done
inv_ready wu_done wu_ready scan_ws v_new scan_o scan_s state_ready head_stat head_root head_normed head_turned dn_ready
merged resid route_q route_scores scores_out ranked ranks_turned ranks_out gate_in gate_exp
h_hi h_lo w_hi w_lo half_used g_hi g_lo hot1_ready hot2_ready hot2_late key2_ready pool_step w_psum w_out gelu_done gated
dve_chain act_chain
rgw_in rg_in rg_conv_done rg_gates rg_sig rg_coeff rg_mult rg_ln rg_pow rg_square lam_exp
logits2 probs2 maps2 o2_stat o2_root o2_ready ff_out ff_conv ff_taps ff_gelu ff_act final_done""".split()


def build(nc, wstream, x_t, cols_in, mats_in, mats1_in, matsa_in, out):
    ctx = ExitStack()
    with ctx:
        arena = ctx.enter_context(nc.sbuf_tensor("arena", [P, ARENA], F32))
        split = ctx.enter_context(nc.sbuf_tensor("split", [P, SPLIT], F32R))
        ps = ctx.enter_context(nc.psum_tensor("banks", [P, 8, 512], F32))
        sem = {n: ctx.enter_context(nc.semaphore(n)) for n in SEMS}
        loaded = [ctx.enter_context(nc.semaphore(f"slot{s}_loaded")) for s in range(RING)]

        holes = [[0, ARENA]]

        def take(n):
            for h in holes:
                if h[1] >= n:
                    at = h[0]
                    h[0] += n
                    h[1] -= n
                    return at
            raise MemoryError(f"arena: {n} of {holes}")

        def give(at, n):
            holes.append([at, n])
            holes.sort()
            for a in range(len(holes) - 1, 0, -1):
                if holes[a - 1][0] + holes[a - 1][1] == holes[a][0]:
                    holes[a - 1][1] += holes.pop(a)[1]

        held = {}
        tops = [ARENA]

        def buf(name, *dims):
            n = int(np.prod(dims))
            at = take(n)
            held[name] = (at, n)
            v = arena[:, at:at + n]
            if len(dims) > 1:
                names = "abcd"[:len(dims)]
                v = v.rearrange(f"p ({' '.join(names)}) -> p {' '.join(names)}", **dict(zip(names[1:], dims[1:])))
            return v

        def top(name, *dims):
            n = int(np.prod(dims))
            h = holes[-1]
            assert h[1] >= n and h[0] + h[1] == tops[0], (name, holes)
            h[1] -= n
            tops[0] -= n
            holes_low = tops[0]
            v = arena[:, holes_low:holes_low + n]
            if len(dims) > 1:
                names = "abcd"[:len(dims)]
                v = v.rearrange(f"p ({' '.join(names)}) -> p {' '.join(names)}", **dict(zip(names[1:], dims[1:])))
            return v

        def release(*names):
            for n in names:
                give(*held.pop(n))

        def bc(ap, axis, n):
            return ap.unsqueeze(axis).to_broadcast([*ap.shape[:axis], n, *ap.shape[axis:]])

        def bank(b, *dims):
            v = ps[:, b, 0:int(np.prod(dims))]
            names = "abcd"[:len(dims)]
            if len(dims) > 1:
                v = v.rearrange(f"p ({' '.join(names)}) -> p {' '.join(names)}", **dict(zip(names[1:], dims[1:])))
            return v

        h_parts = split[:, 0:2 * KT * S].rearrange("p (c k t) -> p c k t", c=2, k=KT)
        w_parts = split[:, 2 * KT * S:2 * KT * S + 4096].rearrange("p (c s n) -> p c s n", c=2, s=4)
        g_parts = split[:, 2 * KT * S + 4096:SPLIT].rearrange("p (c b t) -> p c b t", c=2, b=2)
        PASSES = ((0, 0), (0, 1), (1, 0))

        ring = buf("ring", RING, 1024)
        colbuf = buf("cols", N_COLS)
        mats = buf("mats", sum(MATS.values()))
        small = buf("small", 96)
        modT = buf("modT", 48, 2)
        gain1 = buf("gain1", 2, KT)
        gain2 = buf("gain2", KT)
        root = buf("root", 512)
        rstd = buf("rstd", 512)
        xT, ctxT = buf("xT", KT, S), buf("ctxT", KT, S)
        assert held["ctxT"][0] == held["xT"][0] + KT * S
        xc = arena[:, held["xT"][0]:held["xT"][0] + 2 * KT * S].rearrange("p (c k t) -> p c k t", c=2, k=KT)
        mats1 = buf("mats1", sum(MATS1.values()))

        def col(name, *dims):
            v = colbuf[:, COL_AT[name]:COL_AT[name] + COLS[name]]
            if dims:
                names = "abcd"[:len(dims)]
                v = v.rearrange(f"p ({' '.join(names)}) -> p {' '.join(names)}", **dict(zip(names[1:], dims[1:])))
            return v

        def mat(name):
            if name in MATS:
                return mats[:, MAT_AT[name]:MAT_AT[name] + MATS[name]]
            if name in MATS1:
                return mats1[:, MAT1_AT[name]:MAT1_AT[name] + MATS1[name]]
            return matsa[:, MATA_AT[name]:MATA_AT[name] + MATSA[name]]

        ident, ones = mat("ident"), mat("ones")

        eps = mat("eps")
        modrow = buf("modrow", 6144)
        csT = buf("csT", KT, 2)
        release("modrow", "csT")
        gatesT = buf("gatesT", 16, S)
        oaT = buf("oaT", 4, S)
        odT = buf("odT", 4, S)
        szT = buf("szT", 4, S)
        qdT = buf("qdT", 4, S)
        kdT = buf("kdT", 4, 2 * S)
        ab = buf("ab", 4, 16)
        vdT = buf("vdT", 4, 2 * S)
        qaT = buf("qaT", 4, S)
        kaT = buf("kaT", 2 * S)
        vtm = buf("vtm", 4, P)
        matsa = buf("matsa", sum(MATSA.values()))
        sq = buf("sq", KT, 2 * S)
        hT = buf("hT", KT, 2 * S)
        pad = buf("pad", 2, 2, 260)
        cvo = buf("cvo", 2, 2, S)
        release("sq", "hT", "pad", "cvo", "ctxT")
        swp = buf("swp", 2, S)
        logit = buf("logit", 4, 512)
        turn = buf("turn", 2, 4, P)
        otm = buf("otm", 2, 512)
        l2r = buf("l2r", 2, 512)
        l2q = buf("l2q", 2, 512)
        stat = [{n: small[:, 16 + 24 * d + 4 * i:20 + 24 * d + 4 * i] for i, n in enumerate(("mx", "nm", "sk", "rs", "ri", "es"))}
                for d in range(2)]
        release("swp", "logit", "turn", "otm", "l2r", "l2q", "qaT", "kaT", "vtm", "matsa")
        dec = {n: buf("dec_" + n, 4, 8) for n in ("g", "beta", "G", "eG", "eT", "tail", "kbe", "t1", "t2")}
        ktok = buf("ktok", 4, 4, P)
        vtok = buf("vtok", 4, 4, P)
        release("vdT")
        wt = buf("wt", 8, 4, P)
        uu = buf("uu", 8, 4, P)
        at = buf("at", 4, 4, P)
        pair = [{n: buf(f"{n}{d}", 4, P) for n in ("A", "M", "T", "Z", "Y", "R")} for d in range(2)]
        osum = buf("osum", 2, 4, P)
        gbr = [osum[:, d, :, :] for d in range(2)]
        state = [pair[d]["Y"] for d in range(2)]
        vnew = [pair[d]["Z"] for d in range(2)]

        release("ab", "qdT", "kdT", "szT", "mats1", *("dec_" + n for n in dec), "ktok", "vtok", "wt", "uu", "at",
                *(f"{n}{d}" for d in range(2) for n in ("A", "M", "T", "Z", "Y", "R")), "osum")
        res = top("res", KT, S)
        rT = top("rT", 3, S)
        h2T = buf("h2T", KT, S)
        yT = buf("yT", KT, S)
        sq2 = buf("sq2", KT, S)
        qpT = buf("qpT", KT, S)
        sc = buf("sc", 2, 16, P)
        v16 = buf("v16", 16, 16)
        i16 = buf("i16", 16, 16)
        i16f = buf("i16f", 16, 16)
        cand = buf("cand", 8, 16, 16)
        b16 = buf("b16", 8, 16)
        c16 = buf("c16", 8, 16)
        pick = buf("pick", 8, 16)
        pickf = buf("pickf", 8, 16)
        hot = buf("hot", 8, 16, 16)
        rank = buf("rank", 2, 3, 8, 16)
        gsum = buf("gsum", 8)
        release("h2T", "yT", "sq2", "qpT", "sc", "v16", "i16", "i16f", "cand", "b16", "c16", "pick", "pickf", "hot", "rank",
                "gsum", "oaT", "odT", "gatesT", "xT")
        W = buf("W", S, P)
        assert held["rstd"][0] == held["root"][0] + 512
        hot1 = arena[:, held["root"][0]:held["root"][0] + 1024].rearrange("p (a b) -> p a b", a=8)
        hot2 = buf("hot2", 8, P)
        release("hot2")
        gelu = buf("gelu", 2, S)
        gated = buf("gated", 2, S)
        release("W", "gelu", "gated")
        x2T = buf("x2T", KT, S)
        sq3 = buf("sq3", KT, S)
        h3T = buf("h3T", KT, S)
        g2T = buf("g2T", 24, S)
        q2 = [buf(f"q2{i}", 4, S) for i in range(2)]
        k2 = [buf(f"k2{i}", 4, S) for i in range(2)]
        v2 = [buf(f"v2{i}", 2, 512) for i in range(2)]
        rxp = buf("rxp", KT, S + 3)
        rgl = buf("rgl", KT, S)
        xr = buf("xr", KT, S)
        rr = sq3
        thn = arena[:, held["rxp"][0]:held["rxp"][0] + KT * S].rearrange("p (a b) -> p a b", a=KT)
        ii = buf("ii", KT, S)
        dca = buf("dca", KT, S)
        rgw = dca.rearrange("p a b -> p (a b)").rearrange("p (g n) -> p g n", g=2)
        o2 = [buf(f"o2{i}", 2, 512) for i in range(2)]
        o2T = [buf(f"o2T{i}", 4, S) for i in range(2)]
        lg = res.rearrange("p (a b) c -> p a b c", a=2)
        tn2 = buf("tn2", 2, 2, P)
        vec = buf("vec", 400)
        release("rxp", "xr", "ii", "dca", "q20", "q21", "k20", "k21", "v20", "v21", "o20", "o21")
        y2T = buf("y2T", KT, S)
        h4T = buf("h4T", KT, S)
        upp = buf("upp", 2, 2, S + 2)
        upc = buf("upc", 2, 2, S)
        fft = buf("fft", 2, S)
        outb = buf("outb", KT, S)

        qd_flat, kd_flat = (v.rearrange("p a b -> p (a b)") for v in (qdT, kdT))
        tri = mat("tri").rearrange("p (d i) -> p d i", d=2)
        level = mat("level").rearrange("p (d l i) -> p d l i", d=2, l=7)
        band = mat("band").rearrange("p (q k) -> p q k", q=2)
        chunks = (2, 3, 0, 1)
        scan = (chunks, (3, 2, 1, 0))
        tile_at = lambda n: ring[:, n % RING, :]

        block = ctx.enter_context(nc.Block())

        @block.sync
        def _(sp):
            sp.dma_start(colbuf, cols_in).then_inc(sem["params_in"], 16)
            sp.dma_start(mats, mats_in).then_inc(sem["params_in"], 16)
            for n in range(RING):
                sp.dma_start(tile_at(n), wstream[n]).then_inc(loaded[n], 16)
            sp.dma_start(xc.rearrange("p c k t -> p (c k t)"), x_t).then_inc(sem["x_in"], 16)
            sp.dma_start(mats1, mats1_in).then_inc(sem["x_in"], 16)
            sp.dma_start(matsa, matsa_in).then_inc(sem["x_in"], 16)
            def load_freed_by_matmuls(lo, hi):
                n4 = (hi - lo) // RING
                with sp.Fori(0, n4) as i:
                    for n in range(lo, lo + RING):
                        sp.wait_ge(sem["tiles_done"], i * RING + n - RING + 1)
                        sp.dma_start(ring[:, n % RING, :], wstream[i * RING + n]).then_inc(loaded[n % RING], 16)
                for n in range(lo + n4 * RING, hi):
                    sp.wait_ge(sem["tiles_done"], n - RING + 1)
                    sp.dma_start(tile_at(n), wstream[n]).then_inc(loaded[n % RING], 16)

            def load_freed_by_parts(lo, hi, m):
                n4 = (hi - lo) // RING
                with sp.Fori(0, n4) as i:
                    for q in range(RING):
                        sp.wait_ge(sem["w_lo"], i * 2 * RING + 2 * (m + q) + 2)
                        sp.dma_start(ring[:, (lo + q) % RING, :], wstream[i * RING + lo + q]).then_inc(loaded[(lo + q) % RING], 16)
                for q in range(n4 * RING, hi - lo):
                    sp.wait_ge(sem["w_lo"], 2 * (m + q) + 2)
                    sp.dma_start(tile_at(lo + q), wstream[lo + q]).then_inc(loaded[(lo + q) % RING], 16)

            load_freed_by_matmuls(RING, N_PEER + RING)
            load_freed_by_parts(N_PEER + RING, N_IN2 + RING, M_PEER)
            sp.wait_ge(sem["phase"], 4 * 5)
            for g in range(2):
                sp.dma_start(rgw[:, g, :], wstream[N_ALL + g]).then_inc(sem["rgw_in"], 16)
            load_freed_by_parts(N_IN2 + RING, N_BR2 + RING, M_IN2)
            load_freed_by_matmuls(N_BR2 + RING, N_FFN + RING)
            load_freed_by_parts(N_FFN + RING, N_ALL, M_FFN)
            for half in range(2):
                sp.wait_ge(sem["final_done"], half + 1)
                sp.dma_start(out[:, 4 * S * half:4 * S * half + 4 * S],
                             outb[:, 4 * half:4 * half + 4, :].rearrange("p a b -> p (a b)")).then_inc(sem["out_written"], 16)
            sp.wait_ge(sem["out_written"], 32)

        def phase_end(eng, n):
            eng.drain().then_inc(sem["phase"], 1)
            eng.wait_ge(sem["phase"], 4 * n)

        @block.tensor
        def _(pe):
            def tile_ready(n):
                pe.wait_ge(loaded[n % RING], 16 * (n // RING + 1))

            pe.wait_ge(sem["silu_c"], 1)
            with pe.Fori(0, 6) as i:
                for half in range(2):
                    pe.wait_ge(sem["mod_bank_free"], 2 * i + half + 1)
                    for q in range(4):
                        pe.wait_ge(loaded[q], 32 * i + 16 * half + 16)
                        for k in range(2):
                            mm = pe.matmul(ps[0:2, half, :], csT[:, 2 * q + k, :], ring[:, q, 512 * k:512 * k + 512],
                                           start=(q == 0 and k == 0), stop=(q == 3 and k == 1))
                        mm.then_inc(sem["tiles_done"], 1)
            pe.wait_ge(sem["mod_bank_free"], 14)
            for t in range(48):
                mm = pe.matmul(ps[:, 2, 2 * t:2 * t + 2], modrow[0:2, P * t:P * t + P], ident[0:2, 0:2],
                               start=True, stop=True)
            mm.then_inc(sem["mod_cols"], 1)

            def sum_squares(r, n, b=3):
                for k in range(KT):
                    pe.wait_ge(sem["squares"], KT * r + k + 1)
                    mm = pe.matmul(ps[:, b, 0:n], ones, sq[:, k, 0:n], start=(k == 0), stop=(k == KT - 1))
                mm.then_inc(sem["sums"], 1)

            sum_squares(0, 512)
            pe.wait_ge(sem["normed"], 1)
            for t in range(39):
                n = N_WIN + t
                b = 4 + t % 4
                pe.wait_ge(sem["proj_free"], t + 1)
                tile_ready(n)
                w = tile_at(n)
                if t in (5, 22):
                    m = P if t == 5 else 16
                    for tt in range(4):
                        for k in range(KT):
                            mm = pe.matmul(ps[:, b, m * tt:m * tt + m], hT[:, k, P * tt:P * tt + P],
                                           w[:, P * k:P * k + m], start=(k == 0), stop=(k == KT - 1))
                else:
                    m = 512 if t == 4 or 10 <= t < 18 else S
                    for k in range(KT):
                        mm = pe.matmul(ps[:, b, 0:m], w[:, P * k:P * k + P], hT[:, k, 0:m],
                                       start=(k == 0), stop=(k == KT - 1))
                mm.then_inc(sem["tiles_done"], 1)
            phase_end(pe, 1)

            for t in range(5):
                if t >= 2:
                    pe.wait_ge(sem["roped"], t - 1)
                src = qaT[:, t, :] if t < 4 else kaT[:, 0:S]
                pe.matmul(ps[:, 6 + t % 2, 0:S], mat("perm"), src, start=True, stop=True).then_inc(sem["swap_done"], 1)
            for c in range(6):
                pe.wait_ge(sem["l2_squares"], c + 1)
                pe.matmul(ps[:, c, :], ones, l2q[:, c % 2, :], start=True, stop=True).then_inc(sem["l2_sums"], 1)

            def scores(g):
                qt, kv = g // 2, g % 2
                for t in range(4):
                    if g == 0 and t == 0:
                        pe.wait_ge(sem["roped"], 5)
                        pe.wait_ge(sem["l2_done"], 6)
                    if g:
                        pe.wait_ge(sem["logits_out"], 4 * (g - 1) + t + 1)
                    r = slice(64 * kv, 64 * kv + 64)
                    pe.matmul(ps[:, t, :], qaT[r, t, P * qt:P * qt + P], kaT[r, :], start=True, stop=True).then_inc(
                        sem["score_done"], 1)

            def turn_probs(u):
                pe.wait_ge(sem["exped"], u + 1)
                if u >= 2:
                    pe.wait_ge(sem["turned_out"], u - 1)
                for c in range(4):
                    mm = pe.transpose(ps[:, 4 + u % 2, P * c:P * c + P], logit[:, u % 4, P * c:P * c + P], ident)
                mm.then_inc(sem["turned"], 1)

            def weigh(u):
                g = u // 4
                pe.wait_ge(sem["turned_out"], u + 1)
                if u % 4 == 0 and g >= 2:
                    pe.wait_ge(sem["o_scaled"], g - 1)
                for c in range(4):
                    mm = pe.matmul(ps[:, 6 + g % 2, 64 * (u % 4):64 * (u % 4) + 64], turn[:, u % 2, c, :],
                                   vtm[:, c, 64 * (g % 2):64 * (g % 2) + 64], start=(c == 0), stop=(c == 3))
                mm.then_inc(sem["weighted"], 1)

            scores(0)
            for g in range(4):
                if g < 3:
                    scores(g + 1)
                for t in range(4):
                    turn_probs(4 * g + t)
                    if t:
                        weigh(4 * g + t - 1)
                weigh(4 * g + 3)
            pe.wait_ge(sem["o_scaled"], 4)
            for qt in range(2):
                for f in range(4):
                    mm = pe.transpose(ps[:, qt, P * f:P * f + P], otm[:, qt, P * f:P * f + P], ident)
                mm.then_inc(sem["o_turned"], 1)
            phase_end(pe, 2)

            for n in range(8):
                if n >= 2:
                    pe.wait_ge(sem["tok_ready"], n - 1)
                src = kdT if n < 4 else vdT
                for h in range(4):
                    mm = pe.transpose(ps[:, 4 + n % 2, P * h:P * h + P], src[:, h, P * (n % 4):P * (n % 4) + P], ident)
                mm.then_inc(sem["tok_turned"], 1)
            pe.wait_ge(sem["decay_in"], 1)
            for d in range(2):
                pe.matmul(ps[:, 0, 16 * d:16 * d + 16], tri[:, d, :], dec["g"][:, :, 4 * d:4 * d + 4], start=True, stop=True)
            pe.matmul(ps[:, 0, 32:64], ones, dec["g"], start=True, stop=True).then_inc(sem["decay_sums"], 1)
            pe.wait_ge(sem["decay_ready"], 1)

            for n, tt in enumerate(chunks):
                c = slice(P * tt, P * tt + P)
                if n:
                    pe.wait_ge(sem["inv_ready"], 2 * n)
                for h in range(4):
                    mm = pe.matmul(ps[:, 0, P * h:P * h + P], kdT[:, h, c], kdT[:, h, c], start=True, stop=True)
                if tt < 2:
                    for h in range(4):
                        mm = pe.matmul(ps[:, 1, P * h:P * h + P], kdT[:, h, c], qdT[:, h, c], start=True, stop=True)
                mm.then_inc(sem["k_products"], 1)
                for d in range(2):
                    pe.wait_ge(sem["gb_ready"], 2 * n + d + 1)
                    for h in range(4):
                        mm = pe.matmul(ps[:, 2 + d, P * h:P * h + P], gbr[d][:, h, :], tri[:, d, :], start=True, stop=True)
                    mm.then_inc(sem["g_rows"], 1)
                for l in range(7):
                    for d in range(2):
                        b = pair[d]
                        if l < 2:
                            pe.wait_ge(sem["mask_ready"], 4 * n + 2 * l + d + 1)
                        else:
                            pe.wait_ge(sem["late_mask"], 10 * n + 2 * (l - 2) + d + 1)
                            pe.wait_ge(sem["z_ready"], 10 * n + 2 * (l - 2) + d + 1)
                        if l == 0:
                            if n:
                                pe.wait_ge(sem["wu_ready"], 2 * (n - 1) + d + 1)
                            for h in range(4):
                                mm = pe.matmul(ps[:, 4 + d, P * h:P * h + P], b["M"][:, h, :], ident, start=True, stop=True)
                            mm.then_inc(sem["y_done"], 1)
                            continue
                        for h in range(4):
                            mm = pe.matmul(ps[:, 4 + d, P * h:P * h + P], b["M"][:, h, :], b["Z"][:, h, :], start=True, stop=True)
                        mm.then_inc(sem["y_done"], 1)
                    for d in range(2):
                        if l == 0:
                            continue
                        b = pair[d]
                        pe.wait_ge(sem["y_out"], 12 * n + 2 * (l - 1) + d + 1)
                        if l >= 2:
                            pe.wait_ge(sem["t_ready"], 10 * n + 2 * (l - 2) + d + 1)
                        for h in range(4):
                            mm = pe.matmul(ps[:, d, P * h:P * h + P], b["T"][:, h, :], b["Y"][:, h, :], start=True, stop=True)
                        if l < 6:
                            for h in range(4):
                                mm = pe.matmul(ps[:, 2 + d, P * h:P * h + P], b["Y"][:, h, :], b["T"][:, h, :], start=True, stop=True)
                        mm.then_inc(sem["p_done"], 1)
                for d in range(2):
                    b = pair[d]
                    pe.wait_ge(sem["inv_ready"], 2 * n + d + 1)
                    for h in range(4):
                        pe.matmul(ps[:, 4 + d, P * h:P * h + P], b["M"][:, h, :], b["Z"][:, h, :], start=True, stop=True)
                    for h in range(4):
                        mm = pe.matmul(ps[:, 6 + d, P * h:P * h + P], b["Z"][:, h, :], b["T"][:, h, :], start=True, stop=True)
                    mm.then_inc(sem["wu_done"], 1)

            pe.wait_ge(sem["wu_ready"], 8)
            for st in range(4):
                for d in range(2):
                    tt = scan[d][st]
                    g = 4 * d + tt
                    pe.wait_ge(sem["state_ready"], 2 * st + d + 1)
                    for h in range(4):
                        mm = pe.matmul(ps[:, 4 * d, P * h:P * h + P], wt[:, g, h, :], state[d][:, h, :], start=True, stop=True)
                    mm.then_inc(sem["scan_ws"], 1)
                    if tt < 2:
                        for h in range(4):
                            pe.matmul(ps[:, 4 * d + 1, P * h:P * h + P], qdT[:, h, P * tt:P * tt + P], state[d][:, h, :],
                                      start=True, stop=True)
                for d in range(2):
                    tt = scan[d][st]
                    pe.wait_ge(sem["v_new"], 2 * st + d + 1)
                    if st < 3:
                        for h in range(4):
                            mm = pe.matmul(ps[:, 4 * d + 3, P * h:P * h + P], pair[d]["R"][:, h, :], vnew[d][:, h, :],
                                           start=True, stop=True)
                        mm.then_inc(sem["scan_s"], 1)
                    if tt < 2:
                        for h in range(4):
                            mm = pe.matmul(ps[:, 4 * d + 2, P * h:P * h + P], at[:, 2 * d + tt, h, :], vnew[d][:, h, :],
                                           start=True, stop=True)
                        mm.then_inc(sem["scan_o"], 1)
            pe.wait_ge(sem["head_normed"], 1)
            for tt in range(2):
                for h in range(4):
                    mm = pe.transpose(ps[:, tt, P * h:P * h + P], osum[:, tt, h, :], ident)
                mm.then_inc(sem["head_turned"], 1)
            phase_end(pe, 3)

            for d in range(KT):
                tile_ready(N_BR + d)
                w = tile_at(N_BR + d)
                if d >= 4:
                    pe.wait_ge(sem["merged"], d - 3)
                for k in range(4):
                    pe.matmul(ps[:, d % 4, 0:S], w[:, P * k:P * k + P], oaT[:, k, :], start=(k == 0), stop=(k == 3))
                for k in range(4):
                    mm = pe.matmul(ps[:, d % 4, S:2 * S], w[:, 512 + P * k:512 + P * k + P], odT[:, k, :],
                                   start=(k == 0), stop=(k == 3))
                mm.then_inc(sem["tiles_done"], 1)

            def full(n, src, b, free=None):
                tile_ready(n)
                if free:
                    pe.wait_ge(*free)
                w = tile_at(n)
                for k in range(KT):
                    mm = pe.matmul(ps[:, b, 0:S], w[:, P * k:P * k + P], src[:, k, :], start=(k == 0), stop=(k == KT - 1))
                mm.then_inc(sem["tiles_done"], 1)

            pe.wait_ge(sem["merged"], KT)
            for d in range(KT):
                full(N_OUT + d, yT, 4 + d % 4, (sem["resid"], d - 3) if d >= 4 else None)

            def sum_squares2(r, src, b=3):
                for k in range(KT):
                    pe.wait_ge(sem["squares"], KT * r + k + 1)
                    mm = pe.matmul(ps[:, b, 0:S], ones, src[:, k, :], start=(k == 0), stop=(k == KT - 1))
                mm.then_inc(sem["sums"], 1)

            sum_squares2(1, sq2)
            pe.wait_ge(sem["normed"], 2)
            for h in range(KT):
                full(N_WQ + h, h2T, 4 + h % 4, (sem["route_q"], h - 3) if h >= 4 else None)
            for h in range(8):
                pe.wait_ge(sem["route_q"], h + 1)
                if h % 4 == 0:
                    tile_ready(N_KEYS + h // 4)
                for tt in range(2):
                    j = 2 * h + tt
                    if j >= 4:
                        pe.wait_ge(sem["scores_out"], j - 3)
                    pe.matmul(ps[:, j % 4, 0:S], qpT[:, h, P * tt:P * tt + P],
                              tile_at(N_KEYS + h // 4)[:, S * (h % 4):S * (h % 4) + S], start=True, stop=True).then_inc(
                                  sem["route_scores"], 1)
                if h % 4 == 3:
                    pe.drain().then_inc(sem["tiles_done"], 1)
            for tt in range(2):
                pe.wait_ge(sem["ranked"], tt + 1)
                for c in range(3):
                    mm = pe.transpose(ps[:, 4 + tt, P * c:P * c + P], rank[:, tt, c, :, :].rearrange("p a b -> p (a b)"), ident)
                mm.then_inc(sem["ranks_turned"], 1)
            phase_end(pe, 4)

            with pe.Fori(0, S // 8) as i:
                for t in range(8):
                    pe.wait_ge(sem["hot1_ready"], 8 * i + t + 1)
                    if t < 4:
                        pe.wait_ge(sem["hot2_ready"], 4 * i + t + 1)
                    else:
                        pe.wait_ge(sem["hot2_late"], i + 1)
                    if t % 4 == 0:
                        pe.wait_ge(sem["w_out"], 2 * i + t // 4 + 1)
                    pe.matmul(ps[:, 6 + t // 4, P * (t % 4):P * (t % 4) + P], hot1[:, t, :], hot2[:, t, :],
                              start=True, stop=True).then_inc(sem["w_psum"], 1)

            pe.wait_ge(sem["w_out"], 2 + S // 4)

            def experts_up(h, ready, b):
                for half in range(2):
                    pe.wait_ge(sem["w_lo"], ready + half)
                    for k in range(4):
                        for c, e in PASSES:
                            mm = pe.matmul(ps[:, 4 + b, 0:S], w_parts[:, c, (h + half) % 4, P * k:P * k + P],
                                           h_parts[:, e, 4 * half + k, :], start=(half == 0 and k == 0 and c + e == 0),
                                           stop=(half == 1 and k == 3 and c == 1))
                    mm.then_inc(sem["tiles_done" if half else "half_used"], 1)

            def experts_down(h, ready, b, gated, first=False, last=False):
                pe.wait_ge(sem["g_lo"], gated)
                for half in range(2):
                    pe.wait_ge(sem["w_lo"], ready + half)
                    for k in range(4):
                        d = 4 * half + k
                        for c, e in PASSES:
                            mm = pe.matmul(ps[:, d // 2, S * (d % 2):S * (d % 2) + S], w_parts[:, c, (h + half) % 4, P * k:P * k + P],
                                           g_parts[:, e, b, :], start=(first and d % 2 == 0 and c + e == 0), stop=(last and c == 1),
                                           skip_group_check=True)
                    mm.then_inc(sem["tiles_done" if half else "half_used"], 1)

            pe.wait_ge(sem["h_lo"], 4)
            experts_up(0, 1, 0)
            for j in range(1, 3):
                experts_up(4 * j - 2, 4 * j - 1, j % 2)
                experts_down(4 * j, 4 * j + 1, (j - 1) % 2, j, first=(j == 1))
            with pe.Fori(1, P // 2 - 1) as i:
                for jj in (1, 2):
                    experts_up(4 * jj - 2, 8 * i + 4 * jj - 1, jj % 2)
                    experts_down(4 * jj, 8 * i + 4 * jj + 1, (jj - 1) % 2, 2 * i + jj)
            experts_up(4 * 127 - 2, 4 * 127 - 1, 1)
            experts_down(4 * 127, 4 * 127 + 1, 0, 127)
            experts_down(510, 511, 1, 128, last=True)
            sum_squares2(2, sq3, 5)
            phase_end(pe, 5)

            sum_squares2(3, sq3, 3)
            def full_parts(m, src, out, free=None):
                if free:
                    pe.wait_ge(*free)
                for half in range(2):
                    pe.wait_ge(sem["w_lo"], 2 * m + half + 1)
                    for k in range(4):
                        for c, e in PASSES:
                            mm = pe.matmul(out, w_parts[:, c, (2 * m + half) % 4, P * k:P * k + P], src[:, e, 4 * half + k, :],
                                           start=(half == 0 and k == 0 and c + e == 0), stop=(half == 1 and k == 3 and c == 1))
                    mm.then_inc(sem["tiles_done" if half else "half_used"], 1)

            pe.wait_ge(sem["h_lo"], 8)
            for t in range(64):
                m = M_IN2 + t
                free = (sem["proj_free"], 39 + t + 1)
                if t // 4 in (6, 9):
                    pe.wait_ge(*free)
                    pe.wait_ge(sem["w_lo"], 2 * m + 2)
                    for tt in range(2):
                        for k in range(KT):
                            for c, e in PASSES:
                                mm = pe.matmul(ps[:, 4 + t % 4, P * tt:P * tt + P], h_parts[:, c, k, P * tt:P * tt + P],
                                               w_parts[:, e, (2 * m + k // 4) % 4, P * (k % 4):P * (k % 4) + P],
                                               start=(k == 0 and c + e == 0), stop=(k == KT - 1 and c == 1))
                            if tt == 1 and k % 4 == 3:
                                mm.then_inc(sem["tiles_done" if k == 7 else "half_used"], 1)
                else:
                    full_parts(m, h_parts, ps[:, 4 + t % 4, 0:S], free)
                if 40 <= t < 48:
                    j = t - 40
                    if j == 0:
                        pe.wait_ge(sem["rgw_in"], 32)
                        pe.wait_ge(sem["rg_conv_done"], KT)
                    if j >= 4:
                        pe.wait_ge(sem["rg_sig"], j - 3)
                    for g in range(2):
                        mm = pe.matmul(ps[:, j % 4, S * g:S * g + S], rgw[:, g, P * j:P * j + P], xr[:, j, :], start=True, stop=True)
                    mm.then_inc(sem["rg_gates"], 1)

            def scores2(g):
                qt = g // 2 % 2
                for t in range(4):
                    u = 4 * (g % 2) + t
                    r = slice(64 * (u % 2), 64 * (u % 2) + 64)
                    if g:
                        pe.wait_ge(sem["logits2"], 4 * (g - 1) + t + 1)
                    else:
                        pe.wait_ge(sem["rg_sig"], KT)
                    pe.matmul(ps[:, t, 0:S], q2[g // 4][r, u // 2, P * qt:P * qt + P], k2[g // 4][r, u // 2, :],
                              start=True, stop=True).then_inc(sem["score_done"], 1)

            def turn2(v, g, t):
                pe.wait_ge(sem["probs2"], v + 1)
                if v >= 2:
                    pe.wait_ge(sem["turned_out"], 16 + v - 1)
                for c in range(2):
                    mm = pe.transpose(ps[:, 4 + v % 2, P * c:P * c + P], lg[:, g % 2, t, P * c:P * c + P], ident)
                mm.then_inc(sem["turned"], 1)

            def weigh2(v, g, t):
                pe.wait_ge(sem["turned_out"], 16 + v + 1)
                if g >= 2 and t == 0:
                    pe.wait_ge(sem["o_scaled"], 4 + g - 1)
                m = 64 if g < 4 else P
                at0 = (256 * (g % 2) + 64 * t) if g < 4 else (256 * (g % 2) + P * (t // 2))
                o = 64 * t if g < 4 else P * (t // 2)
                for c in range(2):
                    mm = pe.matmul(ps[:, 6 + g % 2, o:o + m], tn2[:, v % 2, c, :], v2[g // 4][:, c, at0:at0 + m],
                                   start=(c == 0), stop=(c == 1))
                mm.then_inc(sem["weighted"], 1)

            scores2(0)
            v = 0
            for g in range(8):
                if g < 7:
                    scores2(g + 1)
                ts = (0, 1, 2, 3) if g < 4 else (0, 2)
                for n, t in enumerate(ts):
                    turn2(v + n, g, t)
                    if n:
                        weigh2(v + n - 1, g, ts[n - 1])
                weigh2(v + len(ts) - 1, g, ts[-1])
                v += len(ts)
            pe.wait_ge(sem["o2_ready"], 1)
            for m in range(2):
                for qt in range(2):
                    for f in range(4):
                        mm = pe.transpose(ps[:, 2 * m + qt, P * f:P * f + P], o2[m][:, qt, P * f:P * f + P], ident)
                    mm.then_inc(sem["o_turned"], 1)
            phase_end(pe, 6)

            for d in range(KT):
                n = N_BR2 + 2 * d
                b = 2 * (d % 2)
                tile_ready(n)
                if d >= 2:
                    pe.wait_ge(sem["merged"], KT + d - 1)
                for m in range(2):
                    for k in range(4):
                        mm = pe.matmul(ps[:, b, S * m:S * m + S], tile_at(n)[:, 512 * m + P * k:512 * m + P * k + P], o2T[m][:, k, :],
                                       start=(k == 0), stop=(k == 3))
                mm.then_inc(sem["tiles_done"], 1)
                full(n + 1, rgl, b + 1)
            pe.wait_ge(sem["merged"], 2 * KT)
            for d in range(KT):
                full(N_OUT2 + d, y2T, 4 + d % 4, (sem["resid"], 2 * KT + d - 3) if d >= 4 else None)
            sum_squares2(4, sq3, 3)
            pe.wait_ge(sem["h_lo"], 12)

            def ffn_tile(x, i4, moving, out, start, stop, **more):
                for half in range(2):
                    pe.wait_ge(sem["w_lo"], 6 * i4 + 2 * (M_FFN + x) + half + 1)
                    for k in range(4):
                        d = 4 * half + k
                        for c, e in PASSES:
                            mm = pe.matmul(out(d), w_parts[:, c, (2 * (M_FFN + x) + half) % 4, P * k:P * k + P], moving(e, d),
                                           start=start(d) and c + e == 0, stop=stop(d) and c == 1, **more)
                    mm.then_inc(sem["tiles_done" if half else "half_used"], 1)

            def ffn_up(f, i4=0):
                for m in range(2):
                    if m == 0:
                        pe.wait_ge(sem["ff_out"], i4 + f + 1)
                    ffn_tile(max(3 * f - 1, 0) + m, i4, lambda e, d: h_parts[:, e, d, :], lambda d: ps[:, 4 + f % 2, S * m:S * m + S],
                             lambda d: d == 0, lambda d: d == KT - 1)

            def ffn_down(f, i4=0, x=None, first=False, last=False):
                pe.wait_ge(sem["g_lo"], i4 + P + f + 1)
                ffn_tile(x or 3 * f + 4, i4, lambda e, d: g_parts[:, e, f % 2, :],
                         lambda d: ps[:, d // 2, S * (d % 2):S * (d % 2) + S], lambda d: first and d % 2 == 0, lambda d: last,
                         skip_group_check=True)

            ffn_up(0)
            ffn_up(1)
            ffn_down(0, first=True)
            with pe.Fori(0, (FT - 2) // 4) as i:
                for f in range(2, 6):
                    ffn_up(f, 4 * i)
                    ffn_down(f - 1, 4 * i)
            ffn_down(FT - 1, x=3 * FT - 1, last=True)
            sum_squares2(5, sq3, 6)

        @block.scalar
        def _(act):
            def link(ins):
                link.n += 1
                ins.then_inc(sem["act_chain"], 1)
                act.wait_ge(sem["act_chain"], link.n)
            link.n = 0

            act.sem_inc(sem["mod_bank_free"], 2)
            act.sem_inc(sem["proj_free"], 4)
            act.wait_ge(sem["params_in"], 32)
            act.activation(csT, col("c2", KT, 2), ACT.Silu).then_inc(sem["silu_c"], 1)
            with act.Fori(0, 12) as i:
                act.wait_ge(sem["tiles_done"], 4 * i + 4)
                act.activation(modrow[0:2, bass.ds(i * 512, 512)], ps[0:2, bass.ds(i % 2, 1), :].rearrange("p a b -> p (a b)"), ACT.Copy).then_inc(
                    sem["mod_bank_free"], 1)

            def roots(r, n, b=3):
                act.wait_ge(sem["sums"], r + 1)
                act.activation(root[:, 0:n], ps[:, b, 0:n], ACT.Sqrt, bias=eps, scale=1.0 / D).then_inc(sem["roots"], 1)

            act.wait_ge(sem["x_in"], 48)
            for k in range(KT):
                act.activation(sq[:, k, :].rearrange("p (c t) -> p c t", c=2), xc[:, :, k, :], ACT.Square).then_inc(sem["squares"], 1)
            roots(0, 512)
            def conv_silu(j):
                two = 1 if j < 4 else 2
                act.wait_ge(sem["conv_done"], j + 2)
                src = cvo[:, j % 2, 0:two, :]
                if j < 4:
                    dst = qdT[:, j, :].unsqueeze(1)
                else:
                    dst = (kdT if j < 8 else vdT)[:, j % 4, :].rearrange("p (a b) -> p a b", a=2)
                act.activation(dst, src, ACT.Silu).then_inc(sem["conv_used"], 1)

            nconv = 0
            order = list(range(39))
            for t in order:
                b = 4 + t % 4
                act.wait_ge(sem["tiles_done"], N_WIN + t + 1)
                if t < 4:
                    o = act.activation(qaT[:, t, :], ps[:, b, 0:S], ACT.Copy, scale=0.125)
                elif t == 4:
                    o = act.activation(kaT, ps[:, b, :], ACT.Copy)
                elif t == 5:
                    o = act.activation(vtm.rearrange("p a b -> p (a b)"), ps[:, b, :], ACT.Copy)
                elif t < 18:
                    j = t - 6
                    two = 1 if j < 4 else 2
                    act.wait_ge(sem["conv_done"], j)
                    o = act.activation(pad[:, j % 2, 0:two, 2:2 + S], bank(b, 2, S)[:, 0:two, :], ACT.Copy)
                elif t < 22:
                    o = act.activation(szT[:, t - 18, :], ps[:, b, 0:S], ACT.Silu)
                elif t == 22:
                    o = act.activation(ab.rearrange("p a b -> p (a b)"), ps[:, b, 0:64], ACT.Copy)
                else:
                    o = act.activation(gatesT[:, t - 23, :], ps[:, b, 0:S], ACT.Sigmoid,
                                       bias=col("b_gate")[:, t - 23:t - 22])
                o.then_inc(sem["proj_free"], 1)
                if 7 <= t < 19:
                    conv_silu(t - 7)
            phase_end(act, 1)

            for c in range(8):
                if c < 6:
                    if c >= 2:
                        act.wait_ge(sem["l2_sums"], c - 1)
                    src = qd_flat[:, 512 * c:512 * c + 512] if c < 2 else kd_flat[:, 512 * (c - 2):512 * (c - 2) + 512]
                    act.activation(l2q[:, c % 2, :], src, ACT.Square).then_inc(sem["l2_squares"], 1)
                if c >= 2:
                    act.wait_ge(sem["l2_sums"], c - 1)
                    if c >= 4:
                        act.wait_ge(sem["l2_done"], c - 3)
                    act.activation(l2r[:, c % 2, :], ps[:, c - 2, :], ACT.Sqrt, bias=eps).then_inc(sem["l2_roots"], 1)

            for g in range(4):
                st = stat[g % 2]
                act.wait_ge(sem["max_ready"], g + 1)
                for t in range(4):
                    act.activation(logit[:, t, :], logit[:, t, :], ACT.Exp, bias=st["nm"][:, t:t + 1],
                                   accum_out=st["rs"][:, t:t + 1]).then_inc(sem["exped"], 1)
                act.activation(st["es"], st["sk"], ACT.Exp).then_inc(sem["sums_done"], 1)
                for u in range(4 * g, 4 * g + 4):
                    act.wait_ge(sem["turned"], u + 1)
                    if u >= 2:
                        act.wait_ge(sem["weighted"], u - 1)
                    act.activation(turn[:, u % 2, :, :].rearrange("p a b -> p (a b)"), ps[:, 4 + u % 2, :], ACT.Copy).then_inc(
                        sem["turned_out"], 1)
            for qt in range(2):
                act.wait_ge(sem["o_turned"], qt + 1)
                act.activation(oaT[:, :, P * qt:P * qt + P], bank(qt, 4, P), ACT.Copy).then_inc(sem["o_moved"], 1)
            phase_end(act, 2)

            act.activation(dec["beta"], ab[:, :, 8:16], ACT.Sigmoid).then_inc(sem["act_chain"], 1)
            act.activation(small[:, 64:72], col("a_log"), ACT.Exp).then_inc(sem["act_chain"], 1)
            act.wait_ge(sem["ab_ready"], 1)
            act.activation(dec["t2"], dec["t2"], ACT.Exp, scale=-1.0).then_inc(sem["act_chain"], 1)
            act.wait_ge(sem["act_chain"], 3)
            act.activation(dec["t2"], dec["t2"], ACT.Ln, bias=1.0).then_inc(sem["act_chain"], 1)
            for n in range(8):
                act.wait_ge(sem["tok_turned"], n + 1)
                dst = (ktok if n < 4 else vtok)[:, n % 4, :, :].rearrange("p a b -> p (a b)")
                act.activation(dst, ps[:, 4 + n % 2, :], ACT.Copy).then_inc(sem["tok_ready"], 1)
            act.wait_ge(sem["decay_sums"], 1)
            for d in range(2):
                act.activation(dec["G"][:, :, 4 * d:4 * d + 4], ps[:, 0, 16 * d:16 * d + 16].rearrange("p (a b) -> p a b", a=4), ACT.Copy)
            act.activation(dec["eT"], ps[:, 0, 32:64].rearrange("p (a b) -> p a b", a=4), ACT.Copy).then_inc(sem["decay_ready"], 1)
            act.wait_ge(sem["decay_ready"], 1)
            act.activation(dec["eG"], dec["G"], ACT.Exp).then_inc(sem["act_chain"], 1)
            act.wait_ge(sem["tail_gap"], 1)
            act.activation(dec["tail"], dec["tail"], ACT.Exp)
            act.activation(dec["eT"], dec["eT"], ACT.Exp).then_inc(sem["act_chain"], 1)

            for n, tt in enumerate(chunks):
                for d in range(2):
                    b = pair[d]
                    act.wait_ge(sem["gaps"], 2 * n + d + 1)
                    act.activation(b["Y"], b["Y"], ACT.Exp, scale=-1.0)
                    act.activation(b["R"], b["R"], ACT.Exp).then_inc(sem["decays"], 1)
                for l in range(1, 7):
                    for d in range(2):
                        act.wait_ge(sem["y_done"], 14 * n + 2 * l + d + 1)
                        act.activation(pair[d]["Y"].rearrange("p a b -> p (a b)"), ps[:, 4 + d, :], ACT.Copy).then_inc(sem["y_out"], 1)
                for d in range(2):
                    act.wait_ge(sem["wu_done"], 2 * n + d + 1)
                    act.activation(wt[:, 4 * d + tt, :, :], bank(4 + d, 4, P), ACT.Copy)
                    act.activation(uu[:, 4 * d + tt, :, :], bank(6 + d, 4, P), ACT.Copy).then_inc(sem["wu_ready"], 1)
            act.wait_ge(sem["head_stat"], 1)
            act.activation(small[:, 72:80], small[:, 72:80], ACT.Sqrt, bias=eps, scale=1.0 / P).then_inc(sem["head_root"], 1)
            phase_end(act, 3)

            for k in range(KT):
                act.wait_ge(sem["resid"], k + 1)
                act.activation(sq2[:, k, :], res[:, k, :], ACT.Square).then_inc(sem["squares"], 1)
            roots(1, S)
            for h in range(KT):
                act.wait_ge(sem["tiles_done"], N_WQ + h + 1)
                act.activation(qpT[:, h, :], ps[:, 4 + h % 4, 0:S], ACT.Copy).then_inc(sem["route_q"], 1)
            for j in range(16):
                act.wait_ge(sem["route_scores"], j + 1)
                act.activation(sc[:, j % 2, 2 * (j // 2):2 * (j // 2) + 2, :], bank(j % 4, 2, P), ACT.Copy).then_inc(
                    sem["scores_out"], 1)
            for c in range(4):
                act.activation(h_parts[:, 0, 2 * c:2 * c + 2, :], h2T[:, 2 * c:2 * c + 2, :], ACT.Copy).then_inc(sem["h_hi"], 1)

            def tile_hi(slot, count, half, h):
                act.wait_ge(loaded[slot], count)
                act.activation(w_parts[:, 0, h % 4, :], ring[:, slot, 512 * half:512 * half + 512], ACT.Copy).then_inc(
                    sem["w_hi"], 1)

            peer_slot = lambda m: (N_PEER + m) % RING
            peer_count = lambda m: 16 * ((N_PEER + m) // RING + 1)
            for h in range(4):
                tile_hi(peer_slot(h // 2), peer_count(h // 2), h % 2, h)
            for tt in range(2):
                act.wait_ge(sem["gate_in"], tt + 1)
                act.activation(b16, b16, ACT.Exp).then_inc(sem["gate_exp"], 1)
            for tt in range(2):
                act.wait_ge(sem["ranks_turned"], tt + 1)
                act.activation(rT[:, :, P * tt:P * tt + P], bank(4 + tt, 3, P), ACT.Copy).then_inc(sem["ranks_out"], 1)
            act.sem_inc(sem["w_out"], 2)
            phase_end(act, 4)

            Wflat = W.rearrange("p a b -> p (a b)")
            with act.Fori(0, S // 8) as i:
                for half in range(2):
                    act.wait_ge(sem["w_psum"], 8 * i + 4 * half + 12)
                    act.activation(Wflat[:, bass.ds(i * 1024 + 512 * half, 512)], ps[:, 6 + half, :], ACT.Copy).then_inc(
                        sem["w_out"], 1)

            def expert_gelu(done, b):
                act.wait_ge(sem["tiles_done"], done)
                act.activation(gelu[:, b, :], ps[:, 4 + b, 0:S], ACT.Gelu_apprx_tanh).then_inc(sem["gelu_done"], 1)

            def gated_hi(ready, b):
                act.wait_ge(sem["gated"], ready)
                act.activation(g_parts[:, 0, b, :], gated[:, b, :], ACT.Copy).then_inc(sem["g_hi"], 1)

            def tile_hi_at(j, ahead, i2=0):
                h = 4 * j + ahead
                m = h // 2
                tile_hi(peer_slot(m), 8 * i2 + peer_count(m), h % 2, h)

            def step(j, i2=0, last=False):
                act.wait_ge(sem["tiles_done"], N_PEER + 2 * i2 + 2 * j - 1)
                tile_hi_at(j, 1, i2)
                act.wait_ge(sem["half_used"], 2 * i2 + 2 * j)
                tile_hi_at(j, 2, i2)
                expert_gelu(N_PEER + 2 * i2 + 2 * j, j % 2)
                tile_hi_at(j, 3, i2)
                gated_hi(i2 + j + 1, j % 2)
                if not last:
                    act.wait_ge(sem["half_used"], 2 * i2 + 2 * j + 1)
                    tile_hi_at(j, 4, i2)

            act.wait_ge(sem["half_used"], 1)
            tile_hi_at(0, 4)
            expert_gelu(N_PEER + 1, 0)
            gated_hi(1, 0)
            for j in (1, 2):
                step(j)
            with act.Fori(1, P // 2 - 1) as i:
                for jj in (1, 2):
                    step(jj, 2 * i)
            step(127, last=True)
            for k in range(KT):
                act.wait_ge(sem["resid"], KT + k + 1)
                act.activation(sq3[:, k, :], res[:, k, :], ACT.Square).then_inc(sem["squares"], 1)
            roots(2, S, 5)
            phase_end(act, 5)

            for k in range(KT):
                act.activation(sq3[:, k, :], x2T[:, k, :], ACT.Square).then_inc(sem["squares"], 1)

            def part_hi(m, half, i4=0):
                n = tile_of(m)
                tile_hi(n % RING, 12 * i4 + 16 * (n // RING + 1), half, 2 * m + half)

            def act_hi(src):
                for c in range(4):
                    act.activation(h_parts[:, 0, 2 * c:2 * c + 2, :], src[:, 2 * c:2 * c + 2, :], ACT.Copy).then_inc(sem["h_hi"], 1)

            for h in range(4):
                part_hi(M_IN2 + h // 2, h % 2)
            roots(3, S, 3)
            act.wait_ge(sem["normed"], 4)
            act_hi(h3T)
            for t in range(64):
                act.wait_ge(sem["half_used"], M_IN2 + t + 1)
                if t < 62:
                    part_hi(M_IN2 + t + 2, 0)
                act.wait_ge(sem["tiles_done"], N_IN2 + t + 1)
                src = ps[:, 4 + t % 4, 0:S]
                kind, f = t // 4, t % 4
                if kind < 2:
                    o = act.activation(rxp[:, t, 3:3 + S], src, ACT.Copy)
                elif kind < 4:
                    o = act.activation(rgl[:, t - 8, :], src, ACT.Gelu_apprx_tanh)
                elif kind in (4, 7):
                    o = act.activation(q2[kind // 7][:, f, :], src, ACT.Copy, scale=0.125)
                elif kind in (5, 8):
                    o = act.activation(k2[kind // 8][:, f, :], src, ACT.Copy)
                elif kind in (6, 9):
                    o = act.activation(v2[kind // 9][:, :, P * f:P * f + P], bank(4 + f, 2, P), ACT.Copy)
                else:
                    o = act.activation(g2T[:, t - 40, :], src, ACT.Sigmoid, bias=col("b_gate2")[:, t - 40:t - 39])
                o.then_inc(sem["proj_free"], 1)
                if t < 62:
                    part_hi(M_IN2 + t + 2, 1)
                if t == 16:
                    act.wait_ge(sem["rg_in"], 1)
                    act.activation(vec[:, 8:16], vec[:, 8:16], ACT.Exp, scale=-1.0).then_inc(sem["act_chain"], 1)
                    act.activation(vec[:, 32:34], vec[:, 32:34], ACT.Exp).then_inc(sem["lam_exp"], 1)
                    act.wait_ge(sem["act_chain"], 7)
                    act.activation(vec[:, 8:16], vec[:, 8:16], ACT.Ln, bias=1.0).then_inc(sem["rg_ln"], 1)
                if 41 <= t < 49:
                    j = t - 41
                    act.wait_ge(sem["rg_gates"], j + 1)
                    act.activation(rr[:, j, :], ps[:, j % 4, 0:S], ACT.Sigmoid, bias=col("rg_ba")[:, j:j + 1])
                    act.activation(ii[:, j, :], ps[:, j % 4, S:2 * S], ACT.Sigmoid, bias=col("rg_bx")[:, j:j + 1]).then_inc(
                        sem["rg_sig"], 1)
                if t == 50:
                    act.wait_ge(sem["rg_coeff"], 1)
                    act.wait_ge(sem["rg_sig"], KT)
                    for j in range(KT):
                        act.activation(dca[:, j, :], rr[:, j, :], ACT.Exp, scale=vec[:, 16 + j:17 + j])
                if t == 52:
                    for j in range(KT):
                        act.activation(thn[:, j, :], rr[:, j, :], ACT.Tanh, scale=vec[:, 24 + j:25 + j]).then_inc(sem["rg_pow"], 1)
                if t == 57:
                    act.wait_ge(sem["rg_square"], 1)
                    act.activation(thn, thn, ACT.Sqrt).then_inc(sem["rg_mult"], 1)
            v = 0
            for g in range(8):
                st = stat[g % 2]
                act.wait_ge(sem["max_ready"], 4 + g + 1)
                for t in range(4):
                    act.activation(lg[:, g % 2, t, :], lg[:, g % 2, t, :], ACT.Exp, bias=st["nm"][:, t:t + 1],
                                   accum_out=st["rs"][:, t:t + 1]).then_inc(sem["probs2" if g < 4 else "maps2"], 1)
                for t in range(4 if g < 4 else 2):
                    act.wait_ge(sem["turned"], 16 + v + 1)
                    if v >= 2:
                        act.wait_ge(sem["weighted"], 16 + v - 1)
                    act.activation(tn2[:, v % 2, :, :], bank(4 + v % 2, 2, P), ACT.Copy).then_inc(sem["turned_out"], 1)
                    v += 1
            act.wait_ge(sem["o2_stat"], 1)
            act.activation(vec[:, 40:48], vec[:, 40:48], ACT.Sqrt, bias=eps, scale=1.0 / P).then_inc(sem["o2_root"], 1)
            for m in range(2):
                for qt in range(2):
                    act.wait_ge(sem["o_turned"], 2 + 2 * m + qt + 1)
                    dst = o2T[m][:, :, P * qt:P * qt + P]
                    if m == 0:
                        o = act.activation(dst, bank(qt, 4, P), ACT.Copy)
                    else:
                        o = act.activation(dst, bank(2 + qt, 4, P), ACT.Identity, scale=vec[:, 48:49])
                    o.then_inc(sem["o_moved"], 1)
            phase_end(act, 6)

            for k in range(KT):
                act.wait_ge(sem["resid"], 2 * KT + k + 1)
                act.activation(sq3[:, k, :], res[:, k, :], ACT.Square).then_inc(sem["squares"], 1)
            for h in range(4):
                part_hi(M_FFN + h // 2, h % 2)
            roots(4, S, 3)
            act.wait_ge(sem["normed"], 5)
            act_hi(h4T)

            act.sem_inc(sem["ff_out"], 2)

            def used(x, half, i4=0):
                if half:
                    act.wait_ge(sem["tiles_done"], 3 * i4 + N_FFN + x + 1)
                else:
                    act.wait_ge(sem["half_used"], 3 * i4 + M_FFN + x + 1)

            def ahead(x, half, i4=0):
                if x + 2 < 3 * FT:
                    part_hi(M_FFN + x + 2, half, i4)

            def up_out(f, i4=0):
                act.wait_ge(sem["ff_conv"], i4 + f + 1)
                act.activation(upp[:, f % 2, :, 2:2 + S], bank(4 + f % 2, 2, S), ACT.Copy).then_inc(sem["ff_out"], 1)

            def ff_gelu(f, i4=0):
                act.wait_ge(sem["ff_conv"], i4 + f + 3)
                act.activation(upc[:, f % 2, 0, :], upc[:, f % 2, 0, :], ACT.Gelu_apprx_tanh).then_inc(sem["ff_gelu"], 1)

            def act_parts(f, i4=0):
                act.wait_ge(sem["ff_act"], i4 + f + 1)
                act.activation(g_parts[:, 0, f % 2, :], fft[:, f % 2, :], ACT.Copy).then_inc(sem["g_hi"], 1)

            def ff_step(f, i4=0):
                x = 3 * f - 1
                used(x, 0, i4)
                ahead(x, 0, i4)
                act_parts(f - 1, i4)
                used(x, 1, i4)
                ahead(x, 1, i4)
                used(x + 1, 0, i4)
                ahead(x + 1, 0, i4)
                used(x + 1, 1, i4)
                up_out(f, i4)
                ahead(x + 1, 1, i4)
                used(x + 2, 0, i4)
                ahead(x + 2, 0, i4)
                used(x + 2, 1, i4)
                ahead(x + 2, 1, i4)
                ff_gelu(f, i4)

            for x in range(2):
                for half in range(2):
                    used(x, half)
                    if x + half == 2:
                        up_out(0)
                    ahead(x, half)
            ff_gelu(0)
            ff_step(1)
            with act.Fori(0, (FT - 2) // 4 - 1) as i:
                for f in range(2, 6):
                    ff_step(f, 4 * i)
            for f in range(FT - 4, FT):
                ff_step(f)
            act_parts(FT - 1)
            for k in range(KT):
                act.wait_ge(sem["resid"], 3 * KT + k + 1)
                act.activation(sq3[:, k, :], res[:, k, :], ACT.Square).then_inc(sem["squares"], 1)
            roots(5, S, 6)

        @block.vector
        def _(dve):
            def link(ins):
                link.n += 1
                ins.then_inc(sem["dve_chain"], 1)
                dve.wait_ge(sem["dve_chain"], link.n)
            link.n = 0

            link(dve.memset(pad, 0.0))
            dve.wait_ge(sem["mod_cols"], 1)
            link(dve.tensor_tensor(modT, bank(2, 48, 2), bc(col("b_ada"), 2, 2), ALU.add))
            link(dve.tensor_scalar(gain1, modT[:, 8:16, :].rearrange("p a b -> p b a"), 1.0, None, ALU.add))
            dve.tensor_tensor(gain1, gain1, bc(col("norm_mix"), 1, 2), ALU.mult)
            dve.tensor_scalar(small[:, 0:8], modT[:, 32:40, 0], 1.0, None, ALU.add)
            link(dve.memset(small[:, 8:9], 0.0))
            link(dve.tensor_tensor(gain2, small[:, 0:8], col("norm_ffn"), ALU.mult))

            def inverse(r, n):
                dve.wait_ge(sem["roots"], r + 1)
                link(dve.reciprocal(rstd[:, 0:n], root[:, 0:n]))

            inverse(0, 512)
            for half in range(2):
                c = slice(S * half, S * half + S)
                for k in range(KT):
                    dve.scalar_tensor_tensor(hT[:, k, c], xc[:, half, k, :], gain1[:, half, k:k + 1], rstd[:, c],
                                             ALU.mult, ALU.mult)
                link(dve.memset(small[:, 8:9], 0.0))
                for k in range(KT):
                    o = dve.tensor_scalar(hT[:, k, c], hT[:, k, c], modT[:, k, half:half + 1], None, ALU.add)
            o.then_inc(sem["normed"], 1)
            taps = col("conv", 12, 5)
            dve.sem_inc(sem["conv_done"], 1)
            for j in range(12):
                two = 1 if j < 4 else 2
                dve.wait_ge(sem["proj_free"], 4 + 6 + j + 1)
                if j >= 2:
                    dve.wait_ge(sem["conv_used"], j - 1)
                dst = cvo[:, j % 2, 0:two, :]
                src = lambda d: pad[:, j % 2, 0:two, d:d + S]
                link(dve.tensor_scalar(dst, src(0), taps[:, j, 0:1], None, ALU.mult))
                for d in range(1, 5):
                    o = dve.scalar_tensor_tensor(dst, src(d), taps[:, j, d:d + 1], dst, ALU.mult, ALU.add)
                    if d < 4:
                        link(o)
                o.then_inc(sem["conv_done"], 1)
            phase_end(dve, 1)

            for t in range(5):
                dve.wait_ge(sem["swap_done"], t + 1)
                v = qaT[:, t, :] if t < 4 else kaT[:, 0:S]
                dve.tensor_tensor(v, v, mat("cos"), ALU.mult)
                link(dve.tensor_tensor(swp[:, t % 2, :], ps[:, 6 + t % 2, 0:S], mat("sin"), ALU.mult))
                dve.tensor_tensor(v, v, swp[:, t % 2, :], ALU.add).then_inc(sem["roped"], 1)
            for c in range(6):
                dve.wait_ge(sem["l2_roots"], c + 1)
                link(dve.reciprocal(l2r[:, c % 2, :], l2r[:, c % 2, :]))
                v = qd_flat[:, 512 * c:512 * c + 512] if c < 2 else kd_flat[:, 512 * (c - 2):512 * (c - 2) + 512]
                dve.scalar_tensor_tensor(v, v, float(P) ** -0.5 if c < 2 else 1.0, l2r[:, c % 2, :],
                                         ALU.mult, ALU.mult).then_inc(sem["l2_done"], 1)

            def logits(g):
                st = stat[g % 2]
                for t in range(4):
                    dve.wait_ge(sem["score_done"], 4 * g + t + 1)
                    if g:
                        dve.wait_ge(sem["turned"], 4 * (g - 1) + t + 1)
                    dve.tensor_tensor_reduce(logit[:, t, :], ps[:, t, :], band[:, g // 2, :], 1.0, NEG, ALU.add, ALU.max,
                                             st["mx"][:, t:t + 1]).then_inc(sem["logits_out"], 1)

            def maxima(g):
                st = stat[g % 2]
                sink = col("sink")[:, 4 * (g % 2):4 * (g % 2) + 4]
                dve.wait_ge(sem["logits_out"], 4 * g + 4)
                link(dve.tensor_tensor(st["mx"], st["mx"], sink, ALU.max))
                dve.tensor_scalar(st["nm"], st["mx"], -1.0, None, ALU.mult)
                dve.tensor_tensor(st["sk"], sink, st["mx"], ALU.subtract).then_inc(sem["max_ready"], 1)

            def weights(g):
                st = stat[g % 2]
                dve.wait_ge(sem["sums_done"], g + 1)
                link(dve.tensor_tensor(st["ri"], st["rs"], st["es"], ALU.add))
                link(dve.reciprocal(st["ri"], st["ri"]))

            logits(0)
            for g in range(4):
                maxima(g)
                weights(g)
                if g < 3:
                    logits(g + 1)
                dve.wait_ge(sem["weighted"], 4 * g + 4)
                o = otm[:, g // 2, 256 * (g % 2):256 * (g % 2) + 256].rearrange("p (a b) -> p a b", a=4)
                dve.tensor_tensor(o, bank(6 + g % 2, 4, 64), bc(stat[g % 2]["ri"], 2, 64), ALU.mult).then_inc(sem["o_scaled"], 1)
            phase_end(dve, 2)

            a = ab[:, :, 0:8]
            link(dve.tensor_tensor(dec["t1"], a, bc(col("dt"), 1, 4), ALU.add))
            dve.scalar_tensor_tensor(dec["t2"], dec["t1"], -1.0, dec["t1"], ALU.mult, ALU.max).then_inc(sem["ab_ready"], 1)
            link(dve.tensor_scalar(dec["t1"], dec["t1"], 0.0, None, ALU.max))
            dve.wait_ge(sem["act_chain"], 4)
            link(dve.tensor_tensor(dec["t1"], dec["t1"], dec["t2"], ALU.add))
            dve.scalar_tensor_tensor(dec["g"], dec["t1"], -1.0, bc(small[:, 64:72], 1, 4), ALU.mult, ALU.mult).then_inc(
                sem["decay_in"], 1)
            dve.wait_ge(sem["decay_ready"], 1)
            dve.tensor_tensor(dec["tail"], dec["eT"], dec["G"], ALU.subtract).then_inc(sem["tail_gap"], 1)
            dve.wait_ge(sem["act_chain"], 5)
            dve.tensor_tensor(dec["kbe"], dec["beta"], dec["eG"], ALU.mult)
            dve.wait_ge(sem["decay_in"], 1)
            for d in range(2):
                o = dve.tensor_copy(gbr[d], bc(dec["g"][:, chunks[0], 4 * d:4 * d + 4], 2, P))
                o.then_inc(sem["gb_ready"], 1)
            dve.wait_ge(sem["act_chain"], 6)

            for n, tt in enumerate(chunks):
                head = lambda name, d: bc(dec[name][:, tt, 4 * d:4 * d + 4], 2, P)
                for d in range(2):
                    b = pair[d]
                    dve.wait_ge(sem["g_rows"], 2 * n + d + 1)
                    if n:
                        dve.wait_ge(sem["wu_done"], 2 * (n - 1) + d + 1)
                    link(dve.tensor_tensor(b["R"], bank(2 + d, 4, P), head("G", d), ALU.subtract))
                    dve.tensor_scalar(b["Y"], b["R"], 0.0, None, ALU.max)
                    dve.tensor_scalar(b["R"], b["R"], 0.0, None, ALU.min).then_inc(sem["gaps"], 1)
                    if n < 3:
                        dve.tensor_copy(gbr[d], bc(dec["g"][:, chunks[n + 1], 4 * d:4 * d + 4], 2, P)).then_inc(sem["gb_ready"], 1)
                dve.wait_ge(sem["k_products"], n + 1)
                for d in range(2):
                    b = pair[d]
                    dve.wait_ge(sem["decays"], 2 * n + d + 1)
                    link(dve.tensor_tensor(b["A"], b["Y"], bank(0, 4, P), ALU.mult))
                    link(dve.tensor_tensor(b["A"], b["A"], head("beta", d), ALU.mult))
                    dve.tensor_tensor(b["M"], b["A"], bc(level[:, d, 0, :], 1, 4), ALU.mult).then_inc(sem["mask_ready"], 1)
                    if tt < 2:
                        s = at[:, 2 * d + tt, :, :]
                        link(dve.tensor_tensor(s, b["R"], bank(1, 4, P), ALU.mult))
                        link(dve.tensor_tensor(s, s, bc(tri[:, d, :], 1, 4), ALU.mult))
                for d in range(2):
                    b = pair[d]
                    dve.wait_ge(sem["mask_ready"], 4 * n + d + 1)
                    dve.tensor_tensor(b["T"], bc(ident, 1, 4), b["M"], ALU.subtract)
                    dve.wait_ge(sem["y_done"], 14 * n + d + 1)
                    link(dve.tensor_tensor(b["Z"], bc(ident, 1, 4), bank(4 + d, 4, P), ALU.subtract))
                    dve.tensor_tensor(b["M"], b["A"], bc(level[:, d, 1, :], 1, 4), ALU.mult).then_inc(sem["mask_ready"], 1)
                for l in range(1, 7):
                    for d in range(2):
                        b = pair[d]
                        dve.wait_ge(sem["p_done"], 12 * n + 2 * (l - 1) + d + 1)
                        o = dve.tensor_tensor(b["Z"], b["Z"], bank(d, 4, P), ALU.subtract)
                        if l < 6:
                            o.then_inc(sem["z_ready"], 1)
                            dve.tensor_tensor(b["T"], b["T"], bank(2 + d, 4, P), ALU.subtract).then_inc(sem["t_ready"], 1)
                            continue
                        dve.wait_ge(sem["tok_ready"], 8)
                        dve.tensor_tensor(b["M"], ktok[:, tt, :, :], head("kbe", d), ALU.mult)
                        dve.tensor_tensor(b["T"], vtok[:, tt, :, :], head("beta", d), ALU.mult).then_inc(sem["inv_ready"], 1)

            for d in range(2):
                dve.memset(state[d], 0.0).then_inc(sem["state_ready"], 1)
            for d in range(2):
                dve.tensor_tensor(pair[d]["R"], ktok[:, scan[d][0], :, :], bc(dec["tail"][:, scan[d][0], 4 * d:4 * d + 4], 2, P), ALU.mult)
            for st in range(4):
                for d in range(2):
                    tt = scan[d][st]
                    dve.wait_ge(sem["scan_ws"], 2 * st + d + 1)
                    dve.wait_ge(sem["wu_ready"], 8)
                    dve.tensor_tensor(vnew[d], uu[:, 4 * d + tt, :, :], bank(4 * d, 4, P), ALU.subtract).then_inc(sem["v_new"], 1)
                for d in range(2):
                    tt = scan[d][st]
                    head = lambda name: bc(dec[name][:, tt, 4 * d:4 * d + 4], 2, P)
                    if tt < 2:
                        dve.wait_ge(sem["scan_o"], 2 * (st - 2) + d + 1)
                        t = pair[d]["A"]
                        link(dve.tensor_tensor(t, bank(4 * d + 1, 4, P), head("eG"), ALU.mult))
                        if st == 2:
                            link(dve.tensor_tensor(osum[:, tt, :, :], t, bank(4 * d + 2, 4, P), ALU.add))
                        else:
                            link(dve.tensor_tensor(t, t, bank(4 * d + 2, 4, P), ALU.add))
                            link(dve.tensor_tensor(osum[:, tt, :, :], osum[:, tt, :, :], t, ALU.add))
                    if st < 3:
                        nxt = scan[d][st + 1]
                        dve.wait_ge(sem["scan_s"], 2 * st + d + 1)
                        link(dve.tensor_tensor(state[d], state[d], head("eT"), ALU.mult))
                        dve.tensor_tensor(state[d], state[d], bank(4 * d + 3, 4, P), ALU.add).then_inc(sem["state_ready"], 1)
                        dve.tensor_tensor(pair[d]["R"], ktok[:, nxt, :, :],
                                          bc(dec["tail"][:, nxt, 4 * d:4 * d + 4], 2, P), ALU.mult)
            flat = osum.rearrange("p a b c -> p (a b) c")
            sqo = vnew[0]
            for tt in range(2):
                link(dve.tensor_tensor(sqo, osum[:, tt, :, :], osum[:, tt, :, :], ALU.mult))
                o = dve.tensor_reduce(small[:, 72 + 4 * tt:76 + 4 * tt], sqo, AX, ALU.add)
                if tt == 0:
                    link(o)
            o.then_inc(sem["head_stat"], 1)
            dve.wait_ge(sem["head_root"], 1)
            link(dve.reciprocal(small[:, 72:80], small[:, 72:80]))
            dve.tensor_tensor(flat, flat, bc(small[:, 72:80], 2, P), ALU.mult).then_inc(sem["head_normed"], 1)
            for tt in range(2):
                dve.wait_ge(sem["head_turned"], tt + 1)
                dve.scalar_tensor_tensor(odT[:, :, P * tt:P * tt + P], bank(tt, 4, P), col("dn_norm"),
                                         szT[:, :, P * tt:P * tt + P], ALU.mult, ALU.mult).then_inc(sem["dn_ready"], 1)
            phase_end(dve, 3)

            for d in range(KT):
                dve.wait_ge(sem["tiles_done"], N_BR + d + 1)
                t = root[:, S * (d % 2):S * (d % 2) + S]
                link(dve.tensor_tensor(t, ps[:, d % 4, 0:S], gatesT[:, d, :], ALU.mult))
                link(dve.tensor_tensor(yT[:, d, :], ps[:, d % 4, S:2 * S], gatesT[:, 8 + d, :], ALU.mult))
                dve.tensor_tensor(yT[:, d, :], yT[:, d, :], t, ALU.add).then_inc(sem["merged"], 1)
            for d in range(KT):
                dve.wait_ge(sem["tiles_done"], N_OUT + d + 1)
                dve.scalar_tensor_tensor(res[:, d, :], ps[:, 4 + d % 4, 0:S], modT[:, 16 + d, 0:1], xT[:, d, :],
                                         ALU.mult, ALU.add).then_inc(sem["resid"], 1)

            def norm(r, dst, src, gain, shift=None):
                inverse(r, S)
                for k in range(KT):
                    o = dve.scalar_tensor_tensor(dst[:, k, :], src[:, k, :], gain[:, k:k + 1], rstd[:, 0:S], ALU.mult, ALU.mult)
                if shift is not None:
                    link(o)
                    for k in range(KT):
                        o = dve.tensor_scalar(dst[:, k, :], dst[:, k, :], shift[:, k, 0:1], None, ALU.add)
                return o

            norm(1, h2T, res, gain2, modT[:, 24:32, :]).then_inc(sem["normed"], 1)

            for tt in range(2):
                if tt:
                    dve.wait_ge(sem["ranked"], 1)
                dve.wait_ge(sem["scores_out"], 16)
                u16 = i16.bitcast(U32)
                cu = c16.bitcast(U32)
                pu = pick.bitcast(U32)

                def best(n, vals, idx, src):
                    for r in range(2):
                        c = slice(8 * r, 8 * r + 8)
                        for q in range(n):
                            o = dve.max(vals(q)[:, c], src(q))
                        link(o)
                        for q in range(n):
                            o = dve.max_index(idx(q)[:, c], vals(q)[:, c], src(q))
                        link(o)
                        if r == 0:
                            for q in range(n):
                                o = dve.match_replace(src(q), vals(q)[:, c], src(q), -3e38)
                            link(o)

                best(16, lambda q: v16[:, q, :], lambda q: u16[:, q, :], lambda q: sc[:, tt, q, :])
                dve.tensor_copy(i16f, u16)
                halves = v16.rearrange("p (h e) k -> p h e k", e=2)
                link(dve.tensor_tensor(cand, bc(halves[:, :, 0, :], 3, 16), bc(halves[:, :, 1, :], 2, 16), ALU.add))
                best(8, lambda q: b16[:, q, :], lambda q: cu[:, q, :], lambda q: cand[:, q, :, :].rearrange("p a b -> p (a b)"))
                link(dve.tensor_copy(gsum, b16[:, :, 0]))
                dve.tensor_tensor(b16, b16, bc(gsum, 2, 16), ALU.subtract).then_inc(sem["gate_in"], 1)
                i16h = i16f.rearrange("p (h e) k -> p h e k", e=2)
                for e in range(2):
                    if e == 0:
                        link(dve.tensor_scalar(pu, cu, 4, None, ALU.logical_shift_right))
                    else:
                        link(dve.tensor_scalar(pu, cu, 15, None, ALU.bitwise_and))
                    link(dve.tensor_copy(pickf, pu))
                    iota16 = mat("iota")[:, 0:16]
                    for h in range(8):
                        o = dve.tensor_tensor(hot[:, h, :, :], bc(iota16, 1, 16), bc(pickf[:, h, :], 2, 16), ALU.is_equal)
                    link(o)
                    for h in range(8):
                        o = dve.tensor_tensor(hot[:, h, :, :], hot[:, h, :, :], bc(i16h[:, h, e, :], 1, 16), ALU.mult)
                    link(o)
                    link(dve.tensor_reduce(rank[:, tt, e, :, :], hot, AX, ALU.add))
                dve.wait_ge(sem["gate_exp"], tt + 1)
                link(dve.tensor_reduce(gsum, b16, AX, ALU.add))
                link(dve.reciprocal(gsum, gsum))
                dve.tensor_tensor(rank[:, tt, 2, :, :], b16, bc(gsum, 2, 16), ALU.mult).then_inc(sem["ranked"], 1)
            dve.sem_inc(sem["w_psum"], 8)
            phase_end(dve, 4)

            with dve.Fori(0, S // 8) as i:
                for t in range(8):
                    dve.wait_ge(sem["w_psum"], 8 * i + t + 1)
                    dve.tensor_scalar(hot1[:, t, :], mat("iota"), rT[:, 0, bass.ds(8 * i + t, 1)], rT[:, 2, bass.ds(8 * i + t, 1)],
                                      ALU.is_equal, ALU.mult).then_inc(sem["hot1_ready"], 1)
                    if t == 3:
                        dve.wait_ge(sem["w_psum"], 8 * i + 8)
                        dve.tensor_tensor(hot2[:, 4:8, :], bc(mat("iota"), 1, 4), bc(rT[:, 1, bass.ds(8 * i + 4, 4)], 2, P),
                                          ALU.is_equal).then_inc(sem["hot2_late"], 1)

            def gate(j, b, done):
                dve.wait_ge(sem["gelu_done"], done)
                dve.tensor_tensor(gated[:, b, :], gelu[:, b, :], W[:, :, bass.ds(j, 1)].rearrange("p a b -> p (a b)"), ALU.mult).then_inc(
                    sem["gated"], 1)

            def tile_lo(j, ahead, i2=0):
                h = 4 * j + ahead
                slot = (N_PEER + h // 2) % RING
                dve.wait_ge(sem["w_hi"], 4 * i2 + h + 1)
                dve.tensor_tensor(w_parts[:, 1, h % 4, :], ring[:, slot, 512 * (h % 2):512 * (h % 2) + 512],
                                  w_parts[:, 0, h % 4, :].bitcast(F32), ALU.subtract).then_inc(sem["w_lo"], 1)

            def gated_lo(ready, b):
                dve.wait_ge(sem["g_hi"], ready)
                dve.tensor_tensor(g_parts[:, 1, b, :], gated[:, b, :], g_parts[:, 0, b, :].bitcast(F32), ALU.subtract).then_inc(
                    sem["g_lo"], 1)

            def step(j, i2=0, last=False):
                tile_lo(j, 1, i2)
                tile_lo(j, 2, i2)
                gate(i2 + j, j % 2, i2 + j + 1)
                tile_lo(j, 3, i2)
                gated_lo(i2 + j + 1, j % 2)
                if not last:
                    tile_lo(j, 4, i2)

            dve.wait_ge(sem["w_out"], 2 + S // 4)
            tile_lo(0, 4)
            gate(0, 0, 1)
            gated_lo(1, 0)
            for j in (1, 2):
                step(j)
            with dve.Fori(1, P // 2 - 1) as i:
                for jj in (1, 2):
                    step(jj, 2 * i)
            step(127, last=True)
            dve.wait_ge(sem["tiles_done"], N_IN2)
            for d in range(KT):
                dve.scalar_tensor_tensor(res[:, d, :], ps[:, d // 2, S * (d % 2):S * (d % 2) + S], modT[:, 40 + d, 0:1],
                                         res[:, d, :], ALU.mult, ALU.add).then_inc(sem["resid"], 1)
            norm(2, x2T, res, col("final_norm")).then_inc(sem["normed"], 1)
            phase_end(dve, 5)

            def dve_lo(r, src):
                for c in range(4):
                    dve.wait_ge(sem["h_hi"], 4 * r + c + 1)
                    dve.tensor_tensor(h_parts[:, 1, 2 * c:2 * c + 2, :], src[:, 2 * c:2 * c + 2, :],
                                      h_parts[:, 0, 2 * c:2 * c + 2, :].bitcast(F32), ALU.subtract).then_inc(sem["h_lo"], 1)

            norm(3, h3T, x2T, col("norm_mix2")).then_inc(sem["normed"], 1)
            dve_lo(1, h3T)
            dve.memset(rxp[:, :, 0:3], 0.0)
            lam = col("rg_lambda")
            link(dve.scalar_tensor_tensor(vec[:, 8:16], lam, -1.0, lam, ALU.mult, ALU.max))
            link(dve.tensor_scalar(vec[:, 0:8], lam, -1.0, 0.0, ALU.mult, ALU.max))
            lam4 = col("lam", 4, 64)
            link(dve.tensor_tensor(vec[:, 64:192].rearrange("p (a b) -> p a b", a=2), lam4[:, 0:2, :], lam4[:, 2:4, :], ALU.mult))
            dve.tensor_reduce(vec[:, 32:34], vec[:, 64:192].rearrange("p (a b) -> p a b", a=2), AX, ALU.add).then_inc(sem["rg_in"], 1)
            taps = col("rg_conv", KT, 4)
            for j in range(KT):
                dve.wait_ge(sem["proj_free"], 4 + 39 + j + 1)
                link(dve.tensor_scalar(xr[:, j, :], rxp[:, j, 0:S], taps[:, j, 0:1], col("rg_conv_b")[:, j:j + 1], ALU.mult, ALU.add))
                for c in range(1, 4):
                    o = dve.scalar_tensor_tensor(xr[:, j, :], rxp[:, j, c:c + S], taps[:, j, c:c + 1], xr[:, j, :], ALU.mult, ALU.add)
                    if c < 3:
                        link(o)
                o.then_inc(sem["rg_conv_done"], 1)
            dve.wait_ge(sem["rg_ln"], 1)
            link(dve.tensor_tensor(vec[:, 0:8], vec[:, 0:8], vec[:, 8:16], ALU.add))
            dve.tensor_scalar(vec[:, 16:24], vec[:, 0:8], -8.0, None, ALU.mult)
            dve.tensor_scalar(vec[:, 24:32], vec[:, 0:8], 8.0, None, ALU.mult).then_inc(sem["rg_coeff"], 1)
            dve.wait_ge(sem["lam_exp"], 1)
            link(dve.tensor_tensor(vec[:, 34:35], vec[:, 33:34], vec[:, 32:33], ALU.subtract))
            dve.tensor_scalar(vec[:, 34:35], vec[:, 34:35], -LAM_INIT, None, ALU.add)
            dve.tensor_scalar(vec[:, 48:49], col("subln"), 1.0 - LAM_INIT, None, ALU.mult)
            flat = lambda v: v.rearrange("p a b -> p (a b)")
            dve.wait_ge(sem["rg_sig"], KT)
            link(dve.tensor_tensor(flat(ii), flat(ii), flat(xr), ALU.mult))
            dve.wait_ge(sem["rg_pow"], KT)
            link(dve.tensor_tensor(flat(xr), flat(dca), flat(dca), ALU.mult))
            dve.scalar_tensor_tensor(flat(thn), flat(xr), 1.0, flat(thn), ALU.add, ALU.mult).then_inc(sem["rg_square"], 1)
            dve.wait_ge(sem["rg_mult"], 1)
            link(dve.tensor_tensor(flat(ii), flat(ii), flat(thn), ALU.mult))
            for j in range(KT):
                o = dve.tensor_tensor_scan(xr[:, j, :], dca[:, j, :], ii[:, j, :], 0.0, ALU.mult, ALU.add)
            link(o)
            dve.tensor_tensor(flat(rgl), flat(rgl), flat(xr), ALU.mult)

            def logits2(g):
                st = stat[g % 2]
                qt = g // 2 % 2
                for t in range(4):
                    u = 4 * (g % 2) + t
                    slope = 2.0 ** -(u + 1) if g < 4 else 2.0 ** (-2.0 * (u // 2 + 1))
                    dve.wait_ge(sem["score_done"], 16 + 4 * g + t + 1)
                    if g >= 2 and t == 0:
                        dve.wait_ge(sem["turned"], 16 + (4 * (g - 1) if g <= 5 else 16 + 2 * (g - 5)))
                    o = dve.scalar_tensor_tensor(lg[:, g % 2, t, :], alibi[:, qt, :], slope, ps[:, t, 0:S], ALU.mult, ALU.add)
                    o.then_inc(sem["logits2"], 1)
                dve.wait_ge(sem["logits2"], 4 * g + 4)
                link(dve.tensor_reduce(st["mx"], lg[:, g % 2, :, :], AX, ALU.max))
                dve.tensor_scalar(st["nm"], st["mx"], -1.0, None, ALU.mult).then_inc(sem["max_ready"], 1)

            alibi = mat("alibi").rearrange("p (q k) -> p q k", q=2)
            logits2(0)
            v = 0
            for g in range(8):
                st = stat[g % 2]
                qt = g // 2 % 2
                if g < 4:
                    dve.wait_ge(sem["probs2"], 4 * g + 4)
                    link(dve.reciprocal(st["ri"], st["rs"]))
                else:
                    dve.wait_ge(sem["maps2"], 4 * (g - 4) + 4)
                    link(dve.reciprocal(st["ri"], st["rs"]))
                    link(dve.tensor_scalar(st["es"], st["ri"], vec[:, 34:35], None, ALU.mult))
                    for t in (0, 2):
                        p0, p1 = lg[:, g % 2, t, :], lg[:, g % 2, t + 1, :]
                        link(dve.tensor_scalar(p0, p0, st["ri"][:, t:t + 1], None, ALU.mult))
                        dve.scalar_tensor_tensor(p0, p1, st["es"][:, t + 1:t + 2], p0, ALU.mult, ALU.add).then_inc(sem["probs2"], 1)
                if g < 7:
                    logits2(g + 1)
                v += 4 if g < 4 else 2
                dve.wait_ge(sem["weighted"], 16 + v)
                c = slice(256 * (g % 2), 256 * (g % 2) + 256)
                if g < 4:
                    o = o2[0][:, qt, c].rearrange("p (a b) -> p a b", a=4)
                    dve.tensor_tensor(o, bank(6 + g % 2, 4, 64), bc(st["ri"], 2, 64), ALU.mult).then_inc(sem["o_scaled"], 1)
                else:
                    dve.tensor_copy(o2[1][:, qt, c], ps[:, 6 + g % 2, 0:256]).then_inc(sem["o_scaled"], 1)
            dve.wait_ge(sem["o_scaled"], 12)
            heads = o2[1].rearrange("p a (b c) -> p (a b) c", b=4)
            tmp = flat(lg[:, 0, :, :]).rearrange("p (a b) -> p a b", a=8)
            link(dve.tensor_tensor(tmp, heads, heads, ALU.mult))
            dve.tensor_reduce(vec[:, 40:48], tmp, AX, ALU.add).then_inc(sem["o2_stat"], 1)
            dve.wait_ge(sem["o2_root"], 1)
            link(dve.reciprocal(vec[:, 40:48], vec[:, 40:48]))
            dve.tensor_tensor(heads, heads, bc(vec[:, 40:48], 2, P), ALU.mult).then_inc(sem["o2_ready"], 1)
            phase_end(dve, 6)

            for d in range(KT):
                dve.wait_ge(sem["tiles_done"], N_BR2 + 2 * d + 2)
                b = 2 * (d % 2)
                y, t = y2T[:, d, :], fft[:, d % 2, :]
                dve.tensor_tensor(t, ps[:, b, 0:S], g2T[:, d, :], ALU.mult)
                link(dve.tensor_tensor(y, ps[:, b, S:2 * S], g2T[:, 16 + d, :], ALU.mult))
                link(dve.tensor_tensor(y, y, t, ALU.add))
                link(dve.tensor_tensor(t, ps[:, b + 1, 0:S], g2T[:, 8 + d, :], ALU.mult))
                dve.tensor_tensor(y, y, t, ALU.add).then_inc(sem["merged"], 1)
            for d in range(KT):
                dve.wait_ge(sem["tiles_done"], N_OUT2 + d + 1)
                dve.tensor_tensor(res[:, d, :], ps[:, 4 + d % 4, 0:S], x2T[:, d, :], ALU.add).then_inc(sem["resid"], 1)
            norm(4, h4T, res, col("norm_ffn2")).then_inc(sem["normed"], 1)
            dve_lo(2, h4T)
            link(dve.memset(upp[:, :, :, 0:2], 0.0))

            dve.sem_inc(sem["ff_conv"], 2)
            taps3 = col("ff_conv", 44, 3)
            bias3 = col("ff_conv_b")

            def ff_taps(f, b, ready, free):
                dve.wait_ge(sem["ff_out"], ready)
                if free is not None:
                    dve.wait_ge(sem["ff_act"], free)
                one = lambda v, c: v[:, bass.ds(c, 1)]
                for m in range(2):
                    c = f + FT * m
                    dve.tensor_scalar(upc[:, b, m, :], upp[:, b, m, 0:S], one(taps3[:, :, 0], c), one(bias3, c), ALU.mult, ALU.add
                                      ).then_inc(sem["ff_taps"], 1)
                for r in range(1, 3):
                    for m in range(2):
                        c = f + FT * m
                        dve.wait_ge(sem["ff_taps"], 4 * f + 2 * r - 1 + m)
                        o = dve.scalar_tensor_tensor(upc[:, b, m, :], upp[:, b, m, r:r + S], one(taps3[:, :, r], c), upc[:, b, m, :],
                                                     ALU.mult, ALU.add)
                        if r == 1:
                            o.then_inc(sem["ff_taps"], 1)
                o.then_inc(sem["ff_conv"], 1)

            def ff_gate(f, b, ready):
                dve.wait_ge(sem["ff_gelu"], ready)
                dve.tensor_tensor(fft[:, b, :], upc[:, b, 0, :], upc[:, b, 1, :], ALU.mult).then_inc(sem["ff_act"], 1)

            def ff_lo(f, b):
                dve.wait_ge(sem["g_hi"], P + f + 1)
                dve.tensor_tensor(g_parts[:, 1, b, :], fft[:, b, :], g_parts[:, 0, b, :].bitcast(F32), ALU.subtract).then_inc(
                    sem["g_lo"], 1)

            for f in range(2):
                ff_taps(f, f, f + 3, None)
                ff_gate(f, f, f + 1)
                ff_lo(f, f)
            with dve.Fori(1, FT // 2) as i:
                for b in range(2):
                    ff_taps(2 * i + b, b, 2 * i + b + 3, 2 * i + b - 1)
                    ff_gate(2 * i + b, b, 2 * i + b + 1)
                    ff_lo(2 * i + b, b)
            dve.wait_ge(sem["tiles_done"], N_ALL)
            for d in range(KT):
                dve.tensor_tensor(res[:, d, :], ps[:, d // 2, S * (d % 2):S * (d % 2) + S], res[:, d, :], ALU.add).then_inc(sem["resid"], 1)
            inverse(5, S)
            for k in range(KT):
                o = dve.scalar_tensor_tensor(outb[:, k, :], res[:, k, :], col("final2")[:, k:k + 1], rstd[:, 0:S], ALU.mult, ALU.mult)
                if k % 4 == 3:
                    o.then_inc(sem["final_done"], 1)

        @block.gpsimd
        def _(pool):
            for n in range(1, 3):
                phase_end(pool, n)
            for n in range(4):
                for l in range(1, 6):
                    for d in range(2):
                        b = pair[d]
                        pool.wait_ge(sem["y_done"], 14 * n + 2 * l + d + 1)
                        pool.tensor_tensor(b["M"], b["A"], bc(level[:, d, l + 1, :], 1, 4), ALU.mult).then_inc(
                            sem["late_mask"], 1)
            phase_end(pool, 3)
            for c in range(4):
                pool.wait_ge(sem["h_hi"], c + 1)
                pool.tensor_tensor(h_parts[:, 1, 2 * c:2 * c + 2, :], h2T[:, 2 * c:2 * c + 2, :],
                                   h_parts[:, 0, 2 * c:2 * c + 2, :].bitcast(F32), ALU.subtract).then_inc(sem["h_lo"], 1)
            for h in range(4):
                pool.wait_ge(sem["w_hi"], h + 1)
                pool.tensor_tensor(w_parts[:, 1, h, :], ring[:, (N_PEER + h // 2) % RING, 512 * (h % 2):512 * (h % 2) + 512],
                                   w_parts[:, 0, h, :].bitcast(F32), ALU.subtract).then_inc(sem["w_lo"], 1)
            phase_end(pool, 4)
            with pool.Fori(0, S // 8) as i:
                key2 = small[:, 80:84]
                pool.wait_ge(sem["w_psum"], 8 * i + 4)
                pool.sem_inc(sem["pool_step"], 1)
                pool.tensor_copy(key2, rT[:, 1, bass.ds(8 * i, 4)]).then_inc(sem["key2_ready"], 1)
                pool.wait_ge(sem["key2_ready"], i + 1)
                pool.sem_inc(sem["pool_step"], 1)
                for t in range(4):
                    pool.tensor_scalar(hot2[:, t, :], mat("iota"), key2[:, t:t + 1], None, ALU.is_equal).then_inc(
                        sem["hot2_ready"], 1)
            phase_end(pool, 5)

            def rest(m0, count):
                def one(h, n, i=None):
                    if i is None:
                        pool.wait_ge(sem["w_hi"], h + 1)
                    else:
                        pool.wait_ge(sem["w_hi"], 8 * i + h + 1)
                        pool.sem_inc(sem["pool_step"], 1)
                    pool.tensor_tensor(w_parts[:, 1, h % 4, :], ring[:, n % RING, 512 * (h % 2):512 * (h % 2) + 512],
                                       w_parts[:, 0, h % 4, :].bitcast(F32), ALU.subtract).then_inc(sem["w_lo"], 1)

                with pool.Fori(0, count // RING) as i:
                    for q in range(2 * RING):
                        one(2 * m0 + q, tile_of(m0 + q // 2), i)
                for q in range(count // RING * 2 * RING, 2 * count):
                    one(2 * m0 + q, tile_of(m0 + q // 2))

            rest(M_IN2, M_FFN - M_IN2)
            phase_end(pool, 6)
            rest(M_FFN, M_ALL - M_FFN)


def col_tiles(w):
    f = w.shape[1] // P
    return w.reshape(KT, P, f, P).transpose(2, 1, 0, 3).reshape(f, P, KT * P)


def columns(v, n):
    return v.reshape(n, P).T


def shape_constants():
    i = np.arange(P)
    ident = np.eye(P)
    d = np.arange(S)
    alibi = np.zeros((P, 2, S))
    band = np.zeros((P, 2, 512))
    for qt in range(2):
        q = qt * P + i[:, None]
        dist = q - d[None, :]
        alibi[:, qt] = np.where(dist >= 0, -dist, NEG)
        band[:, qt, 0:S] = np.where(np.abs(dist) <= 128, 0.0, NEG)
    mats = np.concatenate([ident, np.ones((P, P)), np.tile(i, (P, 1)), alibi.reshape(P, -1),
                           np.full((P, 1), EPS)], 1)
    f = i % 64
    partner = np.where(f % 32 < 16, i + 16, i - 16)
    perm = np.zeros((P, P))
    perm[partner, i] = 1.0
    inv = (np.float32(10000.0) ** (-np.arange(16, dtype=np.float32) / np.float32(16))).astype(np.float32)
    t = np.arange(S)
    pos = np.where((f < 32)[:, None], (t // 64)[None, :], (t % 64)[None, :]).astype(np.float32)
    ang = (pos * inv[f % 16][:, None]).astype(np.float32).astype(np.float64)
    cos, sin = np.cos(ang), np.sin(ang) * np.where(f % 32 < 16, -1.0, 1.0)[:, None]
    tri = np.stack([i[:, None] <= i[None, :], i[:, None] >= i[None, :]], 1)
    level = np.zeros((P, 2, 7, P))
    for l in range(7):
        s = 2 ** l
        low = (i[:, None] // (2 * s) == i[None, :] // (2 * s)) & (i[:, None] // s % 2 == 1) & (i[None, :] // s % 2 == 0)
        level[:, 0, l], level[:, 1, l] = low, low.T
    mats1 = np.concatenate([tri.reshape(P, -1), level.reshape(P, -1)], 1)
    matsa = np.concatenate([perm, cos, sin, band.reshape(P, -1)], 1)
    return mats.astype(np.float32), mats1.astype(np.float32), matsa.astype(np.float32)


def lay_out(a):
    a = {k: np.asarray(v) for k, v in a.items()}
    w_in = a["w_in"][0]
    q = w_in[:, :512].reshape(D, 2, 4, 64).transpose(0, 2, 1, 3).reshape(D, 512)
    small = np.zeros((D, P), np.float32)
    small[:, :16] = w_in[:, 2816:2832]
    win = np.concatenate([q, w_in[:, 512:2816], small, w_in[:, 2832:]], 1)
    ada = a["w_ada"][0].reshape(4, 2, P, 12, 512).transpose(3, 0, 2, 1, 4).reshape(48, P, 1024)
    br = np.concatenate([a["w_br_attn"][0], a["w_br_dn"][0]], 0)
    keys = np.zeros((P, 8, 2, P), np.float32)
    pk = a["peer_keys"][0]
    for half in range(2):
        keys[64 * half:64 * half + 64, :, half] = pk[:, half].transpose(2, 0, 1)
    keys = keys.reshape(P, 2, 1024).transpose(1, 0, 2)
    u = a["peer_u"][0].reshape(P, P, KT, P).transpose(1, 3, 2, 0).reshape(P, P, 1024)
    v = a["peer_v"][0].reshape(P, P, D).transpose(1, 0, 2)
    peer = np.concatenate([u[:1], np.stack([u[1:], v[:-1]], 1).reshape(254, P, 1024), v[-1:]], 0)
    w2 = a["w_in_2"][0]
    in2 = np.concatenate([w2[:, 3072:5120], w2[:, :3072], w2[:, 5120:]], 1)
    rgw = np.zeros((P, 2, 8, P), np.float32)
    for g, name in enumerate(("rg_w_a_2", "rg_w_x_2")):
        w = a[name][0].reshape(8, 2, 64, 64)
        for half in range(2):
            rgw[64 * half:64 * half + 64, g, :, 64 * half:64 * half + 64] = w[:, half].transpose(1, 0, 2)
    rgw = rgw.reshape(P, 2, 1024).transpose(1, 0, 2)
    br2 = np.concatenate([a["w_branch_a_2"][0], a["w_branch_c_2"][0], a["w_branch_b_2"][0]], 0)
    br2 = br2.reshape(2, 8, P, 8, P).transpose(3, 0, 2, 1, 4).reshape(16, P, 1024)
    up = a["ffn_up_2"][0]
    upt = col_tiles(up)
    down = a["ffn_down_2"][0].reshape(FT, P, D)
    ffn = np.concatenate([upt[:1], upt[FT:FT + 1],
                          np.stack([upt[1:FT], upt[FT + 1:], down[:-1]], 1).reshape(3 * FT - 3, P, 1024), down[-1:]], 0)
    wstream = np.concatenate([ada, col_tiles(win), col_tiles(br), col_tiles(a["w_out"][0]), col_tiles(a["peer_wq"][0]),
                              keys, peer, col_tiles(in2), br2, col_tiles(a["w_out_2"][0]), ffn, rgw], 0)
    assert wstream.shape[0] == N_ALL + 2
    x_t = np.stack([a["x"][0], a["ctx"][0]], 0).reshape(2, S, KT, P).transpose(3, 0, 2, 1).reshape(P, -1)
    wide = lambda v: np.broadcast_to(v.reshape(1, -1), (P, v.size))
    c = dict(
        c2=np.stack([a["c"][0], a["c_ctx"]], 0).reshape(2, KT, P).transpose(2, 1, 0).reshape(P, -1),
        b_ada=columns(a["b_ada"][0], 48), norm_mix=columns(a["norm_mix"][0], 8), norm_ffn=columns(a["norm_ffn"][0], 8),
        final_norm=columns(a["final_norm"], 8), b_gate=columns(a["b_gate"][0], 16),
        conv=a["dn_conv"][0].reshape(5, 12, P).transpose(2, 1, 0).reshape(P, -1),
        a_log=wide(np.stack([a["dn_a_log_f"][0], a["dn_a_log_b"][0]])),
        dt=wide(np.stack([a["dn_dt_bias_f"][0], a["dn_dt_bias_b"][0]])),
        sink=wide(a["attn_sink"][0]), dn_norm=columns(a["dn_norm"][0], 1), norm_mix2=columns(a["norm_mix_g_2"][0], 8),
        b_gate2=columns(a["b_gate_2"][0], 24), rg_conv=a["rg_conv_w_2"][0].reshape(4, 8, P).transpose(2, 1, 0).reshape(P, -1),
        rg_conv_b=columns(a["rg_conv_b_2"][0], 8), rg_ba=columns(a["rg_b_a_2"][0], 8), rg_bx=columns(a["rg_b_x_2"][0], 8),
        rg_lambda=columns(a["rg_lambda_2"][0], 8),
        lam=wide(np.concatenate([a["diff_lq1_2"][0], a["diff_lq2_2"][0], a["diff_lk1_2"][0], a["diff_lk2_2"][0]])),
        subln=columns(a["diff_subln_g_2"][0], 1), norm_ffn2=columns(a["norm_ffn_g_2"][0], 8),
        ff_conv=a["ffn_conv_w_2"][0].reshape(3, 44, P).transpose(2, 1, 0).reshape(P, -1),
        ff_conv_b=columns(a["ffn_conv_b_2"][0], 44), final2=columns(a["final_norm_g_2"], 8))
    cols = np.concatenate([c[n] for n in COLS], 1)
    assert cols.shape == (P, N_COLS)
    mats, mats1, matsa = shape_constants()
    return {"wstream": wstream, "x_t": x_t, "cols": cols, "mats": mats, "mats1": mats1, "matsa": matsa}


def kernel(**inputs):
    import concourse.bacc as bacc
    from concourse.bass_utils import run_bass_kernel_spmd

    arrays = {k: np.ascontiguousarray(v) for k, v in lay_out(inputs).items()}
    nc = bacc.Bacc("TRN2", target_bir_lowering=False, num_devices=1)
    args = [nc.dram_tensor(n, v.shape, F32, kind="ExternalInput").ap() for n, v in arrays.items()]
    out = nc.dram_tensor("out_t", (P, KT * S), F32, kind="ExternalOutput").ap()
    build(nc, *args, out)
    got = run_bass_kernel_spmd(nc, [arrays], core_ids=[0]).results[0]["out_t"]
    return np.ascontiguousarray(got.reshape(P, KT, S).transpose(2, 1, 0).reshape(1, S, D))
```
